# Optimizing a Trainium2 kernel written in Bass

```python
import jax
import jax.numpy as jnp
from jax import lax
import numpy as np

D_MODEL = 1024
BATCH = 1
SEQ = 512
DEPTH = 2
DEC_BATCH = 1
DEC_SEQ = 32
PAST_LEN = 128

CHUNK = 64
HEAD_DIM = 64
ROPE_THETA = 10000.0
EPS = 1e-6
A_HEADS = 8
A_KV_HEADS = 2
WINDOW = 128
A_PREV_CHUNKS = WINDOW // CHUNK
B_HEADS = 8
B_PREV_CHUNKS = 8
B_REACH = B_PREV_CHUNKS * CHUNK
REL_CLIP = 128
C_HEADS = 4
C_DK = 64
C_DV = 128
D_HEADS = 4
D_DK = 64
D_DV = 128
GLA_RANK = 16
GLA_TAU = 16.0
N_BRANCHES = 4
BRANCH_WIDTH = 512
MEM_LEN = 256
X_HEADS = 4
X_HEAD_DIM = 128
D_FF = 4 * D_MODEL

IN_WIDTHS = (A_HEADS * HEAD_DIM, A_KV_HEADS * HEAD_DIM, A_KV_HEADS * HEAD_DIM,
             B_HEADS * HEAD_DIM, B_HEADS * HEAD_DIM, B_HEADS * HEAD_DIM,
             C_HEADS * C_DK, C_HEADS * C_DK, C_HEADS * C_DV, C_HEADS * C_DV,
             D_HEADS * D_DK, D_HEADS * D_DK, D_HEADS * D_DV, D_HEADS * D_DV, GLA_RANK)
IN_WIDTH = sum(IN_WIDTHS)

kernel_name = 'hybrid_streaming_encoder_step'

def _rms(x, g):
    xf = x.astype(jnp.float32)
    y = xf * lax.rsqrt(jnp.mean(xf * xf, axis=-1, keepdims=True) + EPS)
    return (y * g.astype(jnp.float32)).astype(x.dtype)

def _group_ln(x, g):
    xf = x.astype(jnp.float32)
    xc = xf - jnp.mean(xf, axis=-1, keepdims=True)
    y = xc * lax.rsqrt(jnp.mean(xc * xc, axis=-1, keepdims=True) + EPS)
    return (y * g.astype(jnp.float32)).astype(x.dtype)

def _rope(x, pos):
    half = x.shape[-1] // 2
    freqs = ROPE_THETA ** (-jnp.arange(half, dtype=jnp.float32) / half)
    ang = pos.astype(jnp.float32)[:, None] * freqs[None, :]
    cos = jnp.cos(ang)[None, :, None, :]
    sin = jnp.sin(ang)[None, :, None, :]
    xf = x.astype(jnp.float32)
    x1, x2 = xf[..., :half], xf[..., half:]
    return jnp.concatenate([x1 * cos - x2 * sin, x2 * cos + x1 * sin], axis=-1).astype(x.dtype)

def _band_attend(q, k, v, q_pos, k_pos, sink, bias_table):
    B, Tq, H, Dh = q.shape
    Tk, Hkv = k.shape[1], k.shape[2]
    G = H // Hkv
    qg = q.reshape(B, Tq, Hkv, G, Dh)
    s = jnp.einsum('bqhgd,bkhd->bhgqk', qg, k).astype(jnp.float32)
    if bias_table is not None:
        rel = jnp.clip(q_pos[:, None] - k_pos[None, :], -REL_CLIP, REL_CLIP) + REL_CLIP
        s = s + bias_table[:, rel].astype(jnp.float32).reshape(Hkv, G, Tq, Tk)
    s = jnp.where(k_pos >= 0, s, -jnp.inf)
    if sink is not None:
        sink_b = sink.astype(jnp.float32).reshape(1, Hkv, G, 1, 1)
        lse = jnp.logaddexp(jax.nn.logsumexp(s, axis=-1, keepdims=True), sink_b)
        p = jnp.exp(s - lse)
    else:
        p = jax.nn.softmax(s, axis=-1)
    o = jnp.einsum('bhgqk,bkhd->bqhgd', p.astype(v.dtype), v)
    return o.reshape(B, Tq, H * Dh)

def _band_prompt(q, k, v, n_prev, sink, bias_table):
    B, T, H, Dh = q.shape
    n_chunks = T // CHUNK
    pad = n_prev * CHUNK
    band = pad + CHUNK
    kp = jnp.pad(k, ((0, 0), (pad, 0), (0, 0), (0, 0)))
    vp = jnp.pad(v, ((0, 0), (pad, 0), (0, 0), (0, 0)))
    qc = jnp.moveaxis(q.reshape(B, n_chunks, CHUNK, H, Dh), 1, 0)

    def one_chunk(args):
        c, qb = args
        start = c * CHUNK
        kb = lax.dynamic_slice_in_dim(kp, start, band, axis=1)
        vb = lax.dynamic_slice_in_dim(vp, start, band, axis=1)
        q_pos = start + jnp.arange(CHUNK)
        k_pos = start - pad + jnp.arange(band)
        return _band_attend(qb, kb, vb, q_pos, k_pos, sink, bias_table)

    out = lax.map(one_chunk, (jnp.arange(n_chunks), qc))
    return jnp.moveaxis(out, 0, 1).reshape(B, T, H * Dh)

def _band_step(q, k_new, v_new, k_cache, v_cache, q_pos, sink, bias_table):
    L = k_cache.shape[1]
    k = jnp.concatenate([k_cache, k_new], axis=1)
    v = jnp.concatenate([v_cache, v_new], axis=1)
    k_pos = jnp.concatenate([PAST_LEN - L + jnp.arange(L), q_pos])
    return _band_attend(q, k, v, q_pos, k_pos, sink, bias_table)

def _decay_scan(q, k, v, log_a, S0, chunk_len):
    B, T, H, Dk = q.shape
    Dv = v.shape[-1]
    n = T // chunk_len

    def chunks(t):
        return jnp.moveaxis(t.reshape(B, n, chunk_len, H, t.shape[-1]), 1, 0)

    causal = jnp.tril(jnp.ones((chunk_len, chunk_len), dtype=bool))[None, :, :, None, None]

    def step(S, inp):
        qc, kc, vc, ac = inp
        qf, kf, vf = qc.astype(jnp.float32), kc.astype(jnp.float32), vc.astype(jnp.float32)
        Sf = S.astype(jnp.float32)
        cum = jnp.cumsum(ac.astype(jnp.float32), axis=1)
        rel = jnp.where(causal, cum[:, :, None] - cum[:, None, :], -jnp.inf)
        scores = jnp.einsum('bihd,bjhd,bijhd->bhij', qf, kf, jnp.exp(rel))
        o = jnp.einsum('bhij,bjhv->bihv', scores, vf)
        o = o + jnp.einsum('bihd,bhdv->bihv', qf * jnp.exp(cum), Sf)
        last = cum[:, -1]
        S_new = Sf * jnp.exp(last)[..., None] + jnp.einsum(
            'bjhd,bjhv->bhdv', kf * jnp.exp(last[:, None] - cum), vf)
        return S_new.astype(S.dtype), o.astype(v.dtype)

    S_fin, o = lax.scan(step, S0, (chunks(q), chunks(k), chunks(v), chunks(log_a)))
    return jnp.moveaxis(o, 0, 1).reshape(B, T, H, Dv), S_fin

def _merge(h, outs, l, P):
    B, T, _ = h.shape
    gates = jax.nn.sigmoid((h @ P['w_merge'][l]).astype(jnp.float32)).astype(h.dtype)
    gates = gates.reshape(B, T, N_BRANCHES, D_MODEL)
    br = jnp.einsum('btnc,ncd->btnd', jnp.stack(outs, axis=-2), P['w_branch'][l])
    return jnp.sum(gates * br, axis=-2) @ P['w_out'][l]

def _mem_kv(mem, l, P):
    B, M, _ = mem.shape
    kv = _rms(mem, P['norm_mem'][l]) @ P['w_xkv'][l]
    k, v = jnp.split(kv, 2, axis=-1)
    k = _rms(k.reshape(B, M, X_HEADS, X_HEAD_DIM), P['kn_x'][l])
    return k, v.reshape(B, M, X_HEADS, X_HEAD_DIM)

def _cross(h, mk, mv, l, P):
    B, T, _ = h.shape
    q = _rms((h @ P['w_xq'][l]).reshape(B, T, X_HEADS, X_HEAD_DIM), P['qn_x'][l]) * X_HEAD_DIM ** -0.5
    s = jnp.einsum('bqhd,bkhd->bhqk', q, mk).astype(jnp.float32)
    p = jax.nn.softmax(s, axis=-1).astype(mv.dtype)
    o = jnp.einsum('bhqk,bkhd->bqhd', p, mv).reshape(B, T, X_HEADS * X_HEAD_DIM)
    return o @ P['w_xo'][l]

def _layer(x, pos, l, P, mem_k, mem_v, cache):
    B, T, _ = x.shape
    h = _rms(x, P['norm_mix'][l])
    z = h @ P['w_in'][l]
    (qa, ka, va, qb, kb, vb, qc, kc, vc, gc, qd, kd, vd, gd, ad) = jnp.split(
        z, np.cumsum(IN_WIDTHS)[:-1].tolist(), axis=-1)
    sc = HEAD_DIM ** -0.5
    qa = _rope(_rms(qa.reshape(B, T, A_HEADS, HEAD_DIM), P['qn_a'][l]), pos) * sc
    ka = _rope(_rms(ka.reshape(B, T, A_KV_HEADS, HEAD_DIM), P['kn_a'][l]), pos)
    va = va.reshape(B, T, A_KV_HEADS, HEAD_DIM)
    qb = _rms(qb.reshape(B, T, B_HEADS, HEAD_DIM), P['qn_b'][l]) * sc
    kb = _rms(kb.reshape(B, T, B_HEADS, HEAD_DIM), P['kn_b'][l])
    vb = vb.reshape(B, T, B_HEADS, HEAD_DIM)
    qc = _rope(qc.reshape(B, T, C_HEADS, C_DK), pos)
    kc = _rope(kc.reshape(B, T, C_HEADS, C_DK), pos) * C_DK ** -0.5
    vc = vc.reshape(B, T, C_HEADS, C_DV)
    log_gamma = jnp.log1p(-jnp.exp2(-5.0 - jnp.arange(C_HEADS, dtype=jnp.float32)))
    la_c = jnp.broadcast_to(log_gamma[None, None, :, None], (B, T, C_HEADS, C_DK))
    qd = qd.reshape(B, T, D_HEADS, D_DK) * D_DK ** -0.5
    kd = kd.reshape(B, T, D_HEADS, D_DK)
    vd = vd.reshape(B, T, D_HEADS, D_DV)
    la_d = (jax.nn.log_sigmoid((ad @ P['w_alpha_up'][l] + P['b_alpha'][l]).astype(jnp.float32))
            / GLA_TAU).reshape(B, T, D_HEADS, D_DK)
    if cache is None:
        oa = _band_prompt(qa, ka, va, A_PREV_CHUNKS, P['sink_a'][l], None)
        ob = _band_prompt(qb, kb, vb, B_PREV_CHUNKS, None, P['relbias_b'][l])
        s_c0 = jnp.zeros((B, C_HEADS, C_DK, C_DV), x.dtype)
        s_d0 = jnp.zeros((B, D_HEADS, D_DK, D_DV), x.dtype)
        block = CHUNK
        ra, rb = min(WINDOW, T), min(B_REACH, T)
        new_rows = (ka[:, T - ra:], va[:, T - ra:], kb[:, T - rb:], vb[:, T - rb:])
    else:
        win_k, win_v, band_k, band_v, s_c0, s_d0 = cache
        oa = _band_step(qa, ka, va, win_k, win_v, pos, P['sink_a'][l], None)
        ob = _band_step(qb, kb, vb, band_k, band_v, pos, None, P['relbias_b'][l])
        block = T
        new_rows = (ka, va, kb, vb)
    oc, s_c = _decay_scan(qc, kc, vc, la_c, s_c0, block)
    oc = _group_ln(oc, P['gn_c'][l].reshape(C_HEADS, C_DV)).reshape(B, T, C_HEADS * C_DV) * jax.nn.silu(gc)
    od, s_d = _decay_scan(qd, kd, vd, la_d, s_d0, block)
    od = _rms(od, P['gn_d'][l].reshape(D_HEADS, D_DV)).reshape(B, T, D_HEADS * D_DV) * jax.nn.silu(gd)
    x = x + _merge(h, (oa, ob, oc, od), l, P)
    x = x + _cross(_rms(x, P['norm_x'][l]), mem_k, mem_v, l, P)
    hf = _rms(x, P['norm_ffn'][l])
    x = x + jnp.square(jax.nn.relu(hf @ P['w_up'][l])) @ P['w_down'][l]
    return x, new_rows + (s_c, s_d)

def setup_inputs(seed: int = 0) -> dict:
    key = jax.random.key(seed)
    keys = iter(jax.random.split(key, 64))

    def nrm(shape, scale):
        return jax.random.normal(next(keys), shape, jnp.float32) * scale

    def gain(shape):
        return 1.0 + nrm(shape, 0.05)

    la = min(WINDOW, PAST_LEN)
    lb = min(B_REACH, PAST_LEN)
    xw = X_HEADS * X_HEAD_DIM
    return {
        'x_prompt': nrm((BATCH, SEQ, D_MODEL), 1.0),
        'x_sample': nrm((DEC_BATCH, DEC_SEQ, D_MODEL), 1.0),
        'cache_win_k': nrm((DEPTH, DEC_BATCH, la, A_KV_HEADS, HEAD_DIM), 1.0),
        'cache_win_v': nrm((DEPTH, DEC_BATCH, la, A_KV_HEADS, HEAD_DIM), 1.0),
        'cache_band_k': nrm((DEPTH, DEC_BATCH, lb, B_HEADS, HEAD_DIM), 1.0),
        'cache_band_v': nrm((DEPTH, DEC_BATCH, lb, B_HEADS, HEAD_DIM), 1.0),
        'state_ret': nrm((DEPTH, DEC_BATCH, C_HEADS, C_DK, C_DV), 0.1),
        'state_gla': nrm((DEPTH, DEC_BATCH, D_HEADS, D_DK, D_DV), 0.1),
        'cache_mem_k': nrm((DEPTH, DEC_BATCH, MEM_LEN, X_HEADS, X_HEAD_DIM), 1.0),
        'cache_mem_v': nrm((DEPTH, DEC_BATCH, MEM_LEN, X_HEADS, X_HEAD_DIM), 1.0),
        'mem_prompt': nrm((BATCH, MEM_LEN, D_MODEL), 1.0),
        'norm_mix': gain((DEPTH, D_MODEL)),
        'w_in': nrm((DEPTH, D_MODEL, IN_WIDTH), D_MODEL ** -0.5),
        'qn_a': gain((DEPTH, HEAD_DIM)),
        'kn_a': gain((DEPTH, HEAD_DIM)),
        'sink_a': nrm((DEPTH, A_HEADS), 0.5),
        'qn_b': gain((DEPTH, HEAD_DIM)),
        'kn_b': gain((DEPTH, HEAD_DIM)),
        'relbias_b': nrm((DEPTH, B_HEADS, 2 * REL_CLIP + 1), 0.5),
        'gn_c': gain((DEPTH, C_HEADS * C_DV)),
        'w_alpha_up': nrm((DEPTH, GLA_RANK, D_HEADS * D_DK), GLA_RANK ** -0.5),
        'b_alpha': nrm((DEPTH, D_HEADS * D_DK), 0.5),
        'gn_d': gain((DEPTH, D_HEADS * D_DV)),
        'w_branch': nrm((DEPTH, N_BRANCHES, BRANCH_WIDTH, D_MODEL), BRANCH_WIDTH ** -0.5),
        'w_merge': nrm((DEPTH, D_MODEL, N_BRANCHES * D_MODEL), D_MODEL ** -0.5),
        'w_out': nrm((DEPTH, D_MODEL, D_MODEL), D_MODEL ** -0.5),
        'norm_x': gain((DEPTH, D_MODEL)),
        'norm_mem': gain((DEPTH, D_MODEL)),
        'w_xq': nrm((DEPTH, D_MODEL, xw), D_MODEL ** -0.5),
        'w_xkv': nrm((DEPTH, D_MODEL, 2 * xw), D_MODEL ** -0.5),
        'qn_x': gain((DEPTH, X_HEAD_DIM)),
        'kn_x': gain((DEPTH, X_HEAD_DIM)),
        'w_xo': nrm((DEPTH, xw, D_MODEL), xw ** -0.5),
        'norm_ffn': gain((DEPTH, D_MODEL)),
        'w_up': nrm((DEPTH, D_MODEL, D_FF), D_MODEL ** -0.5),
        'w_down': nrm((DEPTH, D_FF, D_MODEL), D_FF ** -0.5),
    }

def reference(x_prompt, x_sample, cache_win_k, cache_win_v, cache_band_k, cache_band_v,
              state_ret, state_gla, cache_mem_k, cache_mem_v, mem_prompt,
              norm_mix, w_in, qn_a, kn_a, sink_a, qn_b, kn_b, relbias_b, gn_c,
              w_alpha_up, b_alpha, gn_d, w_branch, w_merge, w_out, norm_x, norm_mem,
              w_xq, w_xkv, qn_x, kn_x, w_xo, norm_ffn, w_up, w_down):
    P = dict(norm_mix=norm_mix, w_in=w_in, qn_a=qn_a, kn_a=kn_a, sink_a=sink_a, qn_b=qn_b,
             kn_b=kn_b, relbias_b=relbias_b, gn_c=gn_c, w_alpha_up=w_alpha_up, b_alpha=b_alpha,
             gn_d=gn_d, w_branch=w_branch, w_merge=w_merge, w_out=w_out, norm_x=norm_x,
             norm_mem=norm_mem, w_xq=w_xq, w_xkv=w_xkv, qn_x=qn_x, kn_x=kn_x, w_xo=w_xo,
             norm_ffn=norm_ffn, w_up=w_up, w_down=w_down)
    pos_p = jnp.arange(x_prompt.shape[1])
    pos_s = PAST_LEN + jnp.arange(x_sample.shape[1])
    xp, xs = x_prompt, x_sample
    st_p, st_s, mk_p, mv_p = [], [], [], []
    for l in range(DEPTH):
        mk, mv = _mem_kv(mem_prompt, l, P)
        mk_p.append(mk)
        mv_p.append(mv)
        xp, sp = _layer(xp, pos_p, l, P, mk, mv, None)
        xs, ss = _layer(xs, pos_s, l, P, cache_mem_k[l], cache_mem_v[l],
                        (cache_win_k[l], cache_win_v[l], cache_band_k[l], cache_band_v[l],
                         state_ret[l], state_gla[l]))
        st_p.append(sp)
        st_s.append(ss)

    def stk(states, i):
        return jnp.stack([s[i] for s in states])

    return (xp, xs,
            stk(st_p, 0), stk(st_p, 1), stk(st_p, 2), stk(st_p, 3), stk(st_p, 4), stk(st_p, 5),
            jnp.stack(mk_p), jnp.stack(mv_p),
            stk(st_s, 0), stk(st_s, 1), stk(st_s, 2), stk(st_s, 3), stk(st_s, 4), stk(st_s, 5))


_drawn_inputs = setup_inputs


def setup_inputs(seed=0):
    import zlib

    import numpy as np

    out = dict(_drawn_inputs(seed))
    spreads = {}
    factors = {'qn_a': 8.0,
     'sink_a': 64.0,
     'qn_b': 8.0,
     'gn_c': 2.736,
     'gn_d': 2.735,
     'norm_x': 8.0,
     'qn_x': 8.0}
    for name, (base, spread) in spreads.items():
        noise = np.random.default_rng([zlib.crc32(name.encode()), seed]).standard_normal(out[name].shape)
        drawn = base * np.exp(spread * noise) if base else spread * noise
        out[name] = jnp.asarray(drawn.astype(out[name].dtype))
    for name, factor in factors.items():
        out[name] = (out[name] * factor).astype(out[name].dtype)
    return out
```

```python
from contextlib import ExitStack

import numpy as np
import concourse.bass as bass
from concourse import mybir

F32 = mybir.dt.float32
F32R = mybir.dt.float32r
U8 = mybir.dt.uint8
ALU = mybir.AluOpType
ACT = mybir.ActivationFunctionType
AX = mybir.AxisListType

P = 128
D_MODEL, SEQ, DEPTH, DEC_SEQ, PAST = 1024, 512, 2, 32, 128
TOK = SEQ + DEC_SEQ
HALF = TOK // 2
NT = SEQ // P
KB = D_MODEL // P
HD = 64
MEM = 256
XH = 4
D_FF = 4 * D_MODEL
CHUNK = 64
EPS = 1e-6
NEG = -1.0e30
THETA = 10000.0
SLAB = 2048
REV = 640
RING = 2

A_Q, A_K, A_V = 0, 512, 640
B_Q, B_K, B_V = 768, 1280, 1792
C_Q, C_K, C_V, C_G = 2304, 2560, 2816, 3328
D_Q, D_K, D_V, D_G, D_A = 3840, 4096, 4352, 4864, 5376
RANK = 16
MIX = "ABCD"

IDN, ONES, BDIAG, ROT, COS, SIN = 0, 128, 256, 384, 512, 512 + TOK
KDEC = SIN + TOK
G32 = KDEC + 4 * (NT + 1)
EPSC, ONEC = G32 + 2, G32 + 3
QDEC = ONEC + 1
ZEROC = QDEC + 2 * DEC_SEQ
NCONST = ZEROC + 1
PAR_LOADS = 19

GMIX, GX, GFFN, GMEM = 0, 8, 16, 24
GQ = {"A": 32, "B": 34, "X": 36}
GK = {"A": 33, "B": 35, "X": 37}
SINK, GN, BALPHA = 40, {"C": 48, "D": 52}, 56
NPAR = 64

LEVELS = [256, 128, 64, 32, 16, 8, 4, 2, 1, 0]
MASKED = [64, 32, 16, 8, 4, 2, 1, 0]


def constants():
    c = np.zeros((P, NCONST), np.float32)
    p = np.arange(P)
    c[:, IDN:IDN + P] = np.eye(P)
    c[:, ONES:ONES + P] = 1.0
    c[:, BDIAG:BDIAG + P] = p[:, None] // HD == p[None, :] // HD
    half = HD // 2
    for m in range(P):
        k = m + half if m % HD < half else m - half
        c[k, ROT + m] = -1.0 if m % HD < half else 1.0
    freqs = np.float32(THETA) ** (-np.arange(half, dtype=np.float32) / np.float32(half))
    pos = np.concatenate([np.arange(SEQ), PAST + np.arange(DEC_SEQ)]).astype(np.float32)
    ang = (pos[None, :] * freqs[p % half][:, None]).astype(np.float32)
    c[:, COS:COS + TOK] = np.cos(ang)
    c[:, SIN:SIN + TOK] = np.sin(ang)
    log_gamma = np.log1p(-np.exp2(-5.0 - np.arange(4.0)))
    for h in range(4):
        for t in range(NT):
            c[:, KDEC + 4 * t + h] = np.exp(log_gamma[h] * (SEQ - 1 - (t * P + p))) * HD ** -0.5
        c[:DEC_SEQ, KDEC + 4 * NT + h] = np.exp(log_gamma[h] * (DEC_SEQ - 1 - p[:DEC_SEQ])) * HD ** -0.5
        rows = slice(HD * (h % 2), HD * (h % 2) + HD)
        c[rows, G32 + h // 2] = np.exp(log_gamma[h] * DEC_SEQ)
        c[rows, QDEC + DEC_SEQ * (h // 2):QDEC + DEC_SEQ * (h // 2) + DEC_SEQ] = np.exp(
            log_gamma[h] * (np.arange(DEC_SEQ) + 1.0))
    c[:, EPSC] = EPS
    c[:, ONEC] = 1.0
    mask_a = np.zeros((P, 2 * P), np.float32)
    mask_a[:CHUNK, 2 * P - CHUNK:] = NEG
    mask_a[CHUNK:, :CHUNK] = NEG
    d = np.arange(SEQ)[None, :] - p[:, None]
    decay = np.concatenate([np.where(d >= 0, np.exp(log_gamma[h] * np.maximum(d, 0)), 0.0) * HD ** -0.5
                            for h in range(4)], axis=1).astype(np.float32)
    j, i = p[:, None], p[None, :]
    masks = [(j == i) if s == 0 else ((j // (2 * s) == i // (2 * s)) & (j // s % 2 == 0) & (i // s % 2 == 1))
             for s in MASKED]
    return {"const": c, "flip": np.ascontiguousarray(np.eye(P, dtype=np.float32)[::-1]), "mask_a": mask_a, "decay": decay,
            "level_masks": np.concatenate(masks, axis=1).astype(np.float32)}



def layer_slabs():
    s = []

    def w_in(c0, n):
        s.extend(("w_in", 0, c0 + 256 * i, KB, 256) for i in range(n))

    def gates(b):
        s.extend(("w_merge", 0, D_MODEL * b + 256 * i, KB, 256) for i in range(4))

    def branch(b):
        s.extend((f"w_branch{b}", 0, 512 * i, 4, 512) for i in range(2))

    w_in(A_Q, 3), gates(0), branch(0)
    w_in(B_Q, 6), gates(1), branch(1)
    w_in(C_Q, 4), gates(2), w_in(C_G, 2), branch(2)
    w_in(D_Q, 2)
    s.append(("w_in", 0, D_A, KB, P))
    w_in(D_V, 2), gates(3), w_in(D_G, 2), branch(3)
    s.extend(("w_out", 0, 256 * i, KB, 256) for i in range(4))
    s.extend(("w_xkv", 0, 256 * i, KB, 256) for i in range(4))
    s.extend(("w_xq", 0, 256 * i, KB, 256) for i in range(2))
    s.extend(("w_xo", 0, 512 * i, 4, 512) for i in range(2))
    n = D_FF // 256
    for c in range(n + 1):
        if c < n:
            s.append(("w_up", 0, 256 * c, KB, 256))
        if c > 0:
            s.append(("w_down", 2 * (c - 1), 0, 2, D_MODEL))
    return s


def merge(dense, other):
    out, k = [], 0
    for n, d in enumerate(dense):
        out.append(d)
        while k < len(other) and k < (n + 1) * len(other) / len(dense):
            out.append(other[k])
            k += 1
    return out + other[k:]


def layer_steps():
    jobs, dense, steps = [], {}, []
    slab_of, cursor = {}, [0, 0]
    slabs = layer_slabs()

    def new(*key):
        jobs.append(key)
        return len(jobs) - 1

    def take(j, kt, width=P):
        s, b = cursor
        slab_of[j] = (s, b)
        dense[j] = kt
        b += 1
        if b * P >= slabs[s][4]:
            s, b = s + 1, 0
        cursor[:] = s, b

    def mm(*key, kt=KB, parts=1):
        j = new(*key)
        take(j, kt)
        n = kt // parts
        return j, [("mm", j, a, a + n) for a in range(0, kt, n)]

    def full(*key, kt=KB):
        j, m = mm(*key, kt=kt)
        return m + [("ev", j)]

    def small(*key):
        j = new(*key)
        return [("pe", j), ("ev", j)]

    def norm(k):
        return [("ssq", k, b) for b in range(KB)] + [("rstd", k)] + [("h", k, b) for b in range(KB + 1)]

    def gates(m, extra=()):
        out, late = [], []
        for key in [("G", m, d) for d in range(1, KB)] + list(extra):
            j, parts = mm(*key, parts=KB)
            out += parts[:1] + late + parts[1:]
            late = [("ev", j)]
        return out + late

    steps += norm(0)
    for m in MIX:
        nqk, nv = {"A": (5, 1), "B": (8, 4), "C": (4, 4), "D": (4, 4)}[m]
        pend = []
        for b in range(nqk):
            steps += full("D", m, b)
            for p in pend:
                steps += small(*p)
            nxt = []
            if m in "AB":
                nxt.append(("SS", m, b))
            if m == "A":
                nxt += [("ROT", m, q[2]) for q in pend if q[0] == "SS"]
            if m == "C":
                nxt.append(("ROT", m, b))
            pend = nxt
            if m == "B":
                steps += small("RB", b)
        if m == "D":
            steps += full("AD")
        for v in range(nv):
            steps += full("V", m, v)
            for p in pend:
                steps += small(*p)
            pend = [("ROT", m, q[2]) for q in pend if m == "A" and q[0] == "SS"] + [("TRV", m, v)]
        if m in "AB":
            pend.insert(0, ("KC", m))
        j0 = full("G", m, 0)
        steps += j0
        for p in pend:
            steps += small(*p)
        if m == "A":
            steps += [("swap",)] + small("TRK", m, 4)
        if m == "B":
            for b in range(4, 8):
                steps += small("TRK", m, b)
        if m in "AB":
            u0, n = (0, 40) if m == "A" else (40, 40)
            steps += [("vout", m)]
            steps += merge(gates(m), [("it", u0, n, i) for i in range(n + 4)])
        if m == "C":
            for hp in range(2):
                steps += small("TRKC", m, hp) + small("ST", m, hp)
            steps += [("stout", m)]
            other = [("itc", i) for i in range(4 * NT + 2)] + [("smp", m)]
            steps += merge(gates(m), other)
            for h in range(4):
                steps += small("MEAN", m, h)
            steps += sum((small("SSO", m, h) for h in range(4)), [])
            for h in range(4):
                steps += full("GG", m, h)
        if m == "D":
            per = [[], []]
            for hp in range(2):
                steps += small("LA", hp)
                lv = [("lv", hp, i) for i in range(len(LEVELS) + 1)]
                lv += [("avd", hp, e) for e in range(2)]
                out, late = [], []
                for d in (range(1, 4) if hp == 0 else range(4, KB)):
                    j, parts = mm("G", m, d, parts=KB)
                    out += parts[:1] + late + parts[1:]
                    late = [("ev", j)]
                steps += merge(out, lv) + late
                steps += [("kst", hp)] + small("TRKS", m, hp) + small("ST", m, hp)
            steps += [("stout", m), ("smp", m), ("memload",)]
            for h in range(4):
                steps += small("SSO", m, h)
            for h in range(4):
                steps += full("GG", m, h)
        if m != "D":
            steps += [("table", m)]
        for d in range(KB):
            steps += full("BR", m, d, kt=4)
    steps += [("memnorm",)]
    for q in range(2):
        steps += small("TM", q)
    steps += [("xcload",)]
    for d in range(KB):
        steps += full("O", d)
        if d > 0:
            steps.append(("ssq", 1, d - 1))
    for b in range(4):
        steps += full("KV", b)
        if b == 0:
            steps += [("ssq", 1, KB - 1), ("rstd", 1)]
        if b > 0:
            steps += small("SSK", b - 1)
    steps += [("h", 1, b) for b in range(KB + 1)]
    for b in range(4, 8):
        steps += full("KV", b)
        if b == 4:
            steps += small("SSK", 3)
        else:
            steps += small("TRVX", b - 5)
    for b in range(4):
        steps += full("D", "X", b)
        if b == 0:
            steps += small("TRVX", 3)
        else:
            steps += small("SS", "X", b - 1)
        steps += small("TRKX", b)
    steps += small("XC", 0) + small("XC", 1) + small("SS", "X", 3)
    steps += [("zero",), ("vout", "X")] + [("it", 80, 20, i) for i in range(20 + 4)]
    for d in range(KB):
        steps += full("XO", d, kt=4)
        if d > 0:
            steps.append(("ssq", 2, d - 1))
    steps += [("ssq", 2, KB - 1), ("rstd", 2)] + [("h", 2, b) for b in range(KB + 1)]
    n = D_FF // 256
    for c in range(n + 1):
        if c < n:
            steps += full("U", 2 * c) + full("U", 2 * c + 1)
        if c > 0:
            for d in range(KB):
                steps += full("DN", c - 1, d, kt=2)
    assert cursor == [len(slabs), 0], cursor
    return steps, jobs, dense, slab_of, slabs


class InTurn:

    def __init__(self, engine, chain):
        self.engine, self.chain = engine, chain
        self.count, self.last, self.ins = {}, None, None

    def then_inc(self, sem, n, at=None):
        self.ins.then_inc(sem, n)
        self.ins = None
        self.count[sem.name] = self.count.get(sem.name, 0) + n if at is None else at
        self.last = (sem, self.count[sem.name])
        return self

    def wait(self):
        if self.ins is not None:
            self.then_inc(self.chain, 1)
        if self.last is not None:
            self.engine.wait_ge(*self.last)

    def take(self, ins):
        self.ins = ins
        return self

    def activation(self, *a, **k):
        self.wait()
        return self.take(self.engine.activation(*a, **k))

    def tensor_tensor(self, *a, **k):
        self.wait()
        return self.take(self.engine.tensor_tensor(*a, **k))

    def tensor_scalar(self, *a, **k):
        self.wait()
        return self.take(self.engine.tensor_scalar(*a, **k))

    def scalar_tensor_tensor(self, *a, **k):
        self.wait()
        return self.take(self.engine.scalar_tensor_tensor(*a, **k))

    def tensor_tensor_reduce(self, *a, **k):
        self.wait()
        return self.take(self.engine.tensor_tensor_reduce(*a, **k))

    def tensor_tensor_scan(self, *a, **k):
        self.wait()
        return self.take(self.engine.tensor_tensor_scan(*a, **k))

    def copy_predicated(self, *a, **k):
        self.wait()
        return self.take(self.engine.copy_predicated(*a, **k))

    def tensor_copy(self, *a, **k):
        self.wait()
        return self.take(self.engine.tensor_copy(*a, **k))

    def reciprocal(self, *a, **k):
        self.wait()
        return self.take(self.engine.reciprocal(*a, **k))

    def memset(self, *a, **k):
        self.wait()
        return self.take(self.engine.memset(*a, **k))


def build(nc, t_in, t_out):
    steps, jobs, dense, slab_of, slabs = layer_steps()
    job_no = {key: j for j, key in enumerate(jobs)}
    last_job_of_slab = {}
    for j, (s, _) in slab_of.items():
        last_job_of_slab[s] = max(last_job_of_slab.get(s, -1), j)
    with ExitStack() as ctx:
        def sb(name, shape, dt=F32):
            return ctx.enter_context(nc.sbuf_tensor("s_" + name, shape, dt))

        sems = []

        def sem(name):
            sems.append(ctx.enter_context(nc.semaphore(name)))
            return sems[-1]

        const = sb("const", [P, NCONST])
        lmask = sb("lmask", [P, len(MASKED) * P], U8)
        par = sb("par", [P, NPAR])
        walpha = sb("walpha", [RANK, 2 * P])
        xm = sb("xm", [P, KB, TOK])
        hhi = sb("hhi", [P, KB, TOK], F32R)
        hlo = sb("hlo", [P, KB, TOK], F32R)
        ohi = sb("ohi", [P, 4, TOK], F32R)
        olo = sb("olo", [P, 4, TOK], F32R)
        wraw = sb("wraw", [P, RING, SLAB])
        whi = sb("whi", [P, 2, SLAB], F32R)
        wlo = sb("wlo", [P, 2, SLAB], F32R)
        gt = sb("gt", [P, KB, TOK])
        tab = sb("tab", [P, 4096])
        sbuf = sb("sbuf", [P, 3, 512])
        pt = sb("pt", [P, 2, 512])
        tmp = sb("tmp", [P, 3, TOK])
        kst = sb("kst", [P, NT + 1, P])
        z = sb("z", [P, 8, TOK])
        vtm = sb("vtm", [P, NT + 1, 512])
        side = sb("side", [P, 1024])
        stat = sb("stat", [P, 4, 4])
        kct, vc = side[:, 0:512], side[:, 512:1024]
        zx = z[:, :, :].rearrange("p a b -> p (a b)")
        kx = zx[:, 4 * TOK:4 * TOK + XH * MEM].rearrange("p (h m) -> p h m", h=XH)
        kxs = zx[:, 4 * TOK + XH * MEM:4 * TOK + 2 * XH * MEM].rearrange("p (h m) -> p h m", h=XH)
        vt = vtm[:, :, :].rearrange("p a b -> p (a b)")
        vx = vt[:, 0:1024].rearrange("p (a b) -> p a b", a=2)
        vxs = vt[:, 1024:2048].rearrange("p (a b) -> p a b", a=2)
        memn_hi = ohi[:, :, :].rearrange("p a b -> p (a b)")[:, 0:KB * MEM].rearrange("p (b m) -> p b m", b=KB)
        memn_lo = olo[:, :, :].rearrange("p a b -> p (a b)")[:, 0:KB * MEM].rearrange("p (b m) -> p b m", b=KB)
        memr = tab[:, 0:2048].rearrange("p (a b) -> p a b", a=2)
        at = tab[:, :].rearrange("p (e j i) -> p e j i", e=2, j=NT)
        s0 = side[:, 0:256].rearrange("p (a b) -> p a b", a=2)
        stp = side[:, 256:512].rearrange("p (a b) -> p a b", a=2)
        sts = side[:, 512:768].rearrange("p (a b) -> p a b", a=2)
        ats = side[0:DEC_SEQ, 768:896]
        qs = side[:, 896:960].rearrange("p (a b) -> p a b", a=2)
        esm = side[:, 960:992]
        elast = side[:, 992:994]
        mss = side[:, 1000:1004]
        cum = pt[:, :, :].rearrange("p a b -> p (a b)")[:, 0:TOK]
        rs = cum
        sflat = sbuf[:, :, :].rearrange("p a b -> p (a b)")
        qkl = [sflat[:, 0:TOK], sflat[:, TOK:2 * TOK]]
        r2x = qkl
        sqx = qkl
        sq = [gt[:, 6, :], gt[:, 7, :]]
        r2 = [gt[:, 4, :], gt[:, 5, :]]
        rt = gt[:, 3, :]
        flip = gt[:, 2, 0:P]

        slot = [ctx.enter_context(nc.psum_tensor(f"slot{i}", [P, 2, 512], F32)) for i in range(2)]
        psc = ctx.enter_context(nc.psum_tensor("psc", [P, 2, 512], F32))
        pto = ctx.enter_context(nc.psum_tensor("pto", [P, 2, 512], F32))
        ptr, po = pto[:, 0, :], pto[:, 1, :]

        x_keep = nc.dram_tensor("x_keep", [P, KB, TOK], F32, kind="Internal").ap()
        rev = nc.dram_tensor("rev_bias", [DEPTH, 8, REV], F32, kind="Internal").ap()

        raw_loaded = [sem(f"raw_loaded{i}") for i in range(RING)]
        hi_done = sem("hi_done")
        slab_ready = sem("slab_ready")
        job_done = sem("job_done")
        slot_free = [sem("slot_free0"), sem("slot_free1")]
        act_chain, dve_chain = sem("act_chain"), sem("dve_chain")
        par_loaded, scale_done = sem("par_loaded"), sem("scale_done")
        sq_ready, sq_used, norm_summed, rstd_ready = sem("sq_ready"), sem("sq_used"), sem("norm_summed"), sem("rstd_ready")
        h_raw, h_hi_done, h_ready = sem("h_raw"), sem("h_hi_done"), sem("h_ready")
        x_kept, x_restored = sem("x_kept"), sem("x_restored")
        qk_rstd, qn_ready, z_ready, k_swapped = sem("qk_rstd"), sem("qn_ready"), sem("z_ready"), sem("k_swapped")
        kc_loaded, vc_loaded = sem("kc_loaded"), sem("vc_loaded")
        kst_stored, v_stored, st_stored = sem("kst_stored"), sem("v_stored"), sem("st_stored")
        tab_loaded, tab_ready = sem("tab_loaded"), sem("tab_ready")
        scored, top_found, exp_done, p_ready = sem("scored"), sem("top_found"), sem("exp_done"), sem("p_ready")
        turned, pt_ready, av_done = sem("turned"), sem("pt_ready"), sem("av_done")
        o_hi_done, o_ready = sem("o_hi_done"), sem("o_ready")
        m_ready, m_added = sem("m_ready"), sem("m_added")
        c_scored, c_ready, c_av = sem("c_scored"), sem("c_ready"), sem("c_av")
        smp_scored, smp_ready, oc_done, smp_av = sem("smp_scored"), sem("smp_ready"), sem("oc_done"), sem("smp_av")
        s0_loaded, kd_ready = sem("s0_loaded"), sem("kd_ready")
        st_ready, o_sq, o_rstd, on_ready, g_exp = sem("st_ready"), sem("o_sq"), sem("o_rstd"), sem("on_ready"), sem("g_exp")
        la_abs, la_ln, cum_ready = sem("la_abs"), sem("la_ln"), sem("cum_ready")
        dd_ready, d_exp, lv_ready, lv_scored = sem("dd_ready"), sem("d_exp"), sem("lv_ready"), sem("lv_scored")
        lv_read, d_av, oc_read = sem("lv_read"), sem("d_av"), sem("oc_read")
        kd_dd, kd_exp, q_exp = sem("kd_dd"), sem("kd_exp"), sem("q_exp")
        mem_loaded, mem_stat, mem_scaled, mn_ready = sem("mem_loaded"), sem("mem_stat"), sem("mem_scaled"), sem("mn_ready")
        u_sq, hid_ready = sem("u_sq"), sem("hid_ready")
        pro_loaded, pro_pe, pro_act, pro_dve, pro_io, pro_masks = sem("pro_loaded"), sem("pro_pe"), sem("pro_act"), sem("pro_dve"), sem("pro_io"), sem("pro_masks")

        cst = lambda c, n=P: const[:, c:c + n]

        def out_l(name, l):
            return t_out[name][bass.ds(l, 1)]

        def in_l(name, l):
            return t_in[name][bass.ds(l, 1)]

        def clear_all():
            with nc.Block() as block:
                @block.gpsimd
                def _(pool):
                    for s in sems:
                        pool.sem_clear(s)

        xrow = gt[:, :, :].rearrange("p a b -> p (a b)")[:, 0:NT * D_MODEL].rearrange("p (t d) -> p t d", t=NT)
        xrow_s = tab[0:DEC_SEQ, 0:D_MODEL]
        revt = tab[0:16, 1024:1024 + REV]
        mrow = tab[:, 2048:2048 + len(MASKED) * P]
        with nc.Block() as block:
            @block.sync
            def _(sp):
                sp.dma_start(const[:, :], t_in["const"]).then_inc(pro_loaded, 16)
                sp.dma_start(xrow, t_in["x_prompt"][0].rearrange("(t p) d -> p t d", p=P)).then_inc(pro_loaded, 16)
                sp.dma_start(xrow_s, t_in["x_sample"][0]).then_inc(pro_loaded, 16)

            @block.scalar
            def _(act):
                act.dma_start(mrow, t_in["level_masks"]).then_inc(pro_io, 16)
                rb = t_in["relbias_b"]
                with nc.allow_non_contiguous_dma(reason="2 KB of reversed rows, once"):
                    act.dma_start(revt[:, 384 - 1:REV - 1],
                                  bass.AP(rb.tensor, 256, [[257, 16], [-1, 256]])).then_inc(pro_io, 16)
                for b in range(KB):
                    act.wait_ge(pro_pe, b + 1)
                    nc.scalar.activation(xm[:, b, 0:SEQ], slot[b % 2][:, 0, :], ACT.Copy).then_inc(pro_act, 1)
                act.wait_ge(pro_dve, KB + 1)
                act.dma_start(rev.rearrange("l h m -> (l h) m")[:, 0:REV - 1],
                              revt[:, 0:REV - 1]).then_inc(pro_io, 16)
                act.wait_ge(pro_io, 48)
                act.wait_ge(pro_masks, 1)

            @block.vector
            def _(dve):
                dve.wait_ge(pro_io, 32)
                nc.vector.tensor_copy(lmask[:, :], mrow).then_inc(pro_masks, 1)
                nc.vector.tensor_copy(revt[:, 0:383], revt[:, 383:384].to_broadcast([16, 383])).then_inc(pro_dve, 1)
                for b in range(KB):
                    dve.wait_ge(pro_pe, b + 1)
                    dve.wait_ge(pro_act, b + 1)
                    nc.vector.tensor_copy(xm[:, b, SEQ:TOK], slot[b % 2][:, 1, 0:DEC_SEQ]).then_inc(pro_dve, 1)

            @block.tensor
            def _(pe):
                pe.wait_ge(pro_loaded, 48)
                for b in range(KB):
                    if b >= 2:
                        pe.wait_ge(pro_dve, b)
                    for t in range(NT):
                        pe.transpose(slot[b % 2][:, 0, t * P:(t + 1) * P], xrow[:, t, b * P:(b + 1) * P], cst(IDN))
                    pe.transpose(slot[b % 2][:, 1, 0:DEC_SEQ], xrow_s[:, b * P:(b + 1) * P],
                                 const[0:DEC_SEQ, IDN:IDN + DEC_SEQ]).then_inc(pro_pe, 1)
        clear_all()

        def unit(u):
            if u >= 80:
                v = u - 80
                return ("X", v // NT, v % NT) if v < XH * NT else ("X", v - XH * NT, NT)
            m, v = ("A", u) if u < 40 else ("B", u - 40)
            return (m, v // NT, v % NT) if v < 32 else (m, v - 32, NT)

        def rows_of(t):
            return P if t < NT else DEC_SEQ

        def key_tiles(m, t):
            if m == "X":
                return [P, P]
            if t == NT:
                return [P, DEC_SEQ]
            if m == "A":
                return [P] * min(t + 1, 2)
            return [P] * (t + 1)

        def keys_in(m, t):
            return sum(key_tiles(m, t))

        def group_end(u):
            m, h, t = unit(u)
            base = {"A": 0, "B": 5, "X": 10}[m]
            if t == NT:
                return base + 4 if h == (XH if m == "X" else 8) - 1 else None
            if t == NT - 1:
                if m == "X":
                    return base + h
                return base + h // 2 if h % 2 else None
            return None

        def group_of(u):
            m, h, t = unit(u)
            base = {"A": 0, "B": 5, "X": 10}[m]
            return base + (4 if t == NT else h if m == "X" else h // 2)

        def first_in_group(u):
            return u == 0 or group_of(u) != group_of(u - 1)

        O_READY = {"A": 5, "B": 10, "C": 14, "D": 18, "X": 23}
        GROUP_AT = lambda g: g if g < 10 else g + 8

        def freed(eng, *key):
            j = job_no[key]
            eng.wait_ge(slot_free[j % 2], j // 2 + 1)

        def arrived(eng, j):
            eng.wait_ge(job_done, j + 1)

        def frees(ins, j):
            return ins.then_inc(slot_free[j % 2], 1, at=j // 2 + 1)

        kst_jobs = [k for k in jobs if k[0] in ("TRK", "TRKC", "TRKS", "TRKX")]
        kst_no = {k: i for i, k in enumerate(kst_jobs)}
        kst_stores = {}
        n = 0
        for k in kst_jobs:
            kst_stores[k] = n
            n += {"TRK": 2, "TRKX": 1}.get(k[0], 0)
        KST_TOTAL = n
        qkn = [k for k in jobs if k[0] in ("SS", "SSK")]
        qkn_no = {k: i for i, k in enumerate(qkn)}
        rot_no = {k: i for i, k in enumerate([k for k in jobs if k[0] == "ROT"])}

        with nc.Fori(0, DEPTH) as l:
            with nc.Block() as block:

                @block.sync
                def _(sp):
                    for s, (name, rb, c0, kt, width) in enumerate(slabs):
                        if s >= RING:
                            sp.wait_ge(slab_ready, s - RING + 1)
                        if name.startswith("w_branch"):
                            w = t_in["w_branch"][bass.ds(l, 1), int(name[-1])].rearrange("o k n -> (o k) n")
                        else:
                            w = in_l(name, l).rearrange("o k n -> (o k) n")
                        w = w[rb * P:(rb + kt) * P, :].rearrange("(k p) n -> p k n", p=P)
                        dst = wraw[:, s % RING, 0:kt * width].rearrange("p (k n) -> p k n", k=kt)
                        if c0 == D_A and name == "w_in":
                            sp.dma_start(dst[:, :, 0:RANK], w[:, :, D_A:D_A + RANK]).then_inc(raw_loaded[s % RING], 16)
                            sp.dma_start(dst[:, :, RANK:P], w[:, :, D_A - (P - RANK):D_A]).then_inc(raw_loaded[s % RING], 16)
                        else:
                            sp.dma_start(dst, w[:, :, c0:c0 + width]).then_inc(raw_loaded[s % RING], 16)

                @block.gpsimd
                def _(pool):
                    loads = [0] * RING
                    zero = const[:, ZEROC:ZEROC + 1]
                    for s, (name, rb, c0, kt, width) in enumerate(slabs):
                        n = kt * width
                        loads[s % RING] += 2 if (name == "w_in" and c0 == D_A) else 1
                        pool.wait_ge(raw_loaded[s % RING], 16 * loads[s % RING])
                        if s >= 2:
                            pool.wait_ge(job_done, last_job_of_slab[s - 2] + 1)
                        nc.gpsimd.tensor_tensor(whi[:, s % 2, 0:n], wraw[:, s % RING, 0:n],
                                                zero.to_broadcast([P, n]), ALU.add).then_inc(hi_done, 1)
                        pool.wait_ge(hi_done, s + 1)
                        nc.gpsimd.tensor_tensor(wlo[:, s % 2, 0:n], wraw[:, s % RING, 0:n],
                                                whi[:, s % 2, 0:n].bitcast(F32), ALU.subtract).then_inc(slab_ready, 1)

                @block.tensor
                def _(pe):
                    def begin(j):
                        if j >= 2:
                            pe.wait_ge(slot_free[j % 2], j // 2)
                        return slot[j % 2]

                    waited = [0]

                    def dense_part(j, k0, k1):
                        key = jobs[j]
                        s, blk = slab_of[j]
                        _, _, _, kt, width = slabs[s]
                        if k0 == 0:
                            begin(j)
                        if waited[0] < s + 1:
                            pe.wait_ge(slab_ready, s + 1)
                            waited[0] = s + 1
                        if key[0] == "BR":
                            pe.wait_ge(o_ready, O_READY[key[1]])
                        if key[0] == "XO":
                            pe.wait_ge(o_ready, O_READY["X"])
                        if key[0] == "DN":
                            pe.wait_ge(hid_ready, 2 * key[1] + 2)
                        if key[0] == "KV":
                            pe.wait_ge(mn_ready, KB)
                        mem = key[0] == "KV"
                        if mem:
                            src_hi, src_lo, parts = memn_hi, memn_lo, [(0, 0, MEM)]
                        elif key[0] in ("BR", "XO", "DN"):
                            src_hi, src_lo, parts = ohi, olo, [(0, 0, HALF), (1, HALF, HALF)]
                        else:
                            src_hi, src_lo, parts = hhi, hlo, [(0, 0, HALF), (1, HALF, HALF)]
                        first_use = key in (("D", "A", 0), ("D", "X", 0), ("U", 0))
                        norm_k = {"A": 0, "X": 1}.get(key[1] if key[0] == "D" else None, 2)
                        for k in range(k0, k1):
                            if first_use:
                                pe.wait_ge(h_ready, KB * norm_k + k + 1)
                            if key == ("O", 0):
                                pe.wait_ge(m_ready, k + 1)
                            w0 = k * width + blk * P
                            kk = k + 2 * (key[1] % 2) if key[0] == "DN" else k
                            for w, src in ((whi, src_hi), (whi, src_lo), (wlo, src_hi)):
                                for half, c0, n in parts:
                                    ins = pe.matmul(slot[j % 2][:, half, 0:n], w[:, s % 2, w0:w0 + P],
                                                    src[:, kk, c0:c0 + n],
                                                    start=(k == 0 and w is whi and src is src_hi),
                                                    stop=(k == kt - 1 and w is wlo))
                        if k1 == kt:
                            ins.then_inc(job_done, 1)

                    def both_halves(ps, lhs, rhs, n=TOK):
                        if n == MEM:
                            return pe.matmul(ps[:, 0, 0:MEM], lhs, rhs[:, 0:MEM], start=True, stop=True)
                        m = lhs.shape[1]
                        for half in range(2):
                            ins = pe.matmul(ps[0:m, half, 0:HALF], lhs, rhs[:, half * HALF:(half + 1) * HALF],
                                            start=True, stop=True)
                        return ins

                    def turn_tokens(ps, src):
                        for t in range(NT):
                            pe.transpose(ps[:, 0, t * P:(t + 1) * P], src[:, t * P:(t + 1) * P], cst(IDN))
                        return pe.transpose(ps[0:DEC_SEQ, 1, 0:P], src[:, SEQ:TOK], cst(IDN))

                    def scores(u):
                        m, h, t = unit(u)
                        rows = rows_of(t)
                        n = keys_in(m, t)
                        if u >= 2:
                            pe.wait_ge(top_found, u - 1)
                        bank = psc[0:rows, u % 2, :]
                        q0 = t * P
                        if m == "X":
                            if u == 80:
                                pe.wait_ge(qn_ready, qkn_no[("SS", "X", 3)] + 1)
                                freed(pe, "XC", 1)
                            q = z[:, h, q0:q0 + rows]
                            keys = kxs[:, h, :] if t == NT else kx[:, h, :]
                            ins = pe.matmul(bank[:, 0:n], q, keys, start=True, stop=True)
                        else:
                            o = HD * (h % 2)
                            q = z[o:o + HD, h // 2, q0:q0 + rows]
                            if m == "A":
                                if u == 0:
                                    pe.wait_ge(z_ready, rot_no[("ROT", "A", 4)] + 1)
                                    pe.wait_ge(k_swapped, 1)
                                    freed(pe, "KC", "A")
                                kb = 4 if h // 4 == h % 2 else 6
                                kc = kct[o:o + HD, 0:P] if kb == 4 else kct[o:o + HD, P:2 * P]
                                k0 = max(t - 1, 0) * P
                            else:
                                if u == 40:
                                    pe.wait_ge(qn_ready, qkn_no[("SS", "B", 7)] + 1)
                                    freed(pe, "KC", "B")
                                kb = 4 + h // 2
                                kc = kct[o:o + HD, (h // 2) * P:(h // 2 + 1) * P]
                                k0 = 0
                            if t < NT:
                                ins = pe.matmul(bank[:, 0:n], q, z[o:o + HD, kb, k0:k0 + n], start=True, stop=True)
                            else:
                                pe.matmul(bank[:, 0:P], q, kc, start=True, stop=True)
                                ins = pe.matmul(bank[:, P:P + DEC_SEQ], q, z[o:o + HD, kb, SEQ:TOK], start=True, stop=True)
                        ins.then_inc(scored, 1)

                    def turn_probs(u):
                        m, h, t = unit(u)
                        rows = rows_of(t)
                        pe.wait_ge(p_ready, u + 1)
                        if u >= 1:
                            pe.wait_ge(pt_ready, u)
                        c = 0
                        for i, wdt in enumerate(key_tiles(m, t)):
                            ins = pe.transpose(ptr[0:wdt, i * P:i * P + rows], sbuf[0:rows, u % 3, c:c + wdt],
                                               const[0:rows, IDN:IDN + rows])
                            c += wdt
                        ins.then_inc(turned, 1)

                    def values(u):
                        m, h, t = unit(u)
                        rows = rows_of(t)
                        pe.wait_ge(pt_ready, u + 1)
                        if first_in_group(u):
                            if group_of(u) > 0:
                                g = group_of(u)
                                pe.wait_ge(o_ready, GROUP_AT(g))
                            if u in (0, 40, 80):
                                if m == "X":
                                    freed(pe, "TRVX", 3)
                                    pe.wait_ge(vc_loaded, 48)
                                else:
                                    freed(pe, "TRV", m, 0 if m == "A" else 3)
                                    pe.wait_ge(vc_loaded, 16 if m == "A" else 32)
                        if m == "X":
                            v_t = [(vxs if t == NT else vx)[:, i, h * P:(h + 1) * P] for i in range(2)]
                            out = po[:, h * DEC_SEQ:(h + 1) * DEC_SEQ] if t == NT else po[:, t * P:(t + 1) * P]
                        else:
                            o = HD * (h % 2)
                            hk = h // 4 if m == "A" else h
                            c = slice(hk * HD, (hk + 1) * HD)
                            if t == NT:
                                v_t = [vc[:, c], vtm[0:DEC_SEQ, NT, c]]
                                out = po[o:o + HD, (h // 2) * DEC_SEQ:(h // 2 + 1) * DEC_SEQ]
                            else:
                                first = max(t - 1, 0) if m == "A" else 0
                                v_t = [vtm[:, i, c] for i in range(first, t + 1)]
                                out = po[o:o + HD, t * P:(t + 1) * P]
                        for i, (v, wdt) in enumerate(zip(v_t, key_tiles(m, t))):
                            ins = pe.matmul(out, v, pt[0:wdt, u % 2, i * P:i * P + rows],
                                            start=(i == 0), stop=(i == len(v_t) - 1))
                        ins.then_inc(av_done, 1)

                    for st in steps:
                        kind = st[0]
                        if kind == "mm":
                            dense_part(*st[1:])
                        elif kind == "ssq":
                            k, b = st[1:]
                            pe.wait_ge(sq_ready, KB * k + b + 1)
                            for half in range(2):
                                ins = pe.matmul(pto[:, half, 0:HALF], cst(ONES), sqx[b % 2][:, half * HALF:(half + 1) * HALF],
                                                start=(b == 0), stop=(b == KB - 1))
                            ins.then_inc(norm_summed if b == KB - 1 else sq_used, 1)
                        elif kind == "it":
                            _, u0, n, i = st
                            if i < n:
                                scores(u0 + i)
                            if 0 <= i - 2 < n:
                                turn_probs(u0 + i - 2)
                            if 0 <= i - 3 < n:
                                values(u0 + i - 3)
                        elif kind == "itc":
                            i = st[1]
                            if i < 4 * NT:
                                h, jt = divmod(i, NT)
                                o = HD * (h % 2)
                                if i == 0:
                                    pe.wait_ge(z_ready, rot_no[("ROT", "C", 3)] + 1)
                                if i >= 2:
                                    pe.wait_ge(c_ready, i - 1)
                                pe.matmul(psc[:, i % 2, 0:SEQ - jt * P], z[o:o + HD, 2 + h // 2, jt * P:(jt + 1) * P],
                                          z[o:o + HD, h // 2, jt * P:SEQ], start=True, stop=True).then_inc(c_scored, 1)
                            if 1 <= i <= 4 * NT:
                                h, jt = divmod(i - 1, NT)
                                pe.wait_ge(c_ready, i)
                                if jt == 0 and h > 0:
                                    pe.wait_ge(oc_done, h)
                                if i == 1:
                                    freed(pe, "TRV", "C", 3)
                                pe.matmul(po[:, jt * P:SEQ], vtm[:, jt, h * P:(h + 1) * P], sbuf[:, (i - 1) % 3, 0:SEQ - jt * P],
                                          start=(jt == 0), stop=(jt == NT - 1)).then_inc(c_av, 1)
                        elif kind == "lv":
                            _, hp, i = st
                            if i == len(LEVELS):
                                continue
                            s = LEVELS[i]
                            n = hp * len(LEVELS) + i
                            if s:
                                pe.wait_ge(lv_ready, hp * (len(LEVELS) - 1) + i + 1)
                            if n > 0:
                                pe.wait_ge(lv_read, n)
                            if hp == 1 and i == 0:
                                pe.wait_ge(oc_done, 7)
                            for e in range(2):
                                r = slice(HD * e, HD * e + HD)
                                k_s = qkl[i % 2] if s else z[:, 2 + hp, :]
                                q_s = qkl[i % 2] if s else z[:, hp, :]
                                if s == 256:
                                    tiles = [(0, 256, 0, 256), (1, 256, 256, 256)]
                                elif s == 128:
                                    tiles = [(0, 128, 0, 128), (2, 384, 128, 128)]
                                else:
                                    tiles = [(jt, jt * P, jt * P, P) for jt in range(NT)]
                                for jt, i0, c0, w in tiles:
                                    ins = pe.matmul(psc[:, e, c0:c0 + w], k_s[r, jt * P:(jt + 1) * P], q_s[r, i0:i0 + w],
                                                    start=True, stop=True)
                                if s <= 16:
                                    ins = pe.matmul(pto[0:DEC_SEQ, e, 0:DEC_SEQ], k_s[r, SEQ:TOK],
                                                    q_s[r, SEQ:TOK], start=True, stop=True)
                            ins.then_inc(lv_scored, 1)
                        elif kind == "avd":
                            _, hp, e = st
                            h = 2 * hp + e
                            pe.wait_ge(lv_read, (hp + 1) * len(LEVELS))
                            if h == 0:
                                freed(pe, "TRV", "D", 3)
                            else:
                                pe.wait_ge(oc_done, 5 + h)
                            for jt in range(NT):
                                ins = pe.matmul(po[:, jt * P:SEQ], vtm[:, jt, h * P:(h + 1) * P], at[:, e, jt, jt * P:SEQ],
                                                start=(jt == 0), stop=(jt == NT - 1))
                            ins.then_inc(d_av, 1)
                        elif kind == "smp":
                            m = st[1]
                            if m == "C":
                                for h in range(4):
                                    r = slice(HD * (h % 2), HD * (h % 2) + HD)
                                    c = h // 2 * DEC_SEQ
                                    ins = pe.matmul(psc[0:DEC_SEQ, h % 2, c:c + DEC_SEQ], z[r, 2 + h // 2, SEQ:TOK],
                                                    z[r, h // 2, SEQ:TOK], start=True, stop=True)
                                ins.then_inc(smp_scored, 1)
                            pe.wait_ge(smp_ready, 2 if m == "C" else 4)
                            pe.wait_ge(oc_done, 4 if m == "C" else 9)
                            pe.wait_ge(s0_loaded, 16 if m == "C" else 32)
                            for h in range(4):
                                r = slice(HD * (h % 2), HD * (h % 2) + HD)
                                out = po[:, h * DEC_SEQ:(h + 1) * DEC_SEQ]
                                n = 8 * (m == "D") + 2 * h
                                pe.matmul(out, vtm[0:DEC_SEQ, NT, h * P:(h + 1) * P], ats[:, h * DEC_SEQ:(h + 1) * DEC_SEQ],
                                          start=True, stop=False).then_inc(smp_av, 1)
                                pe.wait_ge(smp_av, n + 1)
                                pe.matmul(out, s0[r, h // 2, :], qs[r, h // 2, :], start=False, stop=True).then_inc(smp_av, 1)
                                pe.wait_ge(smp_av, n + 2)
                        elif kind == "pe":
                            j = st[1]
                            key = jobs[j]
                            ps = begin(j)
                            what = key[0]
                            if what == "SS":
                                m, b = key[1:]
                                freed(pe, "D", m, b)
                                ins = both_halves(ps, cst(ONES if m == "X" else BDIAG), sq[b % 2])
                            elif what == "SSK":
                                freed(pe, "KV", key[1])
                                ins = both_halves(ps, cst(ONES), sq[key[1] % 2], MEM)
                            elif what == "ROT":
                                m, b = key[1:]
                                if m == "A":
                                    pe.wait_ge(qn_ready, qkn_no[("SS", "A", b)] + 1)
                                else:
                                    freed(pe, "D", m, b)
                                ins = both_halves(ps, cst(ROT), z[:, b, :])
                            elif what == "TRV":
                                m, v = key[1:]
                                freed(pe, "V", m, v)
                                ins = turn_tokens(ps, tmp[:, v % 2, :])
                            elif what == "TRK":
                                if key[1] == "A":
                                    pe.wait_ge(z_ready, rot_no[("ROT", "A", 4)] + 1)
                                else:
                                    pe.wait_ge(qn_ready, qkn_no[("SS", "B", key[2])] + 1)
                                ins = turn_tokens(ps, z[:, key[2], :])
                            elif what == "TRKC":
                                pe.wait_ge(z_ready, rot_no[("ROT", "C", 3)] + 1)
                                ins = turn_tokens(ps, z[:, 2 + key[2], :])
                            elif what == "TRKS":
                                pe.wait_ge(kd_ready, key[2] + 1)
                                ins = turn_tokens(ps, qkl[0])
                            elif what == "ST":
                                m, hp = key[1:]
                                if m == "C":
                                    freed(pe, "TRKC", m, hp)
                                else:
                                    freed(pe, "TRKS", m, hp)
                                    freed(pe, "TRV", m, 3)
                                if m == "C":
                                    freed(pe, "TRV", m, 3)
                                for e in range(2):
                                    h = 2 * hp + e
                                    r = slice(HD * e, HD * e + HD)
                                    for t in range(NT):
                                        pe.matmul(ps[r, 0, 0:P], kst[:, t, r], vtm[:, t, h * P:(h + 1) * P],
                                                  start=(t == 0), stop=(t == NT - 1))
                                    ins = pe.matmul(ps[r, 1, 0:P], kst[0:DEC_SEQ, NT, r], vtm[0:DEC_SEQ, NT, h * P:(h + 1) * P],
                                                    start=True, stop=True)
                            elif what == "RB":
                                pe.wait_ge(tab_loaded, 48)
                                h = key[1]
                                ins = pe.matmul(ps[:, 0, :], flip, tab[:, h * 512:(h + 1) * 512], start=True, stop=True)
                            elif what == "KC":
                                nb = 1 if key[1] == "A" else 4
                                pe.wait_ge(kc_loaded, 16 if key[1] == "A" else 32)
                                for b in range(nb):
                                    ins = pe.transpose(ps[:, 0, b * P:(b + 1) * P],
                                                       kst[:, b, :], cst(IDN))
                            elif what == "MEAN":
                                pe.wait_ge(oc_done, 5)
                                ins = both_halves(ps, cst(ONES), z[:, 4 + key[2], :])
                            elif what == "SSO":
                                m, h = key[1:]
                                pe.wait_ge(o_sq, h + 1 + (4 if m == "D" else 0))
                                ins = both_halves(ps, cst(ONES), tmp[:, h % 2, :])
                            elif what == "LA":
                                hp = key[1]
                                freed(pe, "AD")
                                ins = both_halves(ps, walpha[:, hp * P:(hp + 1) * P], tmp[0:RANK, 2, :])
                            elif what == "TM":
                                q = key[1]
                                pe.wait_ge(mem_scaled, 2)
                                for bb in range(4):
                                    for t in range(2):
                                        c = (4 * q + bb) * P
                                        ins = pe.transpose(ps[:, bb // 2, (bb % 2) * 256 + t * P:(bb % 2) * 256 + (t + 1) * P],
                                                           memr[:, t, c:c + P], cst(IDN))
                            elif what == "TRVX":
                                v = key[1]
                                freed(pe, "KV", 4 + v)
                                for t in range(2):
                                    ins = pe.transpose(ps[:, 0, t * P:(t + 1) * P], tmp[:, v % 2, t * P:(t + 1) * P], cst(IDN))
                            elif what == "TRKX":
                                b = key[1]
                                pe.wait_ge(qn_ready, qkn_no[("SSK", b)] + 1)
                                for t in range(2):
                                    ins = pe.transpose(ps[:, 0, t * P:(t + 1) * P], kx[:, b, t * P:(t + 1) * P], cst(IDN))
                            elif what == "XC":
                                pe.wait_ge(kc_loaded, 48)
                                for hh in range(2):
                                    for t in range(2):
                                        c = t * 512 + (2 * key[1] + hh) * P
                                        ins = pe.transpose(ps[:, 0, hh * 256 + t * P:hh * 256 + (t + 1) * P], side[:, c:c + P], cst(IDN))
                            ins.then_inc(job_done, 1)

                @block.scalar
                def _(act):
                    turn = InTurn(act, act_chain)
                    A = turn.activation

                    def load_params():
                        for c, name in ((GMIX, "norm_mix"), (GX, "norm_x"), (GFFN, "norm_ffn"), (GMEM, "norm_mem")):
                            act.dma_start(par[:, c:c + KB], in_l(name, l).rearrange("o (b p) -> p (o b)", p=P)).then_inc(par_loaded, 16)
                        for c, name in ((GQ["A"], "qn_a"), (GK["A"], "kn_a"), (GQ["B"], "qn_b"), (GK["B"], "kn_b")):
                            for e in range(2):
                                act.dma_start(par[HD * e:HD * e + HD, c:c + 1], in_l(name, l).rearrange("o p -> p o")).then_inc(par_loaded, 16)
                        for c, name in ((GQ["X"], "qn_x"), (GK["X"], "kn_x")):
                            act.dma_start(par[:, c:c + 1], in_l(name, l).rearrange("o p -> p o")).then_inc(par_loaded, 16)
                        act.dma_start(par[:, SINK:SINK + 8], in_l("sink_a", l).to_broadcast([P, 8])).then_inc(par_loaded, 16)
                        for c, name in ((GN["C"], "gn_c"), (GN["D"], "gn_d")):
                            act.dma_start(par[:, c:c + 4], in_l(name, l).rearrange("o (b p) -> p (o b)", p=P)).then_inc(par_loaded, 16)
                        act.dma_start(par[:, BALPHA:BALPHA + 2], in_l("b_alpha", l).rearrange("o (b p) -> p (o b)", p=P)).then_inc(par_loaded, 16)
                        act.dma_start(walpha[:, :], in_l("w_alpha_up", l).rearrange("o r n -> (o r) n")).then_inc(par_loaded, 16)

                    nc.scalar.preload_act_table_set("natural_log_exp_and_others")
                    with nc.allow_non_contiguous_dma(reason="a few KB of gains per layer, one element per partition"):
                        load_params()
                    act.dma_start(x_keep, xm[:, :, :]).then_inc(x_kept, 16)
                    act.dma_start(tab[:, 0:2 * P], t_in["mask_a"]).then_inc(tab_loaded, 16)
                    act.dma_start(kst[:, 0, :], in_l("cache_win_k", l)[:, 0].rearrange("o t h d -> (o t) (h d)")).then_inc(kc_loaded, 16)
                    act.dma_start(vc[:, 0:P], in_l("cache_win_v", l)[:, 0].rearrange("o t h d -> (o t) (h d)")).then_inc(vc_loaded, 16)
                    act.wait_ge(par_loaded, 16 * PAR_LOADS)
                    n_group = [0]

                    def evac_group(u):
                        g = group_end(u)
                        m, h, t = unit(u)
                        act.wait_ge(av_done, u + 1)
                        if t == NT:
                            ins = A(ohi[:, 0:4, SEQ:TOK], po[:, 0:4 * DEC_SEQ].rearrange("p (a b) -> p a b", a=4), ACT.Copy)
                        else:
                            blk = h if m == "X" else h // 2
                            ins = A(ohi[:, blk, 0:SEQ], po[:, :], ACT.Copy)
                        ins.then_inc(o_hi_done, 1)

                    def exp_unit(u):
                        m, h, t = unit(u)
                        rows, n = rows_of(t), keys_in(m, t)
                        act.wait_ge(top_found, u + 1)
                        s = sbuf[0:rows, u % 3, 0:n]
                        nm = stat[0:rows, u % 4, 1:2]
                        if m == "A":
                            A(stat[0:rows, u % 4, 3:4], par[0:rows, SINK + h:SINK + h + 1], ACT.Exp, bias=nm)
                        A(s, s, ACT.Exp, bias=nm, accum_out=stat[0:rows, u % 4, 2:3]).then_inc(exp_done, 1)

                    def evac_turned(u):
                        m, h, t = unit(u)
                        rows = rows_of(t)
                        act.wait_ge(turned, u + 1)
                        if u >= 2:
                            act.wait_ge(av_done, u - 1)
                        tiles = key_tiles(m, t)
                        if t < NT:
                            w = len(tiles) * P
                            A(pt[:, u % 2, 0:w], ptr[:, 0:w], ACT.Copy).then_inc(pt_ready, 1)
                        elif m == "X":
                            A(pt[:, u % 2, 0:2 * P].rearrange("p (a b) -> p a b", a=2)[:, :, 0:rows],
                              ptr[:, 0:2 * P].rearrange("p (a b) -> p a b", a=2)[:, :, 0:rows], ACT.Copy).then_inc(pt_ready, 1)
                        else:
                            A(pt[:, u % 2, 0:rows], ptr[:, 0:rows], ACT.Copy)
                            A(pt[0:DEC_SEQ, u % 2, P:P + rows], ptr[0:DEC_SEQ, P:P + rows], ACT.Copy).then_inc(pt_ready, 1)

                    for st in steps:
                        kind = st[0]
                        if kind == "ssq":
                            k, b = st[1:]
                            if k == 1:
                                freed(act, "O", b)
                            if k == 2:
                                freed(act, "XO", b)
                            if b >= 2:
                                act.wait_ge(sq_used, (KB - 1) * k + b - 1)
                            A(sqx[b % 2], xm[:, b, :], ACT.Square).then_inc(sq_ready, 1)
                        elif kind == "rstd":
                            k = st[1]
                            act.wait_ge(norm_summed, k + 1)
                            A(rs.rearrange("p (a b) -> p a b", a=2), pto[:, :, 0:HALF], ACT.Ln,
                                   bias=const[:, EPSC:EPSC + 1], scale=1.0 / D_MODEL)
                            A(rs, rs, ACT.Exp, scale=-0.5).then_inc(rstd_ready, 1)
                        elif kind == "h":
                            k, b = st[1:]
                            if b < KB:
                                act.wait_ge(h_raw, KB * k + b + 1)
                                A(hhi[:, b, :], tmp[:, b % 3, :], ACT.Copy).then_inc(h_hi_done, 1)
                        elif kind == "it":
                            _, u0, n, i = st
                            if 0 <= i - 4 < n and group_end(u0 + i - 4) is not None:
                                evac_group(u0 + i - 4)
                            if i < n:
                                exp_unit(u0 + i)
                            if 0 <= i - 2 < n:
                                evac_turned(u0 + i - 2)
                        elif kind == "itc":
                            i = st[1]
                            if i >= 1 + NT and (i - 1) % NT == 0:
                                h = (i - 1) // NT - 1
                                act.wait_ge(c_av, NT * (h + 1))
                                A(z[:, 4 + h, 0:SEQ], po[:, :], ACT.Copy).then_inc(oc_done, 1)
                        elif kind == "avd":
                            _, hp, e = st
                            h = 2 * hp + e
                            act.wait_ge(d_av, h + 1)
                            A(z[:, 4 + h, 0:SEQ], po[:, :], ACT.Copy).then_inc(oc_done, 1)
                        elif kind == "smp":
                            m = st[1]
                            act.wait_ge(smp_av, 8 if m == "C" else 16)
                            A(z[:, 4:8, SEQ:TOK], po[:, 0:4 * DEC_SEQ].rearrange("p (a b) -> p a b", a=4), ACT.Copy).then_inc(oc_done, 1)
                        elif kind == "lv":
                            _, hp, i = st
                            if i < len(LEVELS) and LEVELS[i]:
                                s = LEVELS[i]
                                n = hp * (len(LEVELS) - 1) + i
                                act.wait_ge(dd_ready, n + 1)
                                w = SEQ if s > 16 else TOK
                                v = tmp[:, i % 2, 0:w].rearrange("p (b e s) -> p b e s", e=2, s=s)
                                A(v[:, :, 0, :], v[:, :, 0, :], ACT.Exp, scale=-1.0)
                                A(v[:, :, 1, :], v[:, :, 1, :], ACT.Exp).then_inc(d_exp, 1)
                        elif kind == "kst":
                            hp = st[1]
                            act.wait_ge(cum_ready, hp + 1)
                            A(elast[:, hp:hp + 1], cum[:, TOK - 1:TOK], ACT.Exp)
                            A(esm, cum[:, SEQ:TOK], ACT.Exp).then_inc(q_exp, 1)
                            act.wait_ge(kd_dd, hp + 1)
                            A(tmp[:, 0, :], tmp[:, 0, :], ACT.Exp, scale=-1.0).then_inc(kd_exp, 1)
                        elif kind == "swap":
                            act.wait_ge(z_ready, rot_no[("ROT", "A", 4)] + 1)
                            A(z[0:HD, 6, :], z[HD:P, 4, :], ACT.Copy)
                            A(z[HD:P, 6, :], z[0:HD, 4, :], ACT.Copy).then_inc(k_swapped, 1)
                        elif kind == "vout":
                            m = st[1]
                            if m == "X":
                                freed(act, "TRVX", 3)
                                act.dma_start(out_l("mem_v", l)[:, 0].rearrange("o (t p) h d -> p (o t) (h d)", p=P), vx).then_inc(v_stored, 16)
                            elif m == "A":
                                freed(act, "TRV", "A", 0)
                                act.dma_start(out_l("p_win_v", l)[:, 0].rearrange("o t h d -> (o t) (h d)"), vtm[:, NT - 1, 0:P]).then_inc(v_stored, 16)
                                act.dma_start(out_l("s_win_v", l)[:, 0].rearrange("o t h d -> (o t) (h d)"), vtm[0:DEC_SEQ, NT, 0:P]).then_inc(v_stored, 16)
                            else:
                                freed(act, "TRV", "B", 3)
                                act.dma_start(out_l("p_band_v", l)[:, 0].rearrange("o (t p) h d -> p (o t) (h d)", p=P), vtm[:, 0:NT, :]).then_inc(v_stored, 16)
                                act.dma_start(out_l("s_band_v", l)[:, 0].rearrange("o t h d -> (o t) (h d)"), vtm[0:DEC_SEQ, NT, :]).then_inc(v_stored, 16)
                        elif kind == "stout":
                            m = st[1]
                            name = "ret" if m == "C" else "gla"
                            act.wait_ge(st_ready, 2 if m == "C" else 4)
                            for hp in range(2):
                                freed(act, "ST", m, hp)
                            act.dma_start(out_l(f"p_state_{name}", l)[:, 0].rearrange("o (a e) d v -> (e d) (o a) v", e=2), stp).then_inc(st_stored, 16)
                            act.dma_start(out_l(f"s_state_{name}", l)[:, 0].rearrange("o (a e) d v -> (e d) (o a) v", e=2), sts).then_inc(st_stored, 16)
                        elif kind == "table":
                            m = st[1]
                            if m == "A":
                                act.wait_ge(top_found, 40)
                                act.dma_start(tab[:, :].rearrange("p (h c) -> p h c", h=8), bass.AP(
                                    rev.tensor, rev[bass.ds(l, 1)].offset, [[1, P], [REV, 8], [1, 512]])).then_inc(tab_loaded, 16)
                                act.wait_ge(kst_stored, 16 * 2)
                                act.dma_start(kst[:, 0:4, :].rearrange("p a b -> p (a b)"),
                                              in_l("cache_band_k", l)[:, 0].rearrange("o t h d -> (o t) (h d)")).then_inc(kc_loaded, 16)
                                act.dma_start(vc, in_l("cache_band_v", l)[:, 0].rearrange("o t h d -> (o t) (h d)")).then_inc(vc_loaded, 16)
                            elif m == "B":
                                act.wait_ge(top_found, 80)
                                act.dma_start(tab[:, 0:2048], t_in["decay"]).then_inc(tab_loaded, 16)
                                act.dma_start(s0, in_l("state_ret", l)[:, 0].rearrange("o (a e) d v -> (e d) (o a) v", e=2)).then_inc(s0_loaded, 16)
                            else:
                                act.wait_ge(st_stored, 32)
                                act.dma_start(s0, in_l("state_gla", l)[:, 0].rearrange("o (a e) d v -> (e d) (o a) v", e=2)).then_inc(s0_loaded, 16)
                        elif kind == "memload":
                            act.wait_ge(d_av, 4)
                            act.dma_start(memr, t_in["mem_prompt"][0].rearrange("(t p) d -> p t d", p=P)).then_inc(mem_loaded, 16)
                        elif kind == "memnorm":
                            act.wait_ge(mem_loaded, 16)
                            freed(act, "BR", "D", KB - 1)
                            for t in range(2):
                                A(gt[:, 2 * t:2 * t + 2, 0:512], memr[:, t, :].rearrange("p (a b) -> p a b", a=2), ACT.Square,
                                       accum_out=mss[:, t:t + 1])
                            A(mss[:, 2:4], mss[:, 0:2], ACT.Ln, bias=const[:, EPSC:EPSC + 1], scale=1.0 / D_MODEL)
                            A(mss[:, 0:2], mss[:, 2:4], ACT.Exp, scale=-0.5).then_inc(mem_stat, 1)
                        elif kind == "xcload":
                            act.wait_ge(st_stored, 64)
                            act.wait_ge(mem_scaled, 2)
                            act.dma_start(side[:, :].rearrange("p (t c) -> p t c", t=2),
                                          in_l("cache_mem_k", l)[:, 0].rearrange("o (t p) h d -> p (o t) (h d)", p=P)).then_inc(kc_loaded, 16)
                            act.dma_start(vxs, in_l("cache_mem_v", l)[:, 0].rearrange("o (t p) h d -> p (o t) (h d)", p=P)).then_inc(vc_loaded, 16)
                        elif kind == "ev":
                            j = st[1]
                            key = jobs[j]
                            what = key[0]
                            ps = slot[j % 2]
                            all_tok = ps[:, :, 0:HALF]

                            def tok(ap):
                                return ap.rearrange("p (a b) -> p a b", a=2)

                            if what == "D":
                                m, b = key[1:]
                                if b == 0 and m in "BCD":
                                    freed(act, "BR", MIX[MIX.index(m) - 1], KB - 1)
                                    if m == "B":
                                        act.dma_start(flip, t_in["flip"]).then_inc(tab_loaded, 16)
                                arrived(act, j)
                                if m in "ABX":
                                    if b >= 2:
                                        act.wait_ge(job_done, job_no[("SS", m, b - 2)] + 1)
                                    A(tok(z[:, b, :]), all_tok, ACT.Copy)
                                    frees(A(tok(sq[b % 2]), all_tok, ACT.Square), j)
                                elif m == "C":
                                    frees(A(tok(z[:, b, :]), all_tok, ACT.Copy), j)
                                else:
                                    frees(A(tok(z[:, b, :]), all_tok, ACT.Copy, scale=HD ** -0.5 if b < 2 else 1.0), j)
                            elif what in ("SS", "SSK"):
                                b = key[-1]
                                i = qkn_no[key]
                                arrived(act, j)
                                x_like = what == "SSK" or key[1] == "X"
                                dim = P if x_like else HD
                                if i >= 2:
                                    act.wait_ge(qn_ready, i - 1)
                                if what == "SSK":
                                    src, dst = ps[:, 0, 0:MEM], r2[i % 2][:, 0:MEM]
                                else:
                                    src, dst = all_tok, tok(r2[i % 2])
                                frees(A(dst, src, ACT.Ln, bias=const[:, EPSC:EPSC + 1], scale=1.0 / dim), j)
                                A(dst, dst, ACT.Exp, scale=-0.5).then_inc(qk_rstd, 1)
                            elif what == "V":
                                m, v = key[1:]
                                if v == 0 and m != "A":
                                    act.wait_ge(v_stored, 32 if m == "B" else 64)
                                arrived(act, j)
                                if v >= 2:
                                    act.wait_ge(job_done, job_no[("TRV", m, v - 2)] + 1)
                                frees(A(tok(tmp[:, v % 2, :]), all_tok, ACT.Copy), j)
                            elif what == "TRV":
                                m, v = key[1:]
                                arrived(act, j)
                                A(vtm[:, 0:NT, v * P:(v + 1) * P], ps[:, 0, :].rearrange("p (t c) -> p t c", t=NT), ACT.Copy)
                                frees(A(vtm[0:DEC_SEQ, NT, v * P:(v + 1) * P], ps[0:DEC_SEQ, 1, 0:P], ACT.Copy), j)
                            elif what == "TRK":
                                m, b = key[1:]
                                arrived(act, j)
                                act.wait_ge(kst_stored, 16 * kst_stores[key])
                                freed(act, "KC", m)
                                A(kst[:, 0:NT, :], ps[:, 0, :].rearrange("p (t c) -> p t c", t=NT), ACT.Copy)
                                frees(A(kst[0:DEC_SEQ, NT, :], ps[0:DEC_SEQ, 1, 0:P], ACT.Copy), j)
                                freed(act, *key)
                                if m == "A":
                                    act.dma_start(out_l("p_win_k", l)[:, 0].rearrange("o t h d -> (o t) (h d)"), kst[:, NT - 1, :]).then_inc(kst_stored, 16)
                                    act.dma_start(out_l("s_win_k", l)[:, 0].rearrange("o t h d -> (o t) (h d)"), kst[0:DEC_SEQ, NT, :]).then_inc(kst_stored, 16)
                                else:
                                    c = slice((b - 4) * P, (b - 3) * P)
                                    act.dma_start(out_l("p_band_k", l)[:, 0].rearrange("o (t p) h d -> p (o t) (h d)", p=P)[:, :, c], kst[:, 0:NT, :]).then_inc(kst_stored, 16)
                                    act.dma_start(out_l("s_band_k", l)[:, 0].rearrange("o t h d -> (o t) (h d)")[:, c], kst[0:DEC_SEQ, NT, :]).then_inc(kst_stored, 16)
                            elif what == "TRKS":
                                arrived(act, j)
                                A(kst[:, 0:NT, :], ps[:, 0, :].rearrange("p (t c) -> p t c", t=NT), ACT.Copy)
                                frees(A(kst[0:DEC_SEQ, NT, :], ps[0:DEC_SEQ, 1, 0:P], ACT.Copy), j)
                            elif what == "ST":
                                m, hp = key[1:]
                                arrived(act, j)
                                if hp == 0 and m == "D":
                                    act.wait_ge(st_stored, 32)
                                A(stp[:, hp, :], ps[:, 0, 0:P], ACT.Copy).then_inc(st_ready, 1)
                            elif what == "RB":
                                h = key[1]
                                arrived(act, j)
                                frees(A(tab[:, h * 512:(h + 1) * 512], ps[:, 0, :], ACT.Copy), j)
                            elif what == "KC":
                                m = key[1]
                                arrived(act, j)
                                if m == "A":
                                    A(kct[:, 0:P], ps[:, 0, 0:P], ACT.Copy)
                                    A(kct[0:HD, P:2 * P], ps[HD:P, 0, 0:P], ACT.Copy)
                                    frees(A(kct[HD:P, P:2 * P], ps[0:HD, 0, 0:P], ACT.Copy), j)
                                else:
                                    frees(A(kct, ps[:, 0, :], ACT.Copy), j)
                            elif what == "G":
                                arrived(act, j)
                                frees(A(tok(gt[:, key[2], :]), all_tok, ACT.Exp, scale=-1.0), j)
                            elif what == "MEAN":
                                h = key[2]
                                freed(act, *key)
                                if h < 2:
                                    A(tmp[:, h % 2, :], z[:, 4 + h, :], ACT.Square).then_inc(o_sq, 1)
                            elif what == "SSO":
                                m, h = key[1:]
                                i = h + (4 if m == "D" else 0)
                                if m == "D" and h < 2:
                                    act.wait_ge(oc_done, 10)
                                    if h == 0:
                                        for hh in range(2):
                                            A(tmp[:, hh, :], z[:, 4 + hh, :], ACT.Square).then_inc(o_sq, 1)
                                arrived(act, j)
                                if h >= 2:
                                    act.wait_ge(on_ready, i - 1)
                                frees(A(tok(r2x[h % 2]), all_tok, ACT.Ln, bias=const[:, EPSC:EPSC + 1], scale=1.0 / P), j)
                                A(r2x[h % 2], r2x[h % 2], ACT.Exp, scale=-0.5).then_inc(o_rstd, 1)
                                if h < 2:
                                    if m == "C":
                                        freed(act, "MEAN", m, h + 2)
                                    A(tmp[:, h % 2, :], z[:, 6 + h, :], ACT.Square).then_inc(o_sq, 1)
                            elif what == "GG":
                                h = key[2]
                                i = h + (4 if key[1] == "D" else 0)
                                arrived(act, j)
                                if h >= 2:
                                    act.wait_ge(o_ready, O_READY[key[1]] - 4 + h - 1)
                                A(tok(tmp[:, h % 2, :]), all_tok, ACT.Exp, scale=-1.0).then_inc(g_exp, 1)
                            elif what == "AD":
                                arrived(act, j)
                                act.wait_ge(m_added, 2 * KB)
                                frees(A(tok(tmp[0:RANK, 2, :]), ps[0:RANK, :, 0:HALF], ACT.Copy), j)
                            elif what == "LA":
                                hp = key[1]
                                arrived(act, j)
                                A(tok(tmp[:, 0, :]), all_tok, ACT.Abs, bias=par[:, BALPHA + hp:BALPHA + hp + 1]).then_inc(la_abs, 1)
                                A(tmp[:, 0, :], tmp[:, 0, :], ACT.Exp, scale=-1.0)
                                A(tmp[:, 0, :], tmp[:, 0, :], ACT.Ln, bias=const[:, ONEC:ONEC + 1]).then_inc(la_ln, 1)
                            elif what == "KV":
                                b = key[1]
                                arrived(act, j)
                                if b < 4:
                                    if b >= 2:
                                        act.wait_ge(job_done, job_no[("SSK", b - 2)] + 1)
                                    A(kx[:, b, :], ps[:, 0, 0:MEM], ACT.Copy)
                                    frees(A(sq[b % 2][:, 0:MEM], ps[:, 0, 0:MEM], ACT.Square), j)
                                else:
                                    v = b - 4
                                    if v < 2:
                                        act.wait_ge(h_ready, 2 * KB)
                                    if v >= 2:
                                        act.wait_ge(job_done, job_no[("TRVX", v - 2)] + 1)
                                    frees(A(tmp[:, v % 2, 0:MEM], ps[:, 0, 0:MEM], ACT.Copy), j)
                            elif what == "TRVX":
                                v = key[1]
                                arrived(act, j)
                                frees(A(vx[:, :, v * P:(v + 1) * P], ps[:, 0, 0:2 * P].rearrange("p (t c) -> p t c", t=2), ACT.Copy), j)
                            elif what == "TRKX":
                                b = key[1]
                                arrived(act, j)
                                act.wait_ge(kst_stored, 16 * kst_stores[key])
                                frees(A(kst[:, 0:2, :], ps[:, 0, 0:2 * P].rearrange("p (t c) -> p t c", t=2), ACT.Copy), j)
                                freed(act, *key)
                                act.dma_start(out_l("mem_k", l)[:, 0, :, b].rearrange("o (t p) d -> p (o t) d", p=P), kst[:, 0:2, :]).then_inc(kst_stored, 16)
                            elif what == "XC":
                                arrived(act, j)
                                frees(A(kxs[:, 2 * key[1]:2 * key[1] + 2, :], ps[:, 0, :].rearrange("p (h m) -> p h m", h=2), ACT.Copy), j)
                            elif what == "BR" and key[1] == "D":
                                d = key[2]
                                act.wait_ge(m_ready, d + 1)
                                act.dma_start(xm[:, d, :], x_keep[:, d, :]).then_inc(x_restored, 16)
                            elif what == "U":
                                i = key[1]
                                arrived(act, j)
                                if i >= 2:
                                    act.wait_ge(hid_ready, i - 1)
                                frees(A(tok(tmp[:, i % 2, :]), all_tok, ACT.Relu), j)
                                A(tmp[:, i % 2, :], tmp[:, i % 2, :], ACT.Square).then_inc(u_sq, 1)
                    act.wait_ge(kst_stored, 16 * KST_TOTAL)
                    act.wait_ge(v_stored, 16 * 5)
                    act.wait_ge(st_stored, 16 * 4)
                    act.wait_ge(x_kept, 16)

                @block.vector
                def _(dve):
                    V = InTurn(dve, dve_chain)

                    def tok(ap):
                        return ap.rearrange("p (a b) -> p a b", a=2)

                    def top(u):
                        m, h, t = unit(u)
                        rows, n = rows_of(t), keys_in(m, t)
                        dve.wait_ge(scored, u + 1)
                        if u >= 3:
                            dve.wait_ge(turned, u - 2)
                        if u == 0:
                            dve.wait_ge(tab_loaded, 16)
                        if m == "A":
                            c0 = 0 if t == NT or t > 0 else P
                            table = tab[0:rows, c0:c0 + n]
                        elif m == "B":
                            c0 = h * 512 + (256 if t == NT else 384 - t * P)
                            table = tab[0:rows, c0:c0 + n]
                        else:
                            table = tab[0:rows, 2048:2048 + n]
                        st_ = stat[0:rows, u % 4, :]
                        V.tensor_tensor_reduce(out=sbuf[0:rows, u % 3, 0:n], in0=psc[0:rows, u % 2, 0:n], in1=table,
                                                    scale=1.0, scalar=-3.0e38, op0=ALU.add, op1=ALU.max, accum_out=st_[:, 0:1])
                        if m == "A":
                            ins = V.tensor_scalar(st_[:, 1:2], st_[:, 0:1], par[0:rows, SINK + h:SINK + h + 1], -1.0, ALU.max, ALU.mult)
                        else:
                            ins = V.tensor_scalar(st_[:, 1:2], st_[:, 0:1], -1.0, None, ALU.mult)
                        ins.then_inc(top_found, 1)

                    def normalise(u):
                        m, h, t = unit(u)
                        rows, n = rows_of(t), keys_in(m, t)
                        dve.wait_ge(exp_done, u + 1)
                        st_ = stat[0:rows, u % 4, :]
                        if m == "A":
                            V.tensor_tensor(st_[:, 2:3], st_[:, 2:3], st_[:, 3:4], ALU.add)
                        V.reciprocal(st_[:, 3:4], st_[:, 2:3])
                        s = sbuf[0:rows, u % 3, 0:n]
                        V.tensor_scalar(s, s, st_[:, 3:4], None, ALU.mult).then_inc(p_ready, 1)

                    def evac_group(u):
                        m, h, t = unit(u)
                        g = group_end(u)
                        dve.wait_ge(o_hi_done, g + 1)
                        if t == NT:
                            o, s = (slice(0, 4), slice(SEQ, TOK)), po[:, 0:4 * DEC_SEQ].rearrange("p (a b) -> p a b", a=4)
                        else:
                            o, s = (h if m == "X" else h // 2, slice(0, SEQ)), po[:, :]
                        V.tensor_tensor(olo[:, o[0], o[1]], s, ohi[:, o[0], o[1]].bitcast(F32), ALU.subtract).then_inc(o_ready, 1)

                    def level_read(hp, i):
                        s = LEVELS[i]
                        dve.wait_ge(lv_scored, hp * len(LEVELS) + i + 1)
                        base = at[:, 0, 0, :]
                        for e in range(2):
                            def cells(off, stride, count, w):
                                return bass.AP(base.tensor, base.offset + e * 2048 + off, [[4096, P], [stride, count], [1, w]])

                            if s == 256:
                                ins = V.tensor_copy(cells(256, 512, 2, 256), psc[:, e, :].rearrange("p (a b) -> p a b", a=2))
                            elif s == 128:
                                ins = V.tensor_copy(cells(128, 1280, 2, P), psc[:, e, 0:256].rearrange("p (a b) -> p a b", a=2))
                            else:
                                mk = lmask[:, MASKED.index(s) * P:(MASKED.index(s) + 1) * P]
                                ins = V.copy_predicated(cells(0, 640, 4, P), mk.unsqueeze(1).to_broadcast([P, 4, P]),
                                                        psc[:, e, :].rearrange("p (a b) -> p a b", a=4))
                        if s <= 16:
                            mk = lmask[0:DEC_SEQ, MASKED.index(s) * P:MASKED.index(s) * P + DEC_SEQ]
                            ins = V.copy_predicated(ats[:, hp * 64:(hp + 1) * 64].rearrange("p (a b) -> p a b", a=2),
                                                    mk.unsqueeze(1).to_broadcast([DEC_SEQ, 2, DEC_SEQ]),
                                                    pto[0:DEC_SEQ, :, 0:DEC_SEQ])
                        ins.then_inc(lv_read, 1)

                    dve.wait_ge(par_loaded, 16 * PAR_LOADS)
                    for m, dim in (("A", HD), ("B", HD), ("X", P)):
                        c = GQ[m]
                        V.tensor_scalar(par[:, c:c + 1], par[:, c:c + 1], dim ** -0.5, None, ALU.mult).then_inc(scale_done, 1)

                    for st in steps:
                        kind = st[0]
                        if kind == "h":
                            k, b = st[1:]
                            g = (GMIX, GX, GFFN)[k]
                            if b == 0:
                                dve.wait_ge(rstd_ready, k + 1)
                            if b < KB:
                                V.scalar_tensor_tensor(out=tmp[:, b % 3, :], in0=xm[:, b, :], scalar=par[:, g + b:g + b + 1],
                                                       in1=rs, op0=ALU.mult, op1=ALU.mult).then_inc(h_raw, 1)
                            if b >= 1:
                                dve.wait_ge(h_hi_done, KB * k + b)
                                V.tensor_tensor(hlo[:, b - 1, :], tmp[:, (b - 1) % 3, :], hhi[:, b - 1, :].bitcast(F32),
                                                ALU.subtract).then_inc(h_ready, 1)
                        elif kind == "it":
                            _, u0, n, i = st
                            if u0 == 40 and i == 0:
                                for h in (6, 7):
                                    freed(dve, "RB", h)
                                V.memset(tab[0:CHUNK, :].rearrange("p (h c) -> p h c", h=8)[:, :, 448:512], NEG)
                            if 0 <= i - 4 < n and group_end(u0 + i - 4) is not None:
                                evac_group(u0 + i - 4)
                            if i < n:
                                top(u0 + i)
                            if 0 <= i - 1 < n:
                                normalise(u0 + i - 1)
                        elif kind == "itc":
                            i = st[1]
                            if i < 4 * NT:
                                h, jt = divmod(i, NT)
                                dve.wait_ge(c_scored, i + 1)
                                if i == 0:
                                    dve.wait_ge(tab_loaded, 64)
                                if i >= 3:
                                    dve.wait_ge(c_av, i - 2)
                                w = SEQ - jt * P
                                V.tensor_tensor(sbuf[:, i % 3, 0:w], psc[:, i % 2, 0:w], tab[:, h * 512:h * 512 + w], ALU.mult).then_inc(c_ready, 1)
                        elif kind == "smp":
                            if st[1] == "C":
                                dve.wait_ge(smp_scored, 1)
                                V.tensor_tensor(ats.rearrange("p (a e b) -> p a e b", a=2, e=2),
                                                psc[0:DEC_SEQ, :, 0:2 * DEC_SEQ].rearrange("p e (a b) -> p a e b", a=2),
                                                tab[0:DEC_SEQ, 0:2048].rearrange("p (a e c) -> p a e c", a=2, e=2)[:, :, :, 0:DEC_SEQ],
                                                ALU.mult).then_inc(smp_ready, 1)
                                V.tensor_tensor(qs, z[:, 0:2, SEQ:TOK], const[:, QDEC:QDEC + 64].rearrange("p (a b) -> p a b", a=2), ALU.mult).then_inc(smp_ready, 1)
                        elif kind == "lv":
                            _, hp, i = st
                            if i == 0:
                                base = at[:, 0, 0, :]
                                if hp > 0:
                                    dve.wait_ge(d_av, 2)
                                else:
                                    dve.wait_ge(smp_av, 8)
                                    V.memset(ats, 0.0)
                                for e in range(2):
                                    V.memset(bass.AP(base.tensor, base.offset + e * 2048, [[4096, P], [640, 4], [1, P]]), 0.0)
                            if i < len(LEVELS) and LEVELS[i]:
                                s = LEVELS[i]
                                w = SEQ if s > 16 else TOK
                                n = hp * (len(LEVELS) - 1) + i
                                c = cum[:, 0:w].rearrange("p (b s) -> p b s", s=2 * s)
                                ref = c[:, :, s - 1:s].to_broadcast([P, w // (2 * s), 2 * s])
                                V.tensor_tensor(tmp[:, i % 2, 0:w].rearrange("p (b s) -> p b s", s=2 * s), c, ref, ALU.subtract).then_inc(dd_ready, 1)
                            if i > 0:
                                level_read(hp, i - 1)
                            if i < len(LEVELS) and LEVELS[i]:
                                dve.wait_ge(d_exp, n + 1)
                                v = tmp[:, i % 2, 0:w].rearrange("p (b e s) -> p b e s", e=2, s=s)
                                o = qkl[i % 2][:, 0:w].rearrange("p (b e s) -> p b e s", e=2, s=s)
                                kk = z[:, 2 + hp, 0:w].rearrange("p (b e s) -> p b e s", e=2, s=s)
                                qq = z[:, hp, 0:w].rearrange("p (b e s) -> p b e s", e=2, s=s)
                                V.tensor_tensor(o[:, :, 0, :], kk[:, :, 0, :], v[:, :, 0, :], ALU.mult)
                                V.tensor_tensor(o[:, :, 1, :], qq[:, :, 1, :], v[:, :, 1, :], ALU.mult).then_inc(lv_ready, 1)
                        elif kind == "kst":
                            hp = st[1]
                            V.tensor_scalar(tmp[:, 0, 0:SEQ], cum[:, 0:SEQ], cum[:, SEQ - 1:SEQ], None, ALU.subtract)
                            V.tensor_scalar(tmp[:, 0, SEQ:TOK], cum[:, SEQ:TOK], cum[:, TOK - 1:TOK], None, ALU.subtract).then_inc(kd_dd, 1)
                            dve.wait_ge(q_exp, hp + 1)
                            V.tensor_tensor(qs[:, hp, :], z[:, hp, SEQ:TOK], esm, ALU.mult).then_inc(smp_ready, 1)
                            dve.wait_ge(kd_exp, hp + 1)
                            V.tensor_tensor(qkl[0], z[:, 2 + hp, :], tmp[:, 0, :], ALU.mult).then_inc(kd_ready, 1)
                        elif kind == "zero":
                            V.memset(tab[:, 2048:2048 + MEM], 0.0)
                        elif kind == "memnorm":
                            dve.wait_ge(mem_stat, 1)
                            for t in range(2):
                                V.tensor_scalar(memr[:, t, :], memr[:, t, :], mss[:, t:t + 1], None, ALU.mult).then_inc(mem_scaled, 1)
                        elif kind == "ev":
                            j = st[1]
                            key = jobs[j]
                            what = key[0]
                            ps = slot[j % 2]
                            all_tok = ps[:, :, 0:HALF]
                            if what in ("SS", "SSK"):
                                b = key[-1]
                                i = qkn_no[key]
                                dve.wait_ge(qk_rstd, i + 1)
                                if i == 0:
                                    dve.wait_ge(scale_done, 3)
                                if what == "SSK":
                                    dst, g, r = kx[:, b, :], GK["X"], r2[i % 2][:, 0:MEM]
                                else:
                                    g = GQ[key[1]] if b < 4 else GK[key[1]]
                                    dst, r = z[:, b, :], r2[i % 2]
                                V.scalar_tensor_tensor(out=dst, in0=dst, scalar=par[:, g:g + 1], in1=r, op0=ALU.mult, op1=ALU.mult).then_inc(qn_ready, 1)
                            elif what == "ROT":
                                b = key[2]
                                if b == 0 and key[1] == "C":
                                    freed(dve, "BR", "B", KB - 1)
                                arrived(dve, j)
                                frees(V.tensor_tensor(tok(rt), all_tok, tok(cst(SIN, TOK)), ALU.mult), j)
                                V.tensor_tensor(z[:, b, :], z[:, b, :], cst(COS, TOK), ALU.mult)
                                V.tensor_tensor(z[:, b, :], z[:, b, :], rt, ALU.add).then_inc(z_ready, 1)
                            elif what == "G":
                                d = key[2]
                                freed(dve, *key)
                                V.tensor_scalar(gt[:, d, :], gt[:, d, :], 1.0, None, ALU.add)
                                V.reciprocal(gt[:, d, :], gt[:, d, :])
                            elif what == "BR":
                                m, d = key[1:]
                                arrived(dve, j)
                                if m == "A":
                                    if d == 0:
                                        dve.wait_ge(x_kept, 16)
                                    frees(V.tensor_tensor(tok(xm[:, d, :]), all_tok, tok(gt[:, d, :]), ALU.mult), j)
                                else:
                                    frees(V.tensor_tensor(tok(tmp[:, 2, :]), all_tok, tok(gt[:, d, :]), ALU.mult), j)
                                    V.tensor_tensor(xm[:, d, :], xm[:, d, :], tmp[:, 2, :], ALU.add).then_inc(m_added, 1)
                                    if m == "D":
                                        dve.wait_ge(m_added, 2 * KB + d + 1)
                                        V.tensor_copy(hhi[:, d, :], xm[:, d, :])
                                        V.tensor_tensor(hlo[:, d, :], xm[:, d, :], hhi[:, d, :].bitcast(F32), ALU.subtract).then_inc(m_ready, 1)
                            elif what in ("O", "XO", "DN"):
                                arrived(dve, j)
                                if key == ("O", 0):
                                    dve.wait_ge(x_restored, 16 * KB)
                                d = key[-1]
                                frees(V.tensor_tensor(tok(xm[:, d, :]), tok(xm[:, d, :]), all_tok, ALU.add), j)
                            elif what == "TRKC":
                                hp = key[2]
                                arrived(dve, j)
                                dve.wait_ge(kst_stored, 16 * kst_stores[key])
                                dec = const[:, KDEC:KDEC + 4 * NT].rearrange("p (t h) -> p t h", h=4)[:, :, 2 * hp:2 * hp + 2]
                                for e in range(2):
                                    V.tensor_tensor(kst[:, 0:NT, HD * e:HD * e + HD],
                                                    ps[:, 0, :].rearrange("p (t c) -> p t c", t=NT)[:, :, HD * e:HD * e + HD],
                                                    dec[:, :, e:e + 1].to_broadcast([P, NT, HD]), ALU.mult)
                                sd = const[0:DEC_SEQ, KDEC + 4 * NT + 2 * hp:KDEC + 4 * NT + 2 * hp + 2]
                                frees(V.tensor_tensor(kst[0:DEC_SEQ, NT, :].rearrange("p (e c) -> p e c", e=2),
                                                      ps[0:DEC_SEQ, 1, 0:P].rearrange("p (e c) -> p e c", e=2),
                                                      sd.unsqueeze(2).to_broadcast([DEC_SEQ, 2, HD]), ALU.mult), j)
                            elif what == "ST":
                                m, hp = key[1:]
                                dve.wait_ge(st_ready, hp + 1 + (2 if m == "D" else 0))
                                dve.wait_ge(s0_loaded, 16 if m == "C" else 32)
                                dec = const[:, G32 + hp:G32 + hp + 1] if m == "C" else elast[:, hp:hp + 1]
                                frees(V.scalar_tensor_tensor(out=sts[:, hp, :], in0=s0[:, hp, :], scalar=dec,
                                                             in1=ps[:, 1, 0:P], op0=ALU.mult, op1=ALU.add), j)
                            elif what == "MEAN":
                                h = key[2]
                                arrived(dve, j)
                                frees(V.scalar_tensor_tensor(out=tok(z[:, 4 + h, :]), in0=all_tok, scalar=-1.0 / P,
                                                             in1=tok(z[:, 4 + h, :]), op0=ALU.mult, op1=ALU.add), j)
                            elif what == "SSO":
                                m, h = key[1:]
                                dve.wait_ge(o_rstd, h + 1 + (4 if m == "D" else 0))
                                g = GN[m] + h
                                V.scalar_tensor_tensor(out=z[:, 4 + h, :], in0=z[:, 4 + h, :], scalar=par[:, g:g + 1],
                                                       in1=r2x[h % 2], op0=ALU.mult, op1=ALU.mult).then_inc(on_ready, 1)
                            elif what == "GG":
                                m, h = key[1:]
                                i = h + (4 if m == "D" else 0)
                                dve.wait_ge(g_exp, i + 1)
                                e = tmp[:, h % 2, :]
                                V.tensor_scalar(e, e, 1.0, None, ALU.add)
                                V.reciprocal(e, e)
                                frees(V.tensor_tensor(tok(e), tok(e), all_tok, ALU.mult), j)
                                dve.wait_ge(on_ready, i + 1)
                                V.tensor_tensor(e, e, z[:, 4 + h, :], ALU.mult)
                                V.tensor_copy(ohi[:, h, :], e)
                                V.tensor_tensor(olo[:, h, :], e, ohi[:, h, :].bitcast(F32), ALU.subtract).then_inc(o_ready, 1)
                            elif what == "LA":
                                hp = key[1]
                                dve.wait_ge(la_abs, hp + 1)
                                frees(V.tensor_scalar(tok(tmp[:, 1, :]), all_tok, par[:, BALPHA + hp:BALPHA + hp + 1], 0.0, ALU.add, ALU.min), j)
                                dve.wait_ge(la_ln, hp + 1)
                                V.tensor_tensor(tmp[:, 1, :], tmp[:, 1, :], tmp[:, 0, :], ALU.subtract)
                                V.tensor_scalar(tmp[:, 1, :], tmp[:, 1, :], 1.0 / 16.0, None, ALU.mult)
                                one = const[:, ONEC:ONEC + 1]
                                V.tensor_tensor_scan(cum[:, 0:SEQ], one.to_broadcast([P, SEQ]), tmp[:, 1, 0:SEQ], 0.0, ALU.mult, ALU.add)
                                V.tensor_tensor_scan(cum[:, SEQ:TOK], one.to_broadcast([P, DEC_SEQ]), tmp[:, 1, SEQ:TOK], 0.0,
                                                     ALU.mult, ALU.add).then_inc(cum_ready, 1)
                            elif what == "TM":
                                q = key[1]
                                arrived(dve, j)
                                for bb in range(4):
                                    b = 4 * q + bb
                                    e = tmp[:, 0, 0:MEM]
                                    ins = V.tensor_scalar(e, ps[:, bb // 2, (bb % 2) * 256:(bb % 2 + 1) * 256],
                                                          par[:, GMEM + b:GMEM + b + 1], None, ALU.mult)
                                    if bb == 3:
                                        frees(ins, j)
                                    else:
                                        ins
                                    V.tensor_copy(memn_hi[:, b, :], e)
                                    V.tensor_tensor(memn_lo[:, b, :], e, memn_hi[:, b, :].bitcast(F32), ALU.subtract).then_inc(mn_ready, 1)
                            elif what == "U":
                                i = key[1]
                                c = i // 2
                                blk = 2 * (c % 2) + i % 2
                                dve.wait_ge(u_sq, i + 1)
                                if c >= 2:
                                    dve.wait_ge(job_done, job_no[("DN", c - 2, KB - 1)] + 1)
                                V.tensor_copy(ohi[:, blk, :], tmp[:, i % 2, :])
                                V.tensor_tensor(olo[:, blk, :], tmp[:, i % 2, :], ohi[:, blk, :].bitcast(F32), ALU.subtract).then_inc(hid_ready, 1)
            clear_all()

        with nc.Block() as block:
            @block.tensor
            def _(pe):
                for b in range(KB):
                    if b >= 2:
                        pe.wait_ge(pro_dve, b - 1)
                    for t in range(NT):
                        pe.transpose(slot[b % 2][:, 0, t * P:(t + 1) * P], xm[:, b, t * P:(t + 1) * P], cst(IDN))
                    pe.transpose(slot[b % 2][0:DEC_SEQ, 1, 0:P], xm[:, b, SEQ:TOK], cst(IDN)).then_inc(pro_pe, 1)

            @block.scalar
            def _(act):
                for b in range(KB):
                    act.wait_ge(pro_pe, b + 1)
                    nc.scalar.activation(xrow[:, :, b * P:(b + 1) * P], slot[b % 2][:, 0, :].rearrange("p (t c) -> p t c", t=NT),
                                         ACT.Copy).then_inc(pro_act, 1)

            @block.vector
            def _(dve):
                for b in range(KB):
                    dve.wait_ge(pro_act, b + 1)
                    nc.vector.tensor_copy(xrow_s[:, b * P:(b + 1) * P], slot[b % 2][0:DEC_SEQ, 1, 0:P]).then_inc(pro_dve, 1)

            @block.sync
            def _(sp):
                sp.wait_ge(pro_dve, KB)
                sp.dma_start(t_out["y_prompt"][0].rearrange("(t p) d -> p t d", p=P), xrow).then_inc(pro_io, 16)
                sp.dma_start(t_out["y_sample"][0], xrow_s).then_inc(pro_io, 16)
                sp.wait_ge(pro_io, 32)


_INS = ["x_prompt", "x_sample", "cache_win_k", "cache_win_v", "cache_band_k", "cache_band_v", "state_ret", "state_gla",
        "cache_mem_k", "cache_mem_v", "mem_prompt", "norm_mix", "w_in", "qn_a", "kn_a", "sink_a", "qn_b", "kn_b",
        "relbias_b", "gn_c", "w_alpha_up", "b_alpha", "gn_d", "w_branch", "w_merge", "w_out", "norm_x", "norm_mem",
        "w_xq", "w_xkv", "qn_x", "kn_x", "w_xo", "norm_ffn", "w_up", "w_down"]
_OUTS = [("y_prompt", (1, SEQ, D_MODEL)), ("y_sample", (1, DEC_SEQ, D_MODEL)),
         ("p_win_k", (DEPTH, 1, P, 2, HD)), ("p_win_v", (DEPTH, 1, P, 2, HD)),
         ("p_band_k", (DEPTH, 1, SEQ, 8, HD)), ("p_band_v", (DEPTH, 1, SEQ, 8, HD)),
         ("p_state_ret", (DEPTH, 1, 4, HD, P)), ("p_state_gla", (DEPTH, 1, 4, HD, P)),
         ("mem_k", (DEPTH, 1, MEM, XH, P)), ("mem_v", (DEPTH, 1, MEM, XH, P)),
         ("s_win_k", (DEPTH, 1, DEC_SEQ, 2, HD)), ("s_win_v", (DEPTH, 1, DEC_SEQ, 2, HD)),
         ("s_band_k", (DEPTH, 1, DEC_SEQ, 8, HD)), ("s_band_v", (DEPTH, 1, DEC_SEQ, 8, HD)),
         ("s_state_ret", (DEPTH, 1, 4, HD, P)), ("s_state_gla", (DEPTH, 1, 4, HD, P))]


def kernel(**inputs):
    import concourse.bacc as bacc
    from concourse.bass_utils import run_bass_kernel_spmd

    nc = bacc.Bacc("TRN2", target_bir_lowering=False, num_devices=1)
    arrays, t_in, t_out = {}, {}, {}
    for name, a in [(n, np.ascontiguousarray(inputs[n])) for n in _INS] + list(constants().items()):
        arrays[f"in_{name}"] = a
        t_in[name] = nc.dram_tensor(f"in_{name}", a.shape, mybir.dt.from_np(a.dtype), kind="ExternalInput").ap()
    for name, shape in _OUTS:
        t_out[name] = nc.dram_tensor(f"out_{name}", shape, F32, kind="ExternalOutput").ap()
    build(nc, t_in, t_out)
    r = run_bass_kernel_spmd(nc, [arrays], core_ids=[0])
    return tuple(r.results[0][f"out_{name}"] for name, _ in _OUTS)
```

```python
from contextlib import ExitStack

import numpy as np
import concourse.bass as bass
from concourse import mybir

F32 = mybir.dt.float32
F32R = mybir.dt.float32r
U8 = mybir.dt.uint8
ALU = mybir.AluOpType
ACT = mybir.ActivationFunctionType
AX = mybir.AxisListType

P = 128
D_MODEL, SEQ, DEPTH, DEC_SEQ, PAST = 1024, 512, 2, 32, 128
TOK = SEQ + DEC_SEQ
HALF = TOK // 2
NT = SEQ // P
KB = D_MODEL // P
HD = 64
MEM = 256
XH = 4
D_FF = 4 * D_MODEL
FFN_CHUNKS = D_FF // 512
CHUNK = 64
EPS = 1e-6
NEG = -1.0e30
THETA = 10000.0
SLAB = 2048
REV = 640
RING = 2

A_Q, A_K, A_V = 0, 512, 640
B_Q, B_K, B_V = 768, 1280, 1792
C_Q, C_K, C_V, C_G = 2304, 2560, 2816, 3328
D_Q, D_K, D_V, D_G, D_A = 3840, 4096, 4352, 4864, 5376
RANK = 16
MIX = "ABCD"
NORM_LAG, TURN_LAG = 2, 3
VALUE_LAG = {"A": 4, "B": 4, "X": 5}
SPLIT_LAG = 7

IDN, ONES, BDIAG, ROT, COS, SIN = 0, 128, 256, 384, 512, 512 + TOK
KDEC = SIN + TOK
G32 = KDEC + 4 * (NT + 1)
EPSC, ONEC = G32 + 2, G32 + 3
QDEC = ONEC + 1
ZEROC = QDEC + 2 * DEC_SEQ
NCONST = ZEROC + 1
PAR_LOADS = 18

GMIX, GX, GFFN, GMEM = 0, 8, 16, 24
GQ = {"A": 32, "B": 34, "X": 36}
GK = {"A": 33, "B": 35, "X": 37}
SINK, GN, BALPHA = 40, {"C": 48, "D": 52}, 56
NPAR = 64

LEVELS = [256, 128, 64, 32, 16, 8, 4, 2, 1, 0]
MASKED = [64, 32, 16, 8, 4, 2, 1, 0]


def constants():
    c = np.zeros((P, NCONST), np.float32)
    p = np.arange(P)
    c[:, IDN:IDN + P] = np.eye(P)
    c[:, ONES:ONES + P] = 1.0
    c[:, BDIAG:BDIAG + P] = p[:, None] // HD == p[None, :] // HD
    half = HD // 2
    for m in range(P):
        k = m + half if m % HD < half else m - half
        c[k, ROT + m] = -1.0 if m % HD < half else 1.0
    freqs = np.float32(THETA) ** (-np.arange(half, dtype=np.float32) / np.float32(half))
    pos = np.concatenate([np.arange(SEQ), PAST + np.arange(DEC_SEQ)]).astype(np.float32)
    ang = (pos[None, :] * freqs[p % half][:, None]).astype(np.float32)
    c[:, COS:COS + TOK] = np.cos(ang)
    c[:, SIN:SIN + TOK] = np.sin(ang)
    log_gamma = np.log1p(-np.exp2(-5.0 - np.arange(4.0)))
    for h in range(4):
        for t in range(NT):
            c[:, KDEC + 4 * t + h] = np.exp(log_gamma[h] * (SEQ - 1 - (t * P + p))) * HD ** -0.5
        c[:DEC_SEQ, KDEC + 4 * NT + h] = np.exp(log_gamma[h] * (DEC_SEQ - 1 - p[:DEC_SEQ])) * HD ** -0.5
        rows = slice(HD * (h % 2), HD * (h % 2) + HD)
        c[rows, G32 + h // 2] = np.exp(log_gamma[h] * DEC_SEQ)
        c[rows, QDEC + DEC_SEQ * (h // 2):QDEC + DEC_SEQ * (h // 2) + DEC_SEQ] = np.exp(
            log_gamma[h] * (np.arange(DEC_SEQ) + 1.0))
    c[:, EPSC] = EPS
    c[:, ONEC] = 1.0
    mask_a = np.zeros((P, 2 * P), np.float32)
    mask_a[:CHUNK, 2 * P - CHUNK:] = NEG
    mask_a[CHUNK:, :CHUNK] = NEG
    d = np.arange(SEQ)[None, :] - p[:, None]
    decay = np.concatenate([np.where(d >= 0, np.exp(log_gamma[h] * np.maximum(d, 0)), 0.0) * HD ** -0.5
                            for h in range(4)], axis=1).astype(np.float32)
    j, i = p[:, None], p[None, :]
    masks = [(j == i) if s == 0 else ((j // (2 * s) == i // (2 * s)) & (j // s % 2 == 0) & (i // s % 2 == 1))
             for s in MASKED]
    return {"const": c, "flip": np.ascontiguousarray(np.eye(P, dtype=np.float32)[::-1]), "mask_a": mask_a, "decay": decay,
            "level_masks": np.concatenate(masks, axis=1).astype(np.float32)}



def layer_slabs():
    s = []

    def w_in(c0, n):
        s.extend(("w_in", 0, c0 + 256 * i, KB, 256) for i in range(n))

    def gates(b, first=0, last=4):
        s.extend(("w_merge", 0, D_MODEL * b + 256 * i, KB, 256) for i in range(first, last))

    def branch(b):
        s.extend((f"w_branch{b}", 0, 512 * i, 4, 512) for i in range(2))

    w_in(A_Q, 3), gates(0), branch(0)
    w_in(B_Q, 6), gates(1), branch(1)
    w_in(C_Q, 4), gates(2, 0, 3), w_in(C_G, 2), gates(2, 3, 4), branch(2)
    w_in(D_Q, 2)
    s.append(("w_in", 0, D_A, KB, RANK))
    w_in(D_V, 2), gates(3, 0, 3), w_in(D_G, 2), gates(3, 3, 4), branch(3)
    s.extend(("w_out", 0, 256 * i, KB, 256) for i in range(4))
    s.extend(("w_xkv", 0, 256 * i, KB, 256) for i in range(4))
    s.extend(("w_xq", 0, 256 * i, KB, 256) for i in range(2))
    s.extend(("w_xo", 0, 512 * i, 4, 512) for i in range(2))

    def w_up(block):
        s.append(("w_up", 0, P * block, KB, 2 * P))

    w_up(0), w_up(2)
    for c in range(FFN_CHUNKS):
        if c < FFN_CHUNKS - 1:
            w_up(4 * c + 4)
        s.extend(("w_down", 4 * c, 512 * i, 4, 512) for i in range(2))
        if c < FFN_CHUNKS - 1:
            w_up(4 * c + 6)
    return s


ANY = ("mm", "pe", "ev", "gl", "ge")


def merge(dense, other, counted=("mm", "pe")):
    out, k, n = [], 0, 0
    total = sum(d[0] in counted for d in dense)
    for d in dense:
        out.append(d)
        n += d[0] in counted
        while k < len(other) and k < n * len(other) / total:
            out.append(other[k])
            k += 1
    return out + other[k:]


def layer_steps():
    jobs, dense, steps = [], {}, []
    slab_of, cursor = {}, [0, 0]
    slabs = layer_slabs()

    def new(*key):
        jobs.append(key)
        return len(jobs) - 1

    def take(j, kt, width=P):
        s, b = cursor
        slab_of[j] = (s, b)
        dense[j] = kt
        b += 1
        if b * P >= slabs[s][4]:
            s, b = s + 1, 0
        cursor[:] = s, b

    def mm(*key, kt=KB, parts=1):
        j = new(*key)
        take(j, kt)
        n = kt // parts
        return j, [("mm", j, a, a + n) for a in range(0, kt, n)]

    def full(*key, kt=KB):
        j, m = mm(*key, kt=kt)
        return m + [("ev", j)] + ([("gl", *key[1:]), ("ge", *key[1:])] if key[0] == "G" else [])

    def pair(*keys):
        (j, a), (i, b) = [mm(*key, parts=KB) for key in keys]
        return [st for two in zip(a, b) for st in two] + [("ev", j), ("ev", i)]

    def small(*key):
        j = new(*key)
        return [("pe", j), ("ev", j)]

    def pipeline(u0, n):
        return [(kind, u0, n, i) for i in range(n + SPLIT_LAG) for kind in ("it", "iv")]

    def gates(m, blocks):
        out, late = [], []
        for d in blocks:
            j, parts = mm("G", m, d, parts=KB)
            out += parts[:1] + late[:1] + parts[1:3] + late[1:2] + parts[3:5] + late[2:] + parts[5:]
            late = [("ev", j), ("gl", m, d), ("ge", m, d)]
        return out + late

    def spread(kind, m, blocks):
        out = []
        for b in blocks:
            j, parts = mm(kind, m, b, parts=KB)
            out += parts + [("ev", j)] + ([("gl", m, b), ("ge", m, b)] if kind == "G" else [])
        return out

    steps += [("rstd", 0)] + [("h", 0, b) for b in range(KB + 1)]
    for m in MIX:
        nqk, nv = {"A": (5, 1), "B": (8, 4), "C": (4, 4), "D": (4, 4)}[m]
        pend = []
        for b in range(nqk):
            if m != "A" or b > 1:
                steps += full("D", m, b)
            elif b == 0:
                steps += pair(("D", m, 0), ("D", m, 1))
            for p in pend:
                steps += small(*p)
            nxt = []
            if m in "AB":
                nxt.append(("SS", m, b))
            if m == "A":
                nxt += [("ROT", m, q[2]) for q in pend if q[0] == "SS"]
            if m == "B":
                nxt += [("TRK", m, q[2]) for q in pend if q[0] == "SS" and q[2] >= 4]
            if m == "C":
                nxt.append(("ROT", m, b))
            pend = nxt
            if m == "B":
                steps += small("RB", b)
                if b == 1:
                    steps += small("KC", m)
        if m == "D":
            steps += full("AD") + full("V", m, 0) + small("LA", 0) + small("LA", 1)
            for v in range(1, nv - 1):
                steps += full("V", m, v) + small("TRV", m, v - 1)
            out = spread("V", m, [nv - 1]) + small("TRV", m, nv - 2)
            out += spread("G", m, [0]) + small("TRV", m, nv - 1) + small("TRKS", m, 0)
            out += spread("G", m, [1]) + small("ST", m, 0) + small("TRKS", m, 1) + spread("G", m, [2])
            lv = [[("lv", hp, i) for i in range(len(LEVELS) + 1)] for hp in range(2)]
            for hp in range(2):
                lv[0].insert(4 * hp + 3, ("kst", hp))
            steps += merge(out, lv[0], ANY) + [("avd", 0, 0), ("avd", 0, 1)]
            steps += merge(spread("G", m, [3]) + gates(m, range(4, KB - 2)), lv[1], ANY)
            steps += [("avd", 1, 0), ("avd", 1, 1)] + small("ST", m, 1) + [("stout", m), ("smp", m), ("memload",)]
            for h in range(4):
                steps += small("SSO", m, h)
            for h in range(4):
                steps += full("GG", m, h)
            steps += full("G", m, KB - 2) + [("memnorm",)] + full("G", m, KB - 1)
        else:
            for v in range(nv):
                steps += full("V", m, v)
                for p in pend:
                    steps += small(*p)
                pend = [(k, m, q[2]) for q in pend if q[0] == "SS" and (m == "A" or q[2] >= 4)
                        for k in [{"A": "ROT", "B": "TRK"}[m]]] + [("TRV", m, v)]
            if m == "A":
                pend.insert(0, ("KC", m))
            steps += full("G", m, 0)
            for p in pend:
                steps += small(*p)
        if m == "A":
            steps += [("swap",)] + small("TRK", m, 4)
        if m in "AB":
            u0, n = (0, 40) if m == "A" else (40, 40)
            steps += [("vout", m)]
            steps += merge(gates(m, range(1, KB)), pipeline(u0, n))
        if m == "C":
            steps += small("TRKC", m, 0) + full("G", m, 1) + small("ST", m, 0)
            steps += small("TRKC", m, 1) + full("G", m, 2) + small("ST", m, 1) + [("stout", m)]
            steps += [("smps",)] + merge(gates(m, range(3, 4)), [("itc", i) for i in range(4 * NT + 2)])
            steps += full("G", m, 4) + [("smp", m)]
            for h in range(4):
                steps += small("MEAN", m, h)
            steps += small("SSO", m, 0) + small("SSO", m, 1) + full("G", m, 5)
            steps += small("SSO", m, 2) + small("SSO", m, 3)
            for h in range(4):
                steps += full("GG", m, h)
            steps += full("G", m, KB - 2) + full("G", m, KB - 1)
        if m != "D":
            steps += [("table", m)]
        for d in range(KB):
            steps += full("BR", m, d, kt=4)
    for d in range(KB):
        steps += full("O", d)
        if d < 2:
            steps += small("TM", d)
        if d == 2:
            steps += [("xcload",)]
        if d > 0:
            steps.append(("ssq", 1, d - 1))
    for b in range(4):
        steps += full("KV", b)
        if b == 0:
            steps += [("ssq", 1, KB - 1)]
        if b == 1:
            steps += [("rstd", 1)]
        if b > 0:
            sum_up, take_up = small("SSK", b - 1)
            steps += [sum_up] + ([("h", 1, b - 2)] if b > 1 else []) + [take_up]
    for b in range(4, 8):
        steps += full("KV", b)
        turn, turned_out = small("SSK", 3) if b == 4 else small("TRVX", b - 5)
        blocks = {4: (2, 3), 5: (4,), 6: (5, 6), 7: (7, 8)}[b]
        steps += [turn] + [("h", 1, k) for k in blocks] + [turned_out]
    steps += full("D", "X", 0) + small("TRVX", 3) + small("TRKX", 0) + small("SS", "X", 0)
    steps += [("zero",), ("vout", "X")]
    units = pipeline(XH * 20, (XH + 1) * NT)
    for b in range(1, XH):
        own = spread("D", "X", [b]) + small("TRKX", b)
        own += (small("XC", b - 2) if b > 1 else []) + small("SS", "X", b)
        steps += own[:3] + merge(own[3:], units[2 * NT * (b - 1):2 * NT * b])
    steps += units[2 * NT * (XH - 1):]
    for d in range(KB):
        steps += full("XO", d, kt=4)
        if d > 0:
            steps.append(("ssq", 2, d - 1))
    steps += [("ssq", 2, KB - 1), ("rstd", 2)] + [("h", 2, b) for b in range(KB + 1)]
    steps += pair(("U", 0), ("U", 1)) + [("hid", 0), ("hid", 1)] + full("U", 2) + [("hid", 2)] + full("U", 3) + [("hid", 3)]
    for c in range(FFN_CHUNKS):
        if c < FFN_CHUNKS - 1:
            steps += full("U", 4 * c + 4) + full("U", 4 * c + 5)
        for d in range(KB):
            steps += full("DN", c, d, kt=4)
            if c == 0 and d == 0:
                steps.append(("stored",))
            if c == FFN_CHUNKS - 1 and d > 0:
                steps.append(("ssq", 3, d - 1))
        if c < FFN_CHUNKS - 1:
            for i in (6, 7):
                steps += full("U", 4 * c + i) + [("hid", 4 * c + 2 * i - 8), ("hid", 4 * c + 2 * i - 7)]
    steps.append(("ssq", 3, KB - 1))
    assert cursor == [len(slabs), 0], cursor
    for i in range(len(steps) - 1, -1, -1):
        if steps[i][0] in ("gl", "ge"):
            k, seen = i, 0
            while seen < 2 and steps[k + 1][0] in ("ev", "pe", "mm", "itc", "smp"):
                k += 1
                seen += steps[k][0] == "ev"
            steps.insert(k, steps.pop(i))
    return steps, jobs, dense, slab_of, slabs


class InTurn:

    def __init__(self, engine, chain):
        self.engine, self.chain = engine, chain
        self.count, self.last, self.ins = {}, None, None

    def then_inc(self, sem, n, at=None):
        self.ins.then_inc(sem, n)
        self.ins = None
        self.count[sem.name] = self.count.get(sem.name, 0) + n if at is None else at
        self.last = (sem, self.count[sem.name])
        return self

    def wait(self):
        if self.ins is not None:
            self.then_inc(self.chain, 1)
        if self.last is not None:
            self.engine.wait_ge(*self.last)

    def take(self, ins):
        self.ins = ins
        return self

    def activation(self, *a, **k):
        self.wait()
        return self.take(self.engine.activation(*a, **k))

    def tensor_tensor(self, *a, **k):
        self.wait()
        return self.take(self.engine.tensor_tensor(*a, **k))

    def tensor_scalar(self, *a, **k):
        self.wait()
        return self.take(self.engine.tensor_scalar(*a, **k))

    def scalar_tensor_tensor(self, *a, **k):
        self.wait()
        return self.take(self.engine.scalar_tensor_tensor(*a, **k))

    def tensor_tensor_reduce(self, *a, **k):
        self.wait()
        return self.take(self.engine.tensor_tensor_reduce(*a, **k))

    def tensor_tensor_scan(self, *a, **k):
        self.wait()
        return self.take(self.engine.tensor_tensor_scan(*a, **k))

    def copy_predicated(self, *a, **k):
        self.wait()
        return self.take(self.engine.copy_predicated(*a, **k))

    def tensor_copy(self, *a, **k):
        self.wait()
        return self.take(self.engine.tensor_copy(*a, **k))

    def reciprocal(self, *a, **k):
        self.wait()
        return self.take(self.engine.reciprocal(*a, **k))

    def memset(self, *a, **k):
        self.wait()
        return self.take(self.engine.memset(*a, **k))


def build(nc, t_in, t_out):
    steps, jobs, dense, slab_of, slabs = layer_steps()
    job_no = {key: j for j, key in enumerate(jobs)}
    last_job_of_slab = {}
    for j, (s, _) in slab_of.items():
        last_job_of_slab[s] = max(last_job_of_slab.get(s, -1), j)
    with ExitStack() as ctx:
        def sb(name, shape, dt=F32):
            return ctx.enter_context(nc.sbuf_tensor("s_" + name, shape, dt))

        sems = []

        def sem(name):
            sems.append(ctx.enter_context(nc.semaphore(name)))
            return sems[-1]

        const = sb("const", [P, NCONST])
        lmask = sb("lmask", [P, len(MASKED) * P], U8)
        par = sb("par", [P, NPAR])
        walpha = sb("walpha", [RANK, 2 * P])
        xm = sb("xm", [P, KB, TOK])
        hhi = sb("hhi", [P, KB, TOK], F32R)
        hlo = sb("hlo", [P, KB, TOK], F32R)
        ohi = sb("ohi", [P, 4, TOK], F32R)
        olo = sb("olo", [P, 4, TOK], F32R)
        wraw = sb("wraw", [P, RING, SLAB])
        whi = sb("whi", [P, 2, SLAB], F32R)
        wlo = sb("wlo", [P, 2, SLAB], F32R)
        gt = sb("gt", [P, KB, TOK])
        tab = sb("tab", [P, 4096])
        sbuf = sb("sbuf", [P, 3, 512])
        pt = sb("pt", [P, 2, 512])
        tmp = sb("tmp", [P, 3, TOK])
        kst = sb("kst", [P, NT + 1, P])
        z = sb("z", [P, 8, TOK])
        vtm = sb("vtm", [P, NT + 1, 512])
        side = sb("side", [P, 1024])
        stat = sb("stat", [P, 4, 4])
        kct, vc = side[:, 0:512], side[:, 512:1024]
        zx = z[:, :, :].rearrange("p a b -> p (a b)")
        kx = zx[:, 4 * TOK:4 * TOK + XH * MEM].rearrange("p (h m) -> p h m", h=XH)
        kxs = zx[:, 4 * TOK + XH * MEM:4 * TOK + 2 * XH * MEM].rearrange("p (h m) -> p h m", h=XH)
        vt = vtm[:, :, :].rearrange("p a b -> p (a b)")
        vx = vt[:, 0:1024].rearrange("p (a b) -> p a b", a=2)
        vxs = vt[:, 1024:2048].rearrange("p (a b) -> p a b", a=2)
        memn_hi = ohi[:, :, :].rearrange("p a b -> p (a b)")[:, 0:KB * MEM].rearrange("p (b m) -> p b m", b=KB)
        memn_lo = olo[:, :, :].rearrange("p a b -> p (a b)")[:, 0:KB * MEM].rearrange("p (b m) -> p b m", b=KB)
        memr = tab[:, 0:2048].rearrange("p (a b) -> p a b", a=2)
        at = tab[:, :].rearrange("p (e j i) -> p e j i", e=2, j=NT)
        s0 = side[:, 0:256].rearrange("p (a b) -> p a b", a=2)
        stp = side[:, 256:512].rearrange("p (a b) -> p a b", a=2)
        sts = side[:, 512:768].rearrange("p (a b) -> p a b", a=2)
        ats = side[0:DEC_SEQ, 768:896]
        qs = side[:, 896:960].rearrange("p (a b) -> p a b", a=2)
        esm = side[:, 960:992]
        elast = side[:, 992:994]
        mss = side[:, 1000:1004]
        cum = pt[:, :, :].rearrange("p a b -> p (a b)")[:, 0:TOK]
        rs = cum
        sflat = sbuf[:, :, :].rearrange("p a b -> p (a b)")
        qkl = [sflat[:, 0:TOK], sflat[:, TOK:2 * TOK]]
        cums = [cum, tmp[:, 2, :]]
        r2x = qkl
        sqx = qkl
        sq = [gt[:, 6, :], gt[:, 7, :]]
        r2 = [gt[:, 4, :], gt[:, 5, :]]
        rt = gt[:, 3, :]
        flip = gt[:, 2, 0:P]

        slot = [ctx.enter_context(nc.psum_tensor(f"slot{i}", [P, 2, 512], F32)) for i in range(2)]
        psc = ctx.enter_context(nc.psum_tensor("psc", [P, 2, 512], F32))
        pto = ctx.enter_context(nc.psum_tensor("pto", [P, 2, 512], F32))
        ptr, po = pto[:, 0, :], pto[:, 1, :]

        x_keep = nc.dram_tensor("x_keep", [P, KB, TOK], F32, kind="Internal").ap()
        rev = nc.dram_tensor("rev_bias", [DEPTH, 8, REV], F32, kind="Internal").ap()

        raw_loaded = [sem(f"raw_loaded{i}") for i in range(RING)]
        hi_done = sem("hi_done")
        slab_ready = sem("slab_ready")
        job_done = sem("job_done")
        slot_free = [sem("slot_free0"), sem("slot_free1")]
        act_chain, dve_chain = sem("act_chain"), sem("dve_chain")
        mix_loaded, par_loaded, scale_done = sem("mix_loaded"), sem("par_loaded"), sem("scale_done")
        sq_ready, sq_added, norm_summed, rstd_ready = sem("sq_ready"), sem("sq_added"), sem("norm_summed"), sem("rstd_ready")
        h_raw, h_hi_done, h_ready = sem("h_raw"), sem("h_hi_done"), sem("h_ready")
        x_kept, x_restored = sem("x_kept"), sem("x_restored")
        qk_rstd, qn_ready, z_ready, k_swapped = sem("qk_rstd"), sem("qn_ready"), sem("z_ready"), sem("k_swapped")
        kc_loaded, vc_loaded = sem("kc_loaded"), sem("vc_loaded")
        mem_k_stored = [sem("mem_k_stored0"), sem("mem_k_stored1")]
        kst_stored, v_stored, st_stored = sem("kst_stored"), sem("v_stored"), sem("st_stored")
        tab_loaded = sem("tab_loaded")
        scored, top_found, exp_done, p_ready = sem("scored"), sem("top_found"), sem("exp_done"), sem("p_ready")
        turned, pt_ready, av_done = sem("turned"), sem("pt_ready"), sem("av_done")
        o_copied, o_ready = sem("o_copied"), sem("o_ready")
        m_ready, m_added = sem("m_ready"), sem("m_added")
        gate_ready = sem("gate_ready")
        c_scored, c_ready, c_av = sem("c_scored"), sem("c_ready"), sem("c_av")
        smp_scored, smp_ready, oc_done, smp_av = sem("smp_scored"), sem("smp_ready"), sem("oc_done"), sem("smp_av")
        s0_loaded, kd_ready = sem("s0_loaded"), sem("kd_ready")
        st_ready, o_sq, o_rstd, on_ready, g_exp = sem("st_ready"), sem("o_sq"), sem("o_rstd"), sem("on_ready"), sem("g_exp")
        la_abs, la_ln, cum_ready = sem("la_abs"), sem("la_ln"), sem("cum_ready")
        dd_ready, d_exp, lv_ready, lv_scored = sem("dd_ready"), sem("d_exp"), sem("lv_ready"), sem("lv_scored")
        lv_read, d_av = sem("lv_read"), sem("d_av")
        kd_dd, kd_exp, q_exp = sem("kd_dd"), sem("kd_exp"), sem("q_exp")
        mem_loaded, mem_stat, mem_scaled, mn_ready = sem("mem_loaded"), sem("mem_stat"), sem("mem_scaled"), sem("mn_ready")
        u_sq, hid_ready = sem("u_sq"), sem("hid_ready")
        late = raw_loaded + slot_free + [hi_done, slab_ready, job_done, act_chain, dve_chain, sq_ready, sq_added, norm_summed,
                                         rstd_ready, h_raw, h_hi_done, h_ready, u_sq, hid_ready]
        late_names = {e.name for e in late}
        early_sems = [e for e in sems if e.name not in late_names]   
        pro_ident, pro_loaded, pro_const = sem("pro_ident"), [sem(f"pro_loaded{q}") for q in range(4)], sem("pro_const")
        pro_pe, pro_act, pro_dve, pro_io, pro_masks = sem("pro_pe"), sem("pro_act"), sem("pro_dve"), sem("pro_io"), sem("pro_masks")
        pro_sq, pro_added, pro_split = sem("pro_sq"), sem("pro_added"), sem("pro_split")
        pro_raw = [sem(f"pro_raw{i}") for i in range(RING)]
        epi_pe, epi_act, epi_dve, epi_io = sem("epi_pe"), sem("epi_act"), sem("epi_dve"), sem("epi_io")

        cst = lambda c, n=P: const[:, c:c + n]

        def out_l(name, l):
            return t_out[name][bass.ds(l, 1)]

        def in_l(name, l):
            return t_in[name][bass.ds(l, 1)]

        def clear_all():
            with nc.Block() as block:
                @block.gpsimd
                def _(pool):
                    for s in late:
                        pool.sem_clear(s)

        assert len(slabs) % 2 == 0 and RING == 2

        def load_slab(sp, s, l):
            name, rb, c0, kt, width = slabs[s]
            if name.startswith("w_branch"):
                w = t_in["w_branch"][bass.ds(l, 1), int(name[-1])].rearrange("o k n -> (o k) n")
            else:
                w = in_l(name, l).rearrange("o k n -> (o k) n")
            w = w[rb * P:(rb + kt) * P, :].rearrange("(k p) n -> p k n", p=P)
            return sp.dma_start(wraw[:, s % RING, 0:kt * width].rearrange("p (k n) -> p k n", k=kt), w[:, :, c0:c0 + width])

        def slab_words(s):
            return slabs[s % len(slabs)][3] * slabs[s % len(slabs)][4]

        def split_hi(s):
            n = slab_words(s)
            return nc.gpsimd.tensor_tensor(whi[:, s % 2, 0:n], wraw[:, s % RING, 0:n],
                                           const[:, ZEROC:ZEROC + 1].to_broadcast([P, n]), ALU.add)

        def split_lo(s):
            n = slab_words(s)
            return nc.gpsimd.tensor_tensor(wlo[:, s % 2, 0:n], wraw[:, s % RING, 0:n],
                                           whi[:, s % 2, 0:n].bitcast(F32), ALU.subtract)

        xrow = gt[:, :, :].rearrange("p a b -> p (a b)")[:, 0:NT * D_MODEL].rearrange("p (t d) -> p t d", t=NT)
        xrow_s = tab[0:DEC_SEQ, 0:D_MODEL]
        revt = tab[0:16, 1024:1024 + REV]
        mrow = tab[:, 2048:2048 + len(MASKED) * P]
        with nc.Block() as block:
            @block.sync
            def _(sp):
                sp.dma_start(cst(IDN), t_in["const"][:, IDN:IDN + P]).then_inc(pro_ident, 16)
                sp.dma_start(xrow_s, t_in["x_sample"][0]).then_inc(pro_ident, 16)
                for q in range(4):
                    c = slice(2 * q * P, 2 * (q + 1) * P)
                    sp.dma_start(xrow[:, :, c], t_in["x_prompt"][0].rearrange("(t p) d -> p t d", p=P)[:, :, c]).then_inc(pro_loaded[q], 16)
                    if q == 2:
                        load_slab(sp, 0, 0).then_inc(pro_raw[0], 16)
                    if q == 0:
                        sp.dma_start(const[:, ONES:NCONST], t_in["const"][:, ONES:NCONST]).then_inc(pro_const, 16)
                load_slab(sp, 1, 0).then_inc(pro_raw[1], 16)
                sp.wait_ge(pro_raw[1], 16)

            @block.gpsimd
            def _(pool):
                pool.wait_ge(pro_const, 16)
                pool.wait_ge(pro_raw[0], 16)
                split_hi(0).then_inc(pro_split, 1)
                pool.wait_ge(pro_split, 1)
                split_lo(0).then_inc(pro_split, 1)
                pool.wait_ge(pro_split, 2)

            @block.scalar
            def _(act):
                nc.scalar.preload_act_table_set("natural_log_exp_and_others")
                act.dma_start(mrow, t_in["level_masks"]).then_inc(pro_io, 16)
                rb = t_in["relbias_b"]
                with nc.allow_non_contiguous_dma(reason="2 KB of reversed rows, once"):
                    act.dma_start(revt[:, 384 - 1:REV - 1],
                                  bass.AP(rb.tensor, 256, [[257, 16], [-1, 256]])).then_inc(pro_io, 16)
                for b in range(KB):
                    act.wait_ge(pro_pe, b + 1)
                    nc.scalar.activation(xm[:, b, 0:SEQ], slot[b % 2][:, 0, :], ACT.Copy).then_inc(pro_act, 1)
                    act.wait_ge(pro_dve, b + 2)
                    act.wait_ge(pro_act, b + 1)
                    if b >= 3:
                        act.wait_ge(pro_added, b - 2)
                    nc.scalar.activation(sqx[b % 2] if b else rs, xm[:, b, :], ACT.Square).then_inc(pro_sq, 1)
                act.dma_start(rev.rearrange("l h m -> (l h) m")[:, 0:REV - 1],
                              revt[:, 0:REV - 1]).then_inc(pro_io, 16)
                act.wait_ge(pro_io, 48)
                act.wait_ge(pro_masks, 1)

            @block.vector
            def _(dve):
                dve.wait_ge(pro_io, 32)
                nc.vector.tensor_copy(lmask[:, :], mrow).then_inc(pro_masks, 1)
                nc.vector.tensor_copy(revt[:, 0:383], revt[:, 383:384].to_broadcast([16, 383])).then_inc(pro_dve, 1)
                for b in range(KB + 1):
                    if b < KB:
                        dve.wait_ge(pro_pe, b + 1)
                        dve.wait_ge(pro_act, b + 1)
                        nc.vector.tensor_copy(xm[:, b, SEQ:TOK], slot[b % 2][:, 1, 0:DEC_SEQ]).then_inc(pro_dve, 1)
                    if b >= 2:
                        dve.wait_ge(pro_sq, b)
                        if b >= 3:
                            dve.wait_ge(pro_added, b - 2)
                        nc.vector.tensor_tensor(rs, rs, sqx[(b - 1) % 2], ALU.add).then_inc(pro_added, 1)

            @block.tensor
            def _(pe):
                pe.wait_ge(pro_ident, 32)
                for b in range(KB):
                    pe.wait_ge(pro_loaded[b // 2], 16)
                    if b >= 2:
                        pe.wait_ge(pro_dve, b)
                    for t in range(NT):
                        pe.transpose(slot[b % 2][:, 0, t * P:(t + 1) * P], xrow[:, t, b * P:(b + 1) * P], cst(IDN))
                    pe.transpose(slot[b % 2][:, 1, 0:DEC_SEQ], xrow_s[:, b * P:(b + 1) * P],
                                 const[0:DEC_SEQ, IDN:IDN + DEC_SEQ]).then_inc(pro_pe, 1)

        def unit(u):
            if u >= 80:
                v = u - 80
                return ("X", v // NT, v % NT) if v < XH * NT else ("X", v - XH * NT, NT)
            m, v = ("A", u) if u < 40 else ("B", u - 40)
            return (m, v // NT, v % NT) if v < 32 else (m, v - 32, NT)

        def rows_of(t):
            return P if t < NT else DEC_SEQ

        def key_tiles(m, t):
            if m == "X":
                return [P, P]
            if t == NT:
                return [P, DEC_SEQ]
            if m == "A":
                return [P] * min(t + 1, 2)
            return [P] * (t + 1)

        def keys_in(m, t):
            return sum(key_tiles(m, t))

        def group_end(u):
            m, h, t = unit(u)
            base = {"A": 0, "B": 5, "X": 10}[m]
            if t == NT:
                return base + 4 if h == (XH if m == "X" else 8) - 1 else None
            if t == NT - 1:
                if m == "X":
                    return base + h
                return base + h // 2 if h % 2 else None
            return None

        def group_of(u):
            m, h, t = unit(u)
            base = {"A": 0, "B": 5, "X": 10}[m]
            return base + (4 if t == NT else h if m == "X" else h // 2)

        PROBS, TURNED = {"A": 6, "B": 4, "X": 6}, {"A": 4, "B": 2, "X": 4}

        def place(u):
            return ("A", u) if u < 40 else ("B", u - 40) if u < 80 else ("X", u - 80)

        def probs(u):
            m, v = place(u)
            if m == "B":
                return sbuf[:, v % 4, :] if v % 4 < 3 else tmp[:, 2, 0:512]
            return sflat[:, v % 6 * 256:v % 6 * 256 + 256]

        def turned_probs(u):
            m, v = place(u)
            return pt[:, v % 2, :] if m == "B" else pt[:, v % 4 // 2, v % 2 * 256:v % 2 * 256 + 256]

        def value_scratch(m, v):
            return gt[:, 4 + v % 2, :] if m == "D" else gt[:, v % 2, :] if m == "X" else tmp[:, v % 2, :]

        def first_in_group(u):
            return u == 0 or group_of(u) != group_of(u - 1)

        O_READY = {"A": 5, "B": 10, "C": 14, "D": 18, "X": 23}
        GROUP_AT = lambda g: g if g < 10 else g + 8

        def freed(eng, *key):
            j = job_no[key]
            eng.wait_ge(slot_free[j % 2], j // 2 + 1)

        def arrived(eng, j):
            eng.wait_ge(job_done, j + 1)

        def frees(ins, j):
            return ins.then_inc(slot_free[j % 2], 1, at=j // 2 + 1)

        kst_jobs = [k for k in jobs if k[0] in ("TRK", "TRKC", "TRKS", "TRKX")]
        kst_stores = {}
        n = 0
        for k in kst_jobs:
            kst_stores[k] = n
            n += {"TRK": 2}.get(k[0], 0)
        KST_TOTAL = n
        qkn = [k for k in jobs if k[0] in ("SS", "SSK")]
        qkn_no = {k: i for i, k in enumerate(qkn)}
        rot_no = {k: i for i, k in enumerate([k for k in jobs if k[0] == "ROT"])}

        with nc.Fori(0, DEPTH) as l:
            with nc.Block() as block:

                @block.sync
                def _(sp):
                    def load_params():
                        for c, name in ((GX, "norm_x"), (GFFN, "norm_ffn"), (GMEM, "norm_mem")):
                            sp.dma_start(par[:, c:c + KB], in_l(name, l).rearrange("o (b p) -> p (o b)", p=P)).then_inc(par_loaded, 16)
                        for c, name in ((GQ["A"], "qn_a"), (GK["A"], "kn_a"), (GQ["B"], "qn_b"), (GK["B"], "kn_b")):
                            for e in range(2):
                                sp.dma_start(par[HD * e:HD * e + HD, c:c + 1], in_l(name, l).rearrange("o p -> p o")).then_inc(par_loaded, 16)
                        for c, name in ((GQ["X"], "qn_x"), (GK["X"], "kn_x")):
                            sp.dma_start(par[:, c:c + 1], in_l(name, l).rearrange("o p -> p o")).then_inc(par_loaded, 16)
                        sp.dma_start(par[:, SINK:SINK + 8], in_l("sink_a", l).to_broadcast([P, 8])).then_inc(par_loaded, 16)
                        for c, name in ((GN["C"], "gn_c"), (GN["D"], "gn_d")):
                            sp.dma_start(par[:, c:c + 4], in_l(name, l).rearrange("o (b p) -> p (o b)", p=P)).then_inc(par_loaded, 16)
                        sp.dma_start(par[:, BALPHA:BALPHA + 2], in_l("b_alpha", l).rearrange("o (b p) -> p (o b)", p=P)).then_inc(par_loaded, 16)
                        sp.dma_start(walpha[:, :], in_l("w_alpha_up", l).rearrange("o r n -> (o r) n")).then_inc(par_loaded, 16)

                    with nc.allow_non_contiguous_dma(reason="4 KB of gains, one element per partition"):
                        sp.dma_start(par[:, GMIX:GMIX + KB], in_l("norm_mix", l).rearrange("o (b p) -> p (o b)", p=P)).then_inc(mix_loaded, 16)
                    for s in range(RING, len(slabs) + RING):
                        if s > RING:
                            sp.wait_ge(slab_ready, s - RING)
                        load_slab(sp, s % len(slabs), l if s < len(slabs) else (l + 1) % DEPTH).then_inc(raw_loaded[s % RING], 16)
                        if s == RING:
                            with nc.allow_non_contiguous_dma(reason="a few KB of gains per layer, one element per partition"):
                                load_params()
                            sp.dma_start(tab[:, 0:2 * P], t_in["mask_a"]).then_inc(tab_loaded, 16)
                            sp.dma_start(kst[:, 0, :], in_l("cache_win_k", l)[:, 0].rearrange("o t h d -> (o t) (h d)")).then_inc(kc_loaded, 16)
                            sp.dma_start(vc[:, 0:P], in_l("cache_win_v", l)[:, 0].rearrange("o t h d -> (o t) (h d)")).then_inc(vc_loaded, 16)
                            sp.dma_start(x_keep, xm[:, :, :]).then_inc(x_kept, 16)
                    for s in range(RING):
                        sp.wait_ge(raw_loaded[s], 16 * (len(slabs) // RING))

                @block.gpsimd
                def _(pool):
                    clear_at = slabs.index(("w_up", 0, P * 16, KB, 2 * P))
                    for s in range(1, len(slabs) + 1):
                        if s >= RING:
                            pool.wait_ge(raw_loaded[s % RING], 16 * (s // RING))
                        if s >= 2:
                            pool.wait_ge(job_done, last_job_of_slab[s - 2] + 1)
                        if s == clear_at:
                            pool.wait_ge(hid_ready, 9)
                            pool.wait_ge(job_done, job_no[("DN", 0, KB - 1)] + 1)
                            for e in early_sems:
                                pool.sem_clear(e)
                        split_hi(s).then_inc(hi_done, 1)
                        pool.wait_ge(hi_done, s)
                        split_lo(s).then_inc(slab_ready, 1)
                    pool.wait_ge(slab_ready, len(slabs))

                @block.tensor
                def _(pe):
                    def begin(j):
                        if j >= 2:
                            pe.wait_ge(slot_free[j % 2], j // 2)
                        return slot[j % 2]

                    waited = [0]

                    def dense_part(j, k0, k1):
                        key = jobs[j]
                        s, blk = slab_of[j]
                        _, _, _, kt, width = slabs[s]
                        if k0 == 0:
                            begin(j)
                        if waited[0] < s:
                            pe.wait_ge(slab_ready, s)
                            waited[0] = s
                        if key[0] == "BR":
                            pe.wait_ge(o_ready, O_READY[key[1]])
                        if key[0] == "XO":
                            pe.wait_ge(o_ready, O_READY["X"])
                        if key[0] == "KV":
                            pe.wait_ge(mn_ready, KB)
                        mem = key[0] == "KV"
                        if mem:
                            src_hi, src_lo, parts = memn_hi, memn_lo, [(0, 0, MEM)]
                        elif key[0] in ("BR", "XO", "DN"):
                            src_hi, src_lo, parts = ohi, olo, [(0, 0, HALF), (1, HALF, HALF)]
                        else:
                            src_hi, src_lo, parts = hhi, hlo, [(0, 0, HALF), (1, HALF, HALF)]
                        first_use = key in (("D", "A", 0), ("D", "X", 0), ("U", 0))
                        norm_k = {"A": 0, "X": 1}.get(key[1] if key[0] == "D" else None, 2)
                        for k in range(k0, k1):
                            if first_use:
                                pe.wait_ge(h_ready, KB * norm_k + k + 1)
                            if key == ("O", 0):
                                pe.wait_ge(m_ready, k + 1)
                            if key[0] == "DN" and key[2] == 0:
                                pe.wait_ge(hid_ready, 4 * key[1] + k + 1)
                            cols = min(P, width)
                            w0 = k * width + blk * P
                            for w, src in ((whi, src_hi), (whi, src_lo), (wlo, src_hi)):
                                for half, c0, n in parts:
                                    ins = pe.matmul(slot[j % 2][0:cols, half, 0:n], w[:, s % 2, w0:w0 + cols],
                                                    src[:, k, c0:c0 + n],
                                                    start=(k == 0 and w is whi and src is src_hi),
                                                    stop=(k == kt - 1 and w is wlo))
                        if k1 == kt:
                            ins.then_inc(job_done, 1)

                    def both_halves(ps, lhs, rhs, n=TOK):
                        if n == MEM:
                            return pe.matmul(ps[:, 0, 0:MEM], lhs, rhs[:, 0:MEM], start=True, stop=True)
                        m = lhs.shape[1]
                        for half in range(2):
                            ins = pe.matmul(ps[0:m, half, 0:HALF], lhs, rhs[:, half * HALF:(half + 1) * HALF],
                                            start=True, stop=True)
                        return ins

                    def turn_tokens(ps, src):
                        for t in range(NT):
                            pe.transpose(ps[:, 0, t * P:(t + 1) * P], src[:, t * P:(t + 1) * P], cst(IDN))
                        return pe.transpose(ps[0:DEC_SEQ, 1, 0:P], src[:, SEQ:TOK], cst(IDN))

                    def scores(u):
                        m, h, t = unit(u)
                        rows = rows_of(t)
                        n = keys_in(m, t)
                        if u >= 2:
                            pe.wait_ge(top_found, u - 1)
                        bank = psc[0:rows, u % 2, :]
                        q0 = t * P
                        if m == "X":
                            if t == 0:
                                pe.wait_ge(qn_ready, qkn_no[("SS", "X", h)] + 1)
                            if t == NT and h == 0:
                                freed(pe, "XC", 1)
                            q = z[:, h, q0:q0 + rows]
                            keys = kxs[:, h, :] if t == NT else kx[:, h, :]
                            ins = pe.matmul(bank[:, 0:n], q, keys, start=True, stop=True)
                        else:
                            o = HD * (h % 2)
                            q = z[o:o + HD, h // 2, q0:q0 + rows]
                            if m == "A":
                                if u == 0:
                                    pe.wait_ge(z_ready, rot_no[("ROT", "A", 4)] + 1)
                                    pe.wait_ge(k_swapped, 1)
                                    freed(pe, "KC", "A")
                                kb = 4 if h // 4 == h % 2 else 6
                                kc = kct[o:o + HD, 0:P] if kb == 4 else kct[o:o + HD, P:2 * P]
                                k0 = max(t - 1, 0) * P
                            else:
                                if u == 40:
                                    pe.wait_ge(qn_ready, qkn_no[("SS", "B", 7)] + 1)
                                    freed(pe, "KC", "B")
                                kb = 4 + h // 2
                                kc = kct[o:o + HD, (h // 2) * P:(h // 2 + 1) * P]
                                k0 = 0
                            if t < NT:
                                ins = pe.matmul(bank[:, 0:n], q, z[o:o + HD, kb, k0:k0 + n], start=True, stop=True)
                            else:
                                pe.matmul(bank[:, 0:P], q, kc, start=True, stop=True)
                                ins = pe.matmul(bank[:, P:P + DEC_SEQ], q, z[o:o + HD, kb, SEQ:TOK], start=True, stop=True)
                        ins.then_inc(scored, 1)

                    def turn_probs(u):
                        m, h, t = unit(u)
                        rows = rows_of(t)
                        pe.wait_ge(p_ready, u + 1)
                        if u >= 1:
                            pe.wait_ge(pt_ready, u)
                        c = 0
                        for i, wdt in enumerate(key_tiles(m, t)):
                            ins = pe.transpose(ptr[0:wdt, i * P:i * P + rows], probs(u)[0:rows, c:c + wdt],
                                               const[0:rows, IDN:IDN + rows])
                            c += wdt
                        ins.then_inc(turned, 1)

                    def values(u):
                        m, h, t = unit(u)
                        rows = rows_of(t)
                        pe.wait_ge(pt_ready, u + 1)
                        if first_in_group(u):
                            if group_of(u) > 0:
                                g = group_of(u)
                                pe.wait_ge(o_copied, g)
                            if u in (0, 40, 80):
                                if m == "X":
                                    freed(pe, "TRVX", 3)
                                    pe.wait_ge(vc_loaded, 48)
                                else:
                                    freed(pe, "TRV", m, 0 if m == "A" else 3)
                                    pe.wait_ge(vc_loaded, 16 if m == "A" else 32)
                        if m == "X":
                            v_t = [(vxs if t == NT else vx)[:, i, h * P:(h + 1) * P] for i in range(2)]
                            out = po[:, h * DEC_SEQ:(h + 1) * DEC_SEQ] if t == NT else po[:, t * P:(t + 1) * P]
                        else:
                            o = HD * (h % 2)
                            hk = h // 4 if m == "A" else h
                            c = slice(hk * HD, (hk + 1) * HD)
                            if t == NT:
                                v_t = [vc[:, c], vtm[0:DEC_SEQ, NT, c]]
                                out = po[o:o + HD, (h // 2) * DEC_SEQ:(h // 2 + 1) * DEC_SEQ]
                            else:
                                first = max(t - 1, 0) if m == "A" else 0
                                v_t = [vtm[:, i, c] for i in range(first, t + 1)]
                                out = po[o:o + HD, t * P:(t + 1) * P]
                        for i, (v, wdt) in enumerate(zip(v_t, key_tiles(m, t))):
                            ins = pe.matmul(out, v, turned_probs(u)[0:wdt, i * P:i * P + rows],
                                            start=(i == 0), stop=(i == len(v_t) - 1))
                        ins.then_inc(av_done, 1)

                    for st in steps:
                        kind = st[0]
                        if kind == "mm":
                            dense_part(*st[1:])
                        elif kind == "rstd":
                            k = st[1]
                            if k:
                                pe.wait_ge(sq_added, (KB - 1) * k)
                            for half in range(2):
                                ins = pe.matmul(pto[:, half, 0:HALF], cst(ONES), rs[:, half * HALF:(half + 1) * HALF],
                                                start=True, stop=True)
                            ins.then_inc(norm_summed, 1)
                        elif kind == "it":
                            _, u0, n, i = st
                            if i < n:
                                scores(u0 + i)
                            if 0 <= i - TURN_LAG < n:
                                turn_probs(u0 + i - TURN_LAG)
                        elif kind == "iv":
                            _, u0, n, i = st
                            lag = VALUE_LAG[place(u0)[0]]
                            for v in (i - lag - 1, i - lag):
                                if 0 <= v < n and first_in_group(u0 + v) == (v < i - lag):
                                    values(u0 + v)
                        elif kind == "itc":
                            i = st[1]
                            if i < 4 * NT:
                                h, jt = divmod(i, NT)
                                o = HD * (h % 2)
                                if i == 0:
                                    pe.wait_ge(smp_ready, 1)
                                if i >= 2:
                                    pe.wait_ge(c_ready, i - 1)
                                pe.matmul(psc[:, i % 2, 0:SEQ - jt * P], z[o:o + HD, 2 + h // 2, jt * P:(jt + 1) * P],
                                          z[o:o + HD, h // 2, jt * P:SEQ], start=True, stop=True).then_inc(c_scored, 1)
                            if 1 <= i <= 4 * NT:
                                h, jt = divmod(i - 1, NT)
                                pe.wait_ge(c_ready, i)
                                if jt == 0 and h > 0:
                                    pe.wait_ge(oc_done, h)
                                if i == 1:
                                    freed(pe, "TRV", "C", 3)
                                pe.matmul(po[:, jt * P:SEQ], vtm[:, jt, h * P:(h + 1) * P], sbuf[:, (i - 1) % 3, 0:SEQ - jt * P],
                                          start=(jt == 0), stop=(jt == NT - 1)).then_inc(c_av, 1)
                        elif kind == "lv":
                            _, hp, i = st
                            if i == len(LEVELS):
                                continue
                            s = LEVELS[i]
                            n = hp * len(LEVELS) + i
                            if s:
                                pe.wait_ge(lv_ready, hp * (len(LEVELS) - 1) + i + 1)
                            if n > 0:
                                pe.wait_ge(lv_read, n)
                            if hp == 1 and i == 0:
                                pe.wait_ge(oc_done, 7)
                            for e in range(2):
                                r = slice(HD * e, HD * e + HD)
                                k_s = qkl[i % 2] if s else z[:, hp, :]
                                q_s = qkl[i % 2] if s else z[:, 2 + hp, :]
                                if s == 256:
                                    tiles = [(0, 256, 0, 256), (1, 256, 256, 256)]
                                elif s == 128:
                                    tiles = [(0, 128, 0, 128), (2, 384, 128, 128)]
                                else:
                                    tiles = [(jt, jt * P, jt * P, P) for jt in range(NT)]
                                for jt, i0, c0, w in tiles:
                                    ins = pe.matmul(psc[:, e, c0:c0 + w], k_s[r, jt * P:(jt + 1) * P], q_s[r, i0:i0 + w],
                                                    start=True, stop=True)
                                if s <= 16:
                                    ins = pe.matmul(pto[0:DEC_SEQ, e, 0:DEC_SEQ], k_s[r, SEQ:TOK],
                                                    q_s[r, SEQ:TOK], start=True, stop=True)
                            ins.then_inc(lv_scored, 1)
                        elif kind == "avd":
                            _, hp, e = st
                            h = 2 * hp + e
                            pe.wait_ge(lv_read, (hp + 1) * len(LEVELS))
                            if h == 0:
                                freed(pe, "TRV", "D", 3)
                            else:
                                pe.wait_ge(oc_done, 5 + h)
                            for jt in range(NT):
                                ins = pe.matmul(po[:, jt * P:SEQ], vtm[:, jt, h * P:(h + 1) * P], at[:, e, jt, jt * P:SEQ],
                                                start=(jt == 0), stop=(jt == NT - 1))
                            ins.then_inc(d_av, 1)
                        elif kind == "smps":
                            pe.wait_ge(z_ready, rot_no[("ROT", "C", 3)] + 1)
                            for h in range(4):
                                r = slice(HD * (h % 2), HD * (h % 2) + HD)
                                c = h // 2 * DEC_SEQ
                                ins = pe.matmul(psc[0:DEC_SEQ, h % 2, c:c + DEC_SEQ], z[r, 2 + h // 2, SEQ:TOK],
                                                z[r, h // 2, SEQ:TOK], start=True, stop=True)
                            ins.then_inc(smp_scored, 1)
                        elif kind == "smp":
                            m = st[1]
                            pe.wait_ge(smp_ready, 2 if m == "C" else 4)
                            pe.wait_ge(oc_done, 4 if m == "C" else 9)
                            pe.wait_ge(s0_loaded, 16 if m == "C" else 32)
                            def outs(h):
                                return po[:, h * DEC_SEQ:(h + 1) * DEC_SEQ]

                            for h in range(4):
                                pe.matmul(outs(h), vtm[0:DEC_SEQ, NT, h * P:(h + 1) * P], ats[:, h * DEC_SEQ:(h + 1) * DEC_SEQ],
                                          start=(h == 0), stop=False)
                            for e in range(2):
                                if e:
                                    pe.wait_ge(smp_av, 1 + 2 * (m == "D"))
                                for h in (e, e + 2):
                                    r = slice(HD * e, HD * e + HD)
                                    ins = pe.matmul(outs(h), s0[r, h // 2, :], qs[r, h // 2, :], start=False, stop=(h == 3))
                                ins.then_inc(smp_av, 1)
                        elif kind == "pe":
                            j = st[1]
                            key = jobs[j]
                            ps = begin(j)
                            what = key[0]
                            if what == "SS":
                                m, b = key[1:]
                                freed(pe, "D", m, b)
                                ins = both_halves(ps, cst(ONES if m == "X" else BDIAG), sq[b % 2])
                            elif what == "SSK":
                                freed(pe, "KV", key[1])
                                ins = both_halves(ps, cst(ONES), sq[key[1] % 2], MEM)
                            elif what == "ROT":
                                m, b = key[1:]
                                if m == "A":
                                    pe.wait_ge(qn_ready, qkn_no[("SS", "A", b)] + 1)
                                else:
                                    freed(pe, "D", m, b)
                                ins = both_halves(ps, cst(ROT), z[:, b, :])
                            elif what == "TRV":
                                m, v = key[1:]
                                freed(pe, "V", m, v)
                                ins = turn_tokens(ps, value_scratch(m, v))
                            elif what == "TRK":
                                if key[1] == "A":
                                    pe.wait_ge(z_ready, rot_no[("ROT", "A", 4)] + 1)
                                else:
                                    pe.wait_ge(qn_ready, qkn_no[("SS", "B", key[2])] + 1)
                                ins = turn_tokens(ps, z[:, key[2], :])
                            elif what == "TRKC":
                                pe.wait_ge(z_ready, rot_no[("ROT", "C", 3)] + 1)
                                ins = turn_tokens(ps, z[:, 2 + key[2], :])
                            elif what == "TRKS":
                                pe.wait_ge(kd_ready, key[2] + 1)
                                ins = turn_tokens(ps, gt[:, 6 + key[2], :])
                            elif what == "ST":
                                m, hp = key[1:]
                                if m == "C":
                                    freed(pe, "TRKC", m, hp)
                                else:
                                    freed(pe, "TRKS", m, hp)
                                    freed(pe, "TRV", m, 3)
                                if m == "C":
                                    freed(pe, "TRV", m, 3)
                                for e in range(2):
                                    h = 2 * hp + e
                                    r = slice(HD * e, HD * e + HD)
                                    for t in range(NT):
                                        pe.matmul(ps[r, 0, 0:P], kst[:, t, r], vtm[:, t, h * P:(h + 1) * P],
                                                  start=(t == 0), stop=(t == NT - 1))
                                    ins = pe.matmul(ps[r, 1, 0:P], kst[0:DEC_SEQ, NT, r], vtm[0:DEC_SEQ, NT, h * P:(h + 1) * P],
                                                    start=True, stop=True)
                            elif what == "RB":
                                pe.wait_ge(tab_loaded, 48)
                                h = key[1]
                                ins = pe.matmul(ps[:, 0, :], flip, tab[:, h * 512:(h + 1) * 512], start=True, stop=True)
                            elif what == "KC":
                                nb = 1 if key[1] == "A" else 4
                                pe.wait_ge(kc_loaded, 16 if key[1] == "A" else 32)
                                for b in range(nb):
                                    ins = pe.transpose(ps[:, 0, b * P:(b + 1) * P],
                                                       kst[:, b, :], cst(IDN))
                            elif what == "MEAN":
                                pe.wait_ge(oc_done, 5)
                                ins = both_halves(ps, cst(ONES), z[:, 4 + key[2], :])
                            elif what == "SSO":
                                m, h = key[1:]
                                pe.wait_ge(o_sq, h + 1 + (4 if m == "D" else 0))
                                ins = both_halves(ps, cst(ONES), tmp[:, h % 2, :])
                            elif what == "LA":
                                hp = key[1]
                                freed(pe, "AD")
                                ins = both_halves(ps, walpha[:, hp * P:(hp + 1) * P], tmp[0:RANK, 2, :])
                            elif what == "TM":
                                q = key[1]
                                pe.wait_ge(mem_scaled, 2)
                                for bb in range(4):
                                    for t in range(2):
                                        c = (4 * q + bb) * P
                                        ins = pe.transpose(ps[:, bb // 2, (bb % 2) * 256 + t * P:(bb % 2) * 256 + (t + 1) * P],
                                                           memr[:, t, c:c + P], cst(IDN))
                            elif what == "TRVX":
                                v = key[1]
                                freed(pe, "KV", 4 + v)
                                for t in range(2):
                                    ins = pe.transpose(ps[:, 0, t * P:(t + 1) * P], value_scratch("X", v)[:, t * P:(t + 1) * P], cst(IDN))
                            elif what == "TRKX":
                                b = key[1]
                                pe.wait_ge(qn_ready, qkn_no[("SSK", b)] + 1)
                                for t in range(2):
                                    ins = pe.transpose(ps[:, 0, t * P:(t + 1) * P], kx[:, b, t * P:(t + 1) * P], cst(IDN))
                            elif what == "XC":
                                pe.wait_ge(kc_loaded, 48)
                                for hh in range(2):
                                    for t in range(2):
                                        c = t * 512 + (2 * key[1] + hh) * P
                                        ins = pe.transpose(ps[:, 0, hh * 256 + t * P:hh * 256 + (t + 1) * P], side[:, c:c + P], cst(IDN))
                            ins.then_inc(job_done, 1)

                @block.scalar
                def _(act):
                    turn = InTurn(act, act_chain)
                    A = turn.activation

                    n_group = [0]

                    def evac_group(u):
                        g = group_end(u)
                        m, h, t = unit(u)
                        act.wait_ge(av_done, u + 1)
                        if g % 5 >= 2:
                            act.wait_ge(o_ready, GROUP_AT(g - 1))
                        w = 4 * DEC_SEQ if t == NT else SEQ
                        A(tmp[:, g % 5 % 2, 0:w], po[:, 0:w], ACT.Copy).then_inc(o_copied, 1)

                    def exp_unit(u):
                        m, h, t = unit(u)
                        rows, n = rows_of(t), keys_in(m, t)
                        act.wait_ge(top_found, u + 1)
                        s = probs(u)[0:rows, 0:n]
                        nm = stat[0:rows, u % 4, 1:2]
                        if u == 0:
                            act.wait_ge(par_loaded, 16 * PAR_LOADS)
                        if m == "A":
                            A(stat[0:rows, u % 4, 3:4], par[0:rows, SINK + h:SINK + h + 1], ACT.Exp, bias=nm)
                        A(s, s, ACT.Exp, bias=nm, accum_out=stat[0:rows, u % 4, 2:3]).then_inc(exp_done, 1)

                    def evac_turned(u):
                        m, h, t = unit(u)
                        rows = rows_of(t)
                        act.wait_ge(turned, u + 1)
                        n = TURNED[m]
                        if place(u)[1] >= n:
                            act.wait_ge(av_done, u + 1 - n)
                        tiles = key_tiles(m, t)
                        src, dst = ptr, turned_probs(u)
                        if t < NT:
                            w = len(tiles) * P
                            A(dst[:, 0:w], src[:, 0:w], ACT.Copy).then_inc(pt_ready, 1)
                        elif m == "X":
                            A(dst[:, 0:2 * P].rearrange("p (a b) -> p a b", a=2)[:, :, 0:rows],
                              src[:, 0:2 * P].rearrange("p (a b) -> p a b", a=2)[:, :, 0:rows], ACT.Copy).then_inc(pt_ready, 1)
                        else:
                            A(dst[:, 0:rows], src[:, 0:rows], ACT.Copy)
                            A(dst[0:DEC_SEQ, P:P + rows], src[0:DEC_SEQ, P:P + rows], ACT.Copy).then_inc(pt_ready, 1)

                    for st in steps:
                        kind = st[0]
                        if kind == "ssq":
                            k, b = st[1:]
                            if k == 1:
                                freed(act, "O", b)
                            if k == 2:
                                freed(act, "XO", b)
                            if k == 3:
                                freed(act, "DN", FFN_CHUNKS - 1, b)
                            if b == 0:
                                A(rs, xm[:, b, :], ACT.Square).then_inc(sq_ready, 1)
                            else:
                                if b >= 3:
                                    act.wait_ge(sq_added, (KB - 1) * (k - 1) + b - 2)
                                A(sqx[b % 2], xm[:, b, :], ACT.Square).then_inc(sq_ready, 1)
                        elif kind == "rstd":
                            k = st[1]
                            act.wait_ge(norm_summed, k + 1)
                            A(rs.rearrange("p (a b) -> p a b", a=2), pto[:, :, 0:HALF], ACT.Ln,
                                   bias=const[:, EPSC:EPSC + 1], scale=1.0 / D_MODEL)
                            A(rs, rs, ACT.Exp, scale=-0.5).then_inc(rstd_ready, 1)
                        elif kind == "h":
                            k, b = st[1:]
                            if b < KB:
                                act.wait_ge(h_raw, KB * k + b + 1)
                                A(hhi[:, b, :], tmp[:, b % 3, :], ACT.Copy).then_inc(h_hi_done, 1)
                        elif kind == "it":
                            _, u0, n, i = st
                            lag = VALUE_LAG[place(u0)[0]] + 1
                            if 0 <= i - lag < n and group_end(u0 + i - lag) is not None:
                                evac_group(u0 + i - lag)
                            if 0 <= i - TURN_LAG < n:
                                evac_turned(u0 + i - TURN_LAG)
                            if i < n:
                                exp_unit(u0 + i)
                        elif kind == "itc":
                            i = st[1]
                            if i >= 1 + NT and (i - 1) % NT == 0:
                                h = (i - 1) // NT - 1
                                act.wait_ge(c_av, NT * (h + 1))
                                A(z[:, 4 + h, 0:SEQ], po[:, :], ACT.Copy).then_inc(oc_done, 1)
                        elif kind == "avd":
                            _, hp, e = st
                            h = 2 * hp + e
                            act.wait_ge(d_av, h + 1)
                            A(z[:, 4 + h, 0:SEQ], po[:, :], ACT.Copy).then_inc(oc_done, 1)
                        elif kind == "smp":
                            m = st[1]
                            act.wait_ge(smp_av, 2 if m == "C" else 4)
                            A(z[:, 4:8, SEQ:TOK], po[:, 0:4 * DEC_SEQ].rearrange("p (a b) -> p a b", a=4), ACT.Copy).then_inc(oc_done, 1)
                        elif kind == "lv":
                            _, hp, step = st
                            if hp == 0 and step == len(LEVELS):
                                hp, ahead = 1, (0,)
                            else:
                                ahead = (0, 1) if (hp, step) == (0, 0) else (step + 1,)
                            for i in ahead:
                                if i < len(LEVELS) and LEVELS[i]:
                                    s = LEVELS[i]
                                    act.wait_ge(dd_ready, hp * (len(LEVELS) - 1) + i + 1)
                                    w = SEQ if s > 16 else TOK
                                    v = tmp[:, i % 2, 0:w].rearrange("p (b e s) -> p b e s", e=2, s=s)
                                    A(v[:, :, 0, :], v[:, :, 0, :], ACT.Exp, scale=-1.0)
                                    A(v[:, :, 1, :], v[:, :, 1, :], ACT.Exp).then_inc(d_exp, 1)
                        elif kind == "kst":
                            hp = st[1]
                            act.wait_ge(cum_ready, hp + 1)
                            if hp:
                                act.wait_ge(smp_ready, 3)
                            A(elast[:, hp:hp + 1], cums[hp][:, TOK - 1:TOK], ACT.Exp)
                            A(esm, cums[hp][:, SEQ:TOK], ACT.Exp).then_inc(q_exp, 1)
                            act.wait_ge(kd_dd, hp + 1)
                            A(gt[:, 6 + hp, :], gt[:, 6 + hp, :], ACT.Exp, scale=-1.0).then_inc(kd_exp, 1)
                        elif kind == "swap":
                            act.wait_ge(z_ready, rot_no[("ROT", "A", 4)] + 1)
                            A(z[0:HD, 6, :], z[HD:P, 4, :], ACT.Copy)
                            A(z[HD:P, 6, :], z[0:HD, 4, :], ACT.Copy).then_inc(k_swapped, 1)
                        elif kind == "vout":
                            m = st[1]
                            if m == "X":
                                freed(act, "TRVX", 3)
                                act.dma_start(out_l("mem_v", l)[:, 0].rearrange("o (t p) h d -> p (o t) (h d)", p=P), vx).then_inc(v_stored, 16)
                            elif m == "A":
                                freed(act, "TRV", "A", 0)
                                act.dma_start(out_l("p_win_v", l)[:, 0].rearrange("o t h d -> (o t) (h d)"), vtm[:, NT - 1, 0:P]).then_inc(v_stored, 16)
                                act.dma_start(out_l("s_win_v", l)[:, 0].rearrange("o t h d -> (o t) (h d)"), vtm[0:DEC_SEQ, NT, 0:P]).then_inc(v_stored, 16)
                            else:
                                freed(act, "TRV", "B", 3)
                                act.dma_start(out_l("p_band_v", l)[:, 0].rearrange("o (t p) h d -> p (o t) (h d)", p=P), vtm[:, 0:NT, :]).then_inc(v_stored, 16)
                                act.dma_start(out_l("s_band_v", l)[:, 0].rearrange("o t h d -> (o t) (h d)"), vtm[0:DEC_SEQ, NT, :]).then_inc(v_stored, 16)
                        elif kind == "stout":
                            m = st[1]
                            name = "ret" if m == "C" else "gla"
                            act.wait_ge(st_ready, 2 if m == "C" else 4)
                            for hp in range(2):
                                freed(act, "ST", m, hp)
                            act.dma_start(out_l(f"p_state_{name}", l)[:, 0].rearrange("o (a e) d v -> (e d) (o a) v", e=2), stp).then_inc(st_stored, 16)
                            act.dma_start(out_l(f"s_state_{name}", l)[:, 0].rearrange("o (a e) d v -> (e d) (o a) v", e=2), sts).then_inc(st_stored, 16)
                        elif kind == "table":
                            m = st[1]
                            if m == "A":
                                act.wait_ge(top_found, 40)
                                act.dma_start(tab[:, :].rearrange("p (h c) -> p h c", h=8), bass.AP(
                                    rev.tensor, rev[bass.ds(l, 1)].offset, [[1, P], [REV, 8], [1, 512]])).then_inc(tab_loaded, 16)
                                act.wait_ge(kst_stored, 16 * 2)
                                act.dma_start(kst[:, 0:4, :].rearrange("p a b -> p (a b)"),
                                              in_l("cache_band_k", l)[:, 0].rearrange("o t h d -> (o t) (h d)")).then_inc(kc_loaded, 16)
                                act.dma_start(vc, in_l("cache_band_v", l)[:, 0].rearrange("o t h d -> (o t) (h d)")).then_inc(vc_loaded, 16)
                            elif m == "B":
                                act.wait_ge(top_found, 80)
                                act.dma_start(tab[:, 0:2048], t_in["decay"]).then_inc(tab_loaded, 16)
                                act.dma_start(s0, in_l("state_ret", l)[:, 0].rearrange("o (a e) d v -> (e d) (o a) v", e=2)).then_inc(s0_loaded, 16)
                            else:
                                act.wait_ge(st_stored, 32)
                                act.dma_start(s0, in_l("state_gla", l)[:, 0].rearrange("o (a e) d v -> (e d) (o a) v", e=2)).then_inc(s0_loaded, 16)
                        elif kind == "gl":
                            A(gt[:, st[2], :], gt[:, st[2], :], ACT.Ln, bias=const[:, ONEC:ONEC + 1])
                        elif kind == "ge":
                            A(gt[:, st[2], :], gt[:, st[2], :], ACT.Exp, scale=-1.0).then_inc(gate_ready, 1)
                        elif kind == "stored":
                            act.wait_ge(kst_stored, 16 * KST_TOTAL)
                            for b in range(2):
                                act.wait_ge(mem_k_stored[b], 16 * XH // 2)
                            act.wait_ge(v_stored, 16 * 5)
                            act.wait_ge(st_stored, 16 * 4)
                            act.wait_ge(x_kept, 16)
                        elif kind == "memload":
                            act.wait_ge(d_av, 4)
                            act.dma_start(memr, t_in["mem_prompt"][0].rearrange("(t p) d -> p t d", p=P)).then_inc(mem_loaded, 16)
                        elif kind == "memnorm":
                            act.wait_ge(mem_loaded, 16)
                            freed(act, "TRKS", "D", 1)
                            for t in range(2):
                                A(pt[:, :, :], memr[:, t, :].rearrange("p (a b) -> p a b", a=2), ACT.Square,
                                       accum_out=mss[:, t:t + 1])
                            A(mss[:, 2:4], mss[:, 0:2], ACT.Ln, bias=const[:, EPSC:EPSC + 1], scale=1.0 / D_MODEL)
                            A(mss[:, 0:2], mss[:, 2:4], ACT.Exp, scale=-0.5).then_inc(mem_stat, 1)
                        elif kind == "xcload":
                            act.wait_ge(st_stored, 64)
                            act.wait_ge(mem_scaled, 2)
                            act.dma_start(side[:, :].rearrange("p (t c) -> p t c", t=2),
                                          in_l("cache_mem_k", l)[:, 0].rearrange("o (t p) h d -> p (o t) (h d)", p=P)).then_inc(kc_loaded, 16)
                            act.dma_start(vxs, in_l("cache_mem_v", l)[:, 0].rearrange("o (t p) h d -> p (o t) (h d)", p=P)).then_inc(vc_loaded, 16)
                        elif kind == "ev":
                            j = st[1]
                            key = jobs[j]
                            what = key[0]
                            ps = slot[j % 2]
                            all_tok = ps[:, :, 0:HALF]

                            def tok(ap):
                                return ap.rearrange("p (a b) -> p a b", a=2)

                            if what == "D":
                                m, b = key[1:]
                                if b == 0 and m in "BCD":
                                    freed(act, "BR", MIX[MIX.index(m) - 1], KB - 1)
                                    if m == "B":
                                        act.dma_start(flip, t_in["flip"]).then_inc(tab_loaded, 16)
                                arrived(act, j)
                                if m in "ABX":
                                    if b >= 2:
                                        act.wait_ge(job_done, job_no[("SS", m, b - 2)] + 1)
                                    A(tok(z[:, b, :]), all_tok, ACT.Copy)
                                    frees(A(tok(sq[b % 2]), all_tok, ACT.Square), j)
                                elif m == "C":
                                    frees(A(tok(z[:, b, :]), all_tok, ACT.Copy), j)
                                else:
                                    frees(A(tok(z[:, (b + 2) % 4, :]), all_tok, ACT.Copy, scale=HD ** -0.5 if b < 2 else 1.0), j)
                            elif what in ("SS", "SSK"):
                                b = key[-1]
                                i = qkn_no[key]
                                arrived(act, j)
                                x_like = what == "SSK" or key[1] == "X"
                                dim = P if x_like else HD
                                if i >= 2:
                                    act.wait_ge(qn_ready, i - 1)
                                if what == "SSK":
                                    src, dst = ps[:, 0, 0:MEM], r2[i % 2][:, 0:MEM]
                                else:
                                    src, dst = all_tok, tok(r2[i % 2])
                                frees(A(dst, src, ACT.Ln, bias=const[:, EPSC:EPSC + 1], scale=1.0 / dim), j)
                                A(dst, dst, ACT.Exp, scale=-0.5).then_inc(qk_rstd, 1)
                            elif what == "V":
                                m, v = key[1:]
                                if v == 0 and m != "A":
                                    act.wait_ge(v_stored, 32 if m == "B" else 64)
                                arrived(act, j)
                                if v >= 2:
                                    act.wait_ge(job_done, job_no[("TRV", m, v - 2)] + 1)
                                frees(A(tok(value_scratch(m, v)), all_tok, ACT.Copy), j)
                            elif what == "TRV":
                                m, v = key[1:]
                                arrived(act, j)
                                A(vtm[:, 0:NT, v * P:(v + 1) * P], ps[:, 0, :].rearrange("p (t c) -> p t c", t=NT), ACT.Copy)
                                frees(A(vtm[0:DEC_SEQ, NT, v * P:(v + 1) * P], ps[0:DEC_SEQ, 1, 0:P], ACT.Copy), j)
                            elif what == "TRK":
                                m, b = key[1:]
                                arrived(act, j)
                                act.wait_ge(kst_stored, 16 * kst_stores[key])
                                freed(act, "KC", m)
                                A(kst[:, 0:NT, :], ps[:, 0, :].rearrange("p (t c) -> p t c", t=NT), ACT.Copy)
                                frees(A(kst[0:DEC_SEQ, NT, :], ps[0:DEC_SEQ, 1, 0:P], ACT.Copy), j)
                                freed(act, *key)
                                if m == "A":
                                    act.dma_start(out_l("p_win_k", l)[:, 0].rearrange("o t h d -> (o t) (h d)"), kst[:, NT - 1, :]).then_inc(kst_stored, 16)
                                    act.dma_start(out_l("s_win_k", l)[:, 0].rearrange("o t h d -> (o t) (h d)"), kst[0:DEC_SEQ, NT, :]).then_inc(kst_stored, 16)
                                else:
                                    c = slice((b - 4) * P, (b - 3) * P)
                                    act.dma_start(out_l("p_band_k", l)[:, 0].rearrange("o (t p) h d -> p (o t) (h d)", p=P)[:, :, c], kst[:, 0:NT, :]).then_inc(kst_stored, 16)
                                    act.dma_start(out_l("s_band_k", l)[:, 0].rearrange("o t h d -> (o t) (h d)")[:, c], kst[0:DEC_SEQ, NT, :]).then_inc(kst_stored, 16)
                            elif what == "TRKS":
                                arrived(act, j)
                                A(kst[:, 0:NT, :], ps[:, 0, :].rearrange("p (t c) -> p t c", t=NT), ACT.Copy)
                                frees(A(kst[0:DEC_SEQ, NT, :], ps[0:DEC_SEQ, 1, 0:P], ACT.Copy), j)
                            elif what == "ST":
                                m, hp = key[1:]
                                arrived(act, j)
                                if hp == 0 and m == "D":
                                    act.wait_ge(st_stored, 32)
                                A(stp[:, hp, :], ps[:, 0, 0:P], ACT.Copy).then_inc(st_ready, 1)
                            elif what == "RB":
                                h = key[1]
                                arrived(act, j)
                                frees(A(tab[:, h * 512:(h + 1) * 512], ps[:, 0, :], ACT.Copy), j)
                            elif what == "KC":
                                m = key[1]
                                arrived(act, j)
                                if m == "A":
                                    A(kct[:, 0:P], ps[:, 0, 0:P], ACT.Copy)
                                    A(kct[0:HD, P:2 * P], ps[HD:P, 0, 0:P], ACT.Copy)
                                    frees(A(kct[HD:P, P:2 * P], ps[0:HD, 0, 0:P], ACT.Copy), j)
                                else:
                                    frees(A(kct, ps[:, 0, :], ACT.Copy), j)
                            elif what == "G":
                                arrived(act, j)
                                frees(A(tok(gt[:, key[2], :]), all_tok, ACT.Exp, scale=-1.0), j)
                            elif what == "MEAN":
                                h = key[2]
                                freed(act, *key)
                                if h < 2:
                                    A(tmp[:, h % 2, :], z[:, 4 + h, :], ACT.Square).then_inc(o_sq, 1)
                            elif what == "SSO":
                                m, h = key[1:]
                                i = h + (4 if m == "D" else 0)
                                if m == "D" and h < 2:
                                    act.wait_ge(oc_done, 10)
                                    if h == 0:
                                        for hh in range(2):
                                            A(tmp[:, hh, :], z[:, 4 + hh, :], ACT.Square).then_inc(o_sq, 1)
                                arrived(act, j)
                                if h >= 2:
                                    act.wait_ge(on_ready, i - 1)
                                frees(A(tok(r2x[h % 2]), all_tok, ACT.Ln, bias=const[:, EPSC:EPSC + 1], scale=1.0 / P), j)
                                A(r2x[h % 2], r2x[h % 2], ACT.Exp, scale=-0.5).then_inc(o_rstd, 1)
                                if h < 2:
                                    if m == "C":
                                        freed(act, "MEAN", m, h + 2)
                                    A(tmp[:, h % 2, :], z[:, 6 + h, :], ACT.Square).then_inc(o_sq, 1)
                            elif what == "GG":
                                h = key[2]
                                i = h + (4 if key[1] == "D" else 0)
                                arrived(act, j)
                                if h >= 2:
                                    act.wait_ge(o_ready, O_READY[key[1]] - 4 + h - 1)
                                e = tmp[:, h % 2, :]
                                A(tok(e), all_tok, ACT.Exp, scale=-1.0)
                                A(e, e, ACT.Ln, bias=const[:, ONEC:ONEC + 1])
                                A(e, e, ACT.Exp, scale=-1.0).then_inc(g_exp, 1)
                            elif what == "AD":
                                arrived(act, j)
                                act.wait_ge(m_added, 2 * KB)
                                frees(A(tok(tmp[0:RANK, 2, :]), ps[0:RANK, :, 0:HALF], ACT.Copy), j)
                            elif what == "LA":
                                hp = key[1]
                                arrived(act, j)
                                e = gt[:, 6, :]
                                if hp:
                                    act.wait_ge(cum_ready, 1)
                                A(tok(e), all_tok, ACT.Abs, bias=par[:, BALPHA + hp:BALPHA + hp + 1]).then_inc(la_abs, 1)
                                A(e, e, ACT.Exp, scale=-1.0)
                                A(e, e, ACT.Ln, bias=const[:, ONEC:ONEC + 1]).then_inc(la_ln, 1)
                            elif what == "KV":
                                b = key[1]
                                arrived(act, j)
                                if b < 4:
                                    if b >= 2:
                                        act.wait_ge(job_done, job_no[("SSK", b - 2)] + 1)
                                    A(kx[:, b, :], ps[:, 0, 0:MEM], ACT.Copy)
                                    frees(A(sq[b % 2][:, 0:MEM], ps[:, 0, 0:MEM], ACT.Square), j)
                                else:
                                    v = b - 4
                                    if v >= 2:
                                        act.wait_ge(job_done, job_no[("TRVX", v - 2)] + 1)
                                    frees(A(value_scratch("X", v)[:, 0:MEM], ps[:, 0, 0:MEM], ACT.Copy), j)
                            elif what == "TRVX":
                                v = key[1]
                                arrived(act, j)
                                frees(A(vx[:, :, v * P:(v + 1) * P], ps[:, 0, 0:2 * P].rearrange("p (t c) -> p t c", t=2), ACT.Copy), j)
                            elif what == "TRKX":
                                b = key[1]
                                arrived(act, j)
                                keys = kst[:, 2 * (b % 2):2 * (b % 2) + 2, :]
                                act.wait_ge(kst_stored, 16 * KST_TOTAL)
                                if b >= 2:
                                    act.wait_ge(mem_k_stored[b % 2], 16)
                                frees(A(keys, ps[:, 0, 0:2 * P].rearrange("p (t c) -> p t c", t=2), ACT.Copy), j)
                                freed(act, *key)
                                act.dma_start(out_l("mem_k", l)[:, 0, :, b].rearrange("o (t p) d -> p (o t) d", p=P), keys).then_inc(mem_k_stored[b % 2], 16)
                            elif what == "XC":
                                arrived(act, j)
                                frees(A(kxs[:, 2 * key[1]:2 * key[1] + 2, :], ps[:, 0, :].rearrange("p (h m) -> p h m", h=2), ACT.Copy), j)
                            elif what == "BR" and key[1] == "D":
                                d = key[2]
                                act.wait_ge(m_ready, d + 1)
                                act.dma_start(xm[:, d, :], x_keep[:, d, :]).then_inc(x_restored, 16)
                            elif what == "U":
                                i = key[1]
                                arrived(act, j)
                                if i >= 3:
                                    act.wait_ge(hid_ready, i - 2)
                                frees(A(tok(tmp[:, i % 3, :]), all_tok, ACT.Relu), j)
                                A(tmp[:, i % 3, :], tmp[:, i % 3, :], ACT.Square).then_inc(u_sq, 1)

                @block.vector
                def _(dve):
                    V = InTurn(dve, dve_chain)

                    def tok(ap):
                        return ap.rearrange("p (a b) -> p a b", a=2)

                    def top(u):
                        m, h, t = unit(u)
                        rows, n = rows_of(t), keys_in(m, t)
                        dve.wait_ge(scored, u + 1)
                        if place(u)[1] >= PROBS[m]:
                            dve.wait_ge(turned, u + 1 - PROBS[m])
                        if u == 0:
                            dve.wait_ge(tab_loaded, 16)
                        if m == "A":
                            c0 = 0 if t == NT or t > 0 else P
                            table = tab[0:rows, c0:c0 + n]
                        elif m == "B":
                            c0 = h * 512 + (256 if t == NT else 384 - t * P)
                            table = tab[0:rows, c0:c0 + n]
                        else:
                            table = tab[0:rows, 2048:2048 + n]
                        st_ = stat[0:rows, u % 4, :]
                        V.tensor_tensor_reduce(out=probs(u)[0:rows, 0:n], in0=psc[0:rows, u % 2, 0:n], in1=table,
                                                    scale=1.0, scalar=-3.0e38, op0=ALU.add, op1=ALU.max, accum_out=st_[:, 0:1])
                        if m == "A":
                            ins = V.tensor_scalar(st_[:, 1:2], st_[:, 0:1], par[0:rows, SINK + h:SINK + h + 1], -1.0, ALU.max, ALU.mult)
                        else:
                            ins = V.tensor_scalar(st_[:, 1:2], st_[:, 0:1], -1.0, None, ALU.mult)
                        ins.then_inc(top_found, 1)

                    def normalise(u):
                        m, h, t = unit(u)
                        rows, n = rows_of(t), keys_in(m, t)
                        dve.wait_ge(exp_done, u + 1)
                        st_ = stat[0:rows, u % 4, :]
                        if m == "A":
                            V.tensor_tensor(st_[:, 2:3], st_[:, 2:3], st_[:, 3:4], ALU.add)
                        V.reciprocal(st_[:, 3:4], st_[:, 2:3])
                        s = probs(u)[0:rows, 0:n]
                        V.tensor_scalar(s, s, st_[:, 3:4], None, ALU.mult).then_inc(p_ready, 1)

                    def evac_group(u):
                        m, h, t = unit(u)
                        g = group_end(u)
                        dve.wait_ge(o_copied, g + 1)
                        if t == NT:
                            o, w = (slice(0, 4), slice(SEQ, TOK)), 4 * DEC_SEQ
                            src = tmp[:, g % 5 % 2, 0:w].rearrange("p (a b) -> p a b", a=4)
                        else:
                            o = (h if m == "X" else h // 2, slice(0, SEQ))
                            src = tmp[:, g % 5 % 2, 0:SEQ]
                        V.tensor_copy(ohi[:, o[0], o[1]], src)
                        V.tensor_tensor(olo[:, o[0], o[1]], src, ohi[:, o[0], o[1]].bitcast(F32), ALU.subtract).then_inc(o_ready, 1)

                    def level_read(hp, i):
                        s = LEVELS[i]
                        dve.wait_ge(lv_scored, hp * len(LEVELS) + i + 1)
                        base = at[:, 0, 0, :]

                        def cells(off, stride, count, w):
                            return bass.AP(base.tensor, base.offset + off, [[4096, P], [2048, 2], [stride, count], [1, w]])

                        if s == 256:
                            ins = V.tensor_copy(cells(256, 512, 2, 256), psc[:, :, :].rearrange("p e (a b) -> p e a b", a=2))
                        elif s == 128:
                            ins = V.tensor_copy(cells(128, 1280, 2, P), psc[:, :, 0:256].rearrange("p e (a b) -> p e a b", a=2))
                        else:
                            mk = lmask[:, MASKED.index(s) * P:(MASKED.index(s) + 1) * P]
                            ins = V.copy_predicated(cells(0, 640, 4, P), mk.unsqueeze(1).unsqueeze(1).to_broadcast([P, 2, 4, P]),
                                                    psc[:, :, :].rearrange("p e (a b) -> p e a b", a=4))
                        if s <= 16:
                            mk = lmask[0:DEC_SEQ, MASKED.index(s) * P:MASKED.index(s) * P + DEC_SEQ]
                            ins = V.copy_predicated(ats[:, hp * 64:(hp + 1) * 64].rearrange("p (a b) -> p a b", a=2),
                                                    mk.unsqueeze(1).to_broadcast([DEC_SEQ, 2, DEC_SEQ]),
                                                    pto[0:DEC_SEQ, :, 0:DEC_SEQ])
                        ins.then_inc(lv_read, 1)

                    def differences(hp, i):
                        s = LEVELS[i]
                        w = SEQ if s > 16 else TOK
                        c = cums[hp][:, 0:w].rearrange("p (b s) -> p b s", s=2 * s)
                        ref = c[:, :, s - 1:s].to_broadcast([P, w // (2 * s), 2 * s])
                        V.tensor_tensor(tmp[:, i % 2, 0:w].rearrange("p (b s) -> p b s", s=2 * s), c, ref,
                                        ALU.subtract).then_inc(dd_ready, 1)

                    for st in steps:
                        kind = st[0]
                        if kind == "ssq":
                            k, b = st[1:]
                            if b > 0:
                                dve.wait_ge(sq_ready, KB * (k - 1) + b + 1)
                                V.tensor_tensor(rs, rs, sqx[b % 2], ALU.add).then_inc(sq_added, 1)
                        elif kind == "h":
                            k, b = st[1:]
                            g = (GMIX, GX, GFFN)[k]
                            if b == 0:
                                if k == 0:
                                    dve.wait_ge(mix_loaded, 16)
                                dve.wait_ge(rstd_ready, k + 1)
                            if b < KB:
                                V.scalar_tensor_tensor(out=tmp[:, b % 3, :], in0=xm[:, b, :], scalar=par[:, g + b:g + b + 1],
                                                       in1=rs, op0=ALU.mult, op1=ALU.mult).then_inc(h_raw, 1)
                            if b >= 1:
                                dve.wait_ge(h_hi_done, KB * k + b)
                                V.tensor_tensor(hlo[:, b - 1, :], tmp[:, (b - 1) % 3, :], hhi[:, b - 1, :].bitcast(F32),
                                                ALU.subtract).then_inc(h_ready, 1)
                            if (k, b) == (0, KB):
                                dve.wait_ge(par_loaded, 16 * PAR_LOADS)
                                for m, dim in (("A", HD), ("B", HD), ("X", P)):
                                    c = GQ[m]
                                    V.tensor_scalar(par[:, c:c + 1], par[:, c:c + 1], dim ** -0.5, None, ALU.mult).then_inc(scale_done, 1)
                        elif kind == "it":
                            _, u0, n, i = st
                            if u0 == 40 and i == 0:
                                for h in (6, 7):
                                    freed(dve, "RB", h)
                                V.memset(tab[0:CHUNK, :].rearrange("p (h c) -> p h c", h=8)[:, :, 448:512], NEG)
                            if 0 <= i - SPLIT_LAG < n and group_end(u0 + i - SPLIT_LAG) is not None:
                                evac_group(u0 + i - SPLIT_LAG)
                            if 0 <= i - NORM_LAG < n:
                                normalise(u0 + i - NORM_LAG)
                            if i < n:
                                top(u0 + i)
                        elif kind == "itc":
                            i = st[1]
                            if i < 4 * NT:
                                h, jt = divmod(i, NT)
                                dve.wait_ge(c_scored, i + 1)
                                if i == 0:
                                    dve.wait_ge(tab_loaded, 64)
                                if i >= 3:
                                    dve.wait_ge(c_av, i - 2)
                                w = SEQ - jt * P
                                V.tensor_tensor(sbuf[:, i % 3, 0:w], psc[:, i % 2, 0:w], tab[:, h * 512:h * 512 + w], ALU.mult).then_inc(c_ready, 1)
                        elif kind == "smps":
                            dve.wait_ge(smp_scored, 1)
                            dve.wait_ge(tab_loaded, 64)
                            V.tensor_tensor(ats.rearrange("p (a e b) -> p a e b", a=2, e=2),
                                            psc[0:DEC_SEQ, :, 0:2 * DEC_SEQ].rearrange("p e (a b) -> p a e b", a=2),
                                            tab[0:DEC_SEQ, 0:2048].rearrange("p (a e c) -> p a e c", a=2, e=2)[:, :, :, 0:DEC_SEQ],
                                            ALU.mult).then_inc(smp_ready, 1)
                            V.tensor_tensor(qs, z[:, 0:2, SEQ:TOK], const[:, QDEC:QDEC + 64].rearrange("p (a b) -> p a b", a=2), ALU.mult).then_inc(smp_ready, 1)
                        elif kind == "lv":
                            _, hp, i = st
                            if i == 0:
                                base = at[:, 0, 0, :]
                                if hp == 0:
                                    differences(0, 0)
                                if hp > 0:
                                    dve.wait_ge(d_av, 2)
                                else:
                                    dve.wait_ge(smp_av, 2)
                                    V.memset(ats, 0.0)
                                for e in range(2):
                                    V.memset(bass.AP(base.tensor, base.offset + e * 2048, [[4096, P], [640, 4], [1, P]]), 0.0)
                            if i < len(LEVELS) and LEVELS[i]:
                                s = LEVELS[i]
                                w = SEQ if s > 16 else TOK
                                dve.wait_ge(d_exp, hp * (len(LEVELS) - 1) + i + 1)
                                v = tmp[:, i % 2, 0:w].rearrange("p (b e s) -> p b e s", e=2, s=s)
                                o = qkl[i % 2][:, 0:w].rearrange("p (b e s) -> p b e s", e=2, s=s)
                                base = z[:, hp, :]
                                kq = bass.AP(base.tensor, base.offset, [[8 * TOK, P], [2 * s, w // (2 * s)], [2 * TOK + s, 2], [1, s]])
                                V.tensor_tensor(o, kq, v, ALU.mult).then_inc(lv_ready, 1)
                            if i > 0:
                                level_read(hp, i - 1)
                            if i + 1 < len(LEVELS) and LEVELS[i + 1]:
                                differences(hp, i + 1)
                            if hp == 0 and i == len(LEVELS):
                                differences(1, 0)
                        elif kind == "kst":
                            hp = st[1]
                            c, kd = cums[hp], gt[:, 6 + hp, :]
                            V.tensor_scalar(kd[:, 0:SEQ], c[:, 0:SEQ], c[:, SEQ - 1:SEQ], None, ALU.subtract)
                            V.tensor_scalar(kd[:, SEQ:TOK], c[:, SEQ:TOK], c[:, TOK - 1:TOK], None, ALU.subtract).then_inc(kd_dd, 1)
                            dve.wait_ge(q_exp, hp + 1)
                            V.tensor_tensor(qs[:, hp, :], z[:, 2 + hp, SEQ:TOK], esm, ALU.mult).then_inc(smp_ready, 1)
                            dve.wait_ge(kd_exp, hp + 1)
                            V.tensor_tensor(kd, z[:, hp, :], kd, ALU.mult).then_inc(kd_ready, 1)
                        elif kind == "hid":
                            i = st[1]
                            c, blk = divmod(i, 4)
                            dve.wait_ge(u_sq, i + 1)
                            if c >= 1:
                                dve.wait_ge(job_done, job_no[("DN", c - 1, KB - 1)] + 1)
                            V.tensor_copy(ohi[:, blk, :], tmp[:, i % 3, :])
                            V.tensor_tensor(olo[:, blk, :], tmp[:, i % 3, :], ohi[:, blk, :].bitcast(F32), ALU.subtract).then_inc(hid_ready, 1)
                        elif kind == "zero":
                            V.memset(tab[:, 2048:2048 + MEM], 0.0)
                        elif kind == "memnorm":
                            dve.wait_ge(mem_stat, 1)
                            for t in range(2):
                                V.tensor_scalar(memr[:, t, :], memr[:, t, :], mss[:, t:t + 1], None, ALU.mult).then_inc(mem_scaled, 1)
                        elif kind == "ev":
                            j = st[1]
                            key = jobs[j]
                            what = key[0]
                            ps = slot[j % 2]
                            all_tok = ps[:, :, 0:HALF]
                            if what in ("SS", "SSK"):
                                b = key[-1]
                                i = qkn_no[key]
                                dve.wait_ge(qk_rstd, i + 1)
                                if i == 0:
                                    dve.wait_ge(scale_done, 3)
                                if what == "SSK":
                                    dst, g, r = kx[:, b, :], GK["X"], r2[i % 2][:, 0:MEM]
                                else:
                                    g = GQ[key[1]] if b < 4 else GK[key[1]]
                                    dst, r = z[:, b, :], r2[i % 2]
                                V.scalar_tensor_tensor(out=dst, in0=dst, scalar=par[:, g:g + 1], in1=r, op0=ALU.mult, op1=ALU.mult).then_inc(qn_ready, 1)
                            elif what == "ROT":
                                b = key[2]
                                if b == 0 and key[1] == "C":
                                    freed(dve, "BR", "B", KB - 1)
                                arrived(dve, j)
                                frees(V.tensor_tensor(tok(rt), all_tok, tok(cst(SIN, TOK)), ALU.mult), j)
                                V.tensor_tensor(z[:, b, :], z[:, b, :], cst(COS, TOK), ALU.mult)
                                V.tensor_tensor(z[:, b, :], z[:, b, :], rt, ALU.add).then_inc(z_ready, 1)
                            elif what == "BR":
                                m, d = key[1:]
                                arrived(dve, j)
                                dve.wait_ge(gate_ready, KB * MIX.index(m) + d + 1)
                                if m == "A":
                                    if d == 0:
                                        dve.wait_ge(x_kept, 16)
                                    frees(V.tensor_tensor(tok(xm[:, d, :]), all_tok, tok(gt[:, d, :]), ALU.mult), j)
                                else:
                                    frees(V.tensor_tensor(tok(tmp[:, 2, :]), all_tok, tok(gt[:, d, :]), ALU.mult), j)
                                    V.tensor_tensor(xm[:, d, :], xm[:, d, :], tmp[:, 2, :], ALU.add).then_inc(m_added, 1)
                                    if m == "D":
                                        dve.wait_ge(m_added, 2 * KB + d + 1)
                                        V.tensor_copy(hhi[:, d, :], xm[:, d, :])
                                        V.tensor_tensor(hlo[:, d, :], xm[:, d, :], hhi[:, d, :].bitcast(F32), ALU.subtract).then_inc(m_ready, 1)
                            elif what in ("O", "XO", "DN"):
                                arrived(dve, j)
                                if key == ("O", 0):
                                    dve.wait_ge(x_restored, 16 * KB)
                                d = key[-1]
                                frees(V.tensor_tensor(tok(xm[:, d, :]), tok(xm[:, d, :]), all_tok, ALU.add), j)
                            elif what == "TRKC":
                                hp = key[2]
                                arrived(dve, j)
                                dve.wait_ge(kst_stored, 16 * kst_stores[key])
                                dec = const[:, KDEC:KDEC + 4 * NT].rearrange("p (t h) -> p t h", h=4)[:, :, 2 * hp:2 * hp + 2]
                                for e in range(2):
                                    V.tensor_tensor(kst[:, 0:NT, HD * e:HD * e + HD],
                                                    ps[:, 0, :].rearrange("p (t c) -> p t c", t=NT)[:, :, HD * e:HD * e + HD],
                                                    dec[:, :, e:e + 1].to_broadcast([P, NT, HD]), ALU.mult)
                                sd = const[0:DEC_SEQ, KDEC + 4 * NT + 2 * hp:KDEC + 4 * NT + 2 * hp + 2]
                                frees(V.tensor_tensor(kst[0:DEC_SEQ, NT, :].rearrange("p (e c) -> p e c", e=2),
                                                      ps[0:DEC_SEQ, 1, 0:P].rearrange("p (e c) -> p e c", e=2),
                                                      sd.unsqueeze(2).to_broadcast([DEC_SEQ, 2, HD]), ALU.mult), j)
                            elif what == "ST":
                                m, hp = key[1:]
                                dve.wait_ge(st_ready, hp + 1 + (2 if m == "D" else 0))
                                dve.wait_ge(s0_loaded, 16 if m == "C" else 32)
                                dec = const[:, G32 + hp:G32 + hp + 1] if m == "C" else elast[:, hp:hp + 1]
                                frees(V.scalar_tensor_tensor(out=sts[:, hp, :], in0=s0[:, hp, :], scalar=dec,
                                                             in1=ps[:, 1, 0:P], op0=ALU.mult, op1=ALU.add), j)
                            elif what == "MEAN":
                                h = key[2]
                                arrived(dve, j)
                                frees(V.scalar_tensor_tensor(out=tok(z[:, 4 + h, :]), in0=all_tok, scalar=-1.0 / P,
                                                             in1=tok(z[:, 4 + h, :]), op0=ALU.mult, op1=ALU.add), j)
                            elif what == "SSO":
                                m, h = key[1:]
                                dve.wait_ge(o_rstd, h + 1 + (4 if m == "D" else 0))
                                g = GN[m] + h
                                V.scalar_tensor_tensor(out=z[:, 4 + h, :], in0=z[:, 4 + h, :], scalar=par[:, g:g + 1],
                                                       in1=r2x[h % 2], op0=ALU.mult, op1=ALU.mult).then_inc(on_ready, 1)
                            elif what == "GG":
                                m, h = key[1:]
                                i = h + (4 if m == "D" else 0)
                                dve.wait_ge(g_exp, i + 1)
                                e = tmp[:, h % 2, :]
                                frees(V.tensor_tensor(tok(e), tok(e), all_tok, ALU.mult), j)
                                dve.wait_ge(on_ready, i + 1)
                                V.tensor_tensor(e, e, z[:, 4 + h, :], ALU.mult)
                                V.tensor_copy(ohi[:, h, :], e)
                                V.tensor_tensor(olo[:, h, :], e, ohi[:, h, :].bitcast(F32), ALU.subtract).then_inc(o_ready, 1)
                            elif what == "LA":
                                hp = key[1]
                                dve.wait_ge(la_abs, hp + 1)
                                a, c = gt[:, 7, :], cums[hp]
                                frees(V.tensor_scalar(tok(a), all_tok, par[:, BALPHA + hp:BALPHA + hp + 1], 0.0, ALU.add, ALU.min), j)
                                dve.wait_ge(la_ln, hp + 1)
                                V.tensor_tensor(a, a, gt[:, 6, :], ALU.subtract)
                                V.tensor_scalar(a, a, 1.0 / 16.0, None, ALU.mult)
                                one = const[:, ONEC:ONEC + 1]
                                V.tensor_tensor_scan(c[:, 0:SEQ], one.to_broadcast([P, SEQ]), a[:, 0:SEQ], 0.0, ALU.mult, ALU.add)
                                V.tensor_tensor_scan(c[:, SEQ:TOK], one.to_broadcast([P, DEC_SEQ]), a[:, SEQ:TOK], 0.0,
                                                     ALU.mult, ALU.add).then_inc(cum_ready, 1)
                            elif what == "TM":
                                q = key[1]
                                arrived(dve, j)
                                for bb in range(4):
                                    b = 4 * q + bb
                                    e = tmp[:, 0, 0:MEM]
                                    ins = V.tensor_scalar(e, ps[:, bb // 2, (bb % 2) * 256:(bb % 2 + 1) * 256],
                                                          par[:, GMEM + b:GMEM + b + 1], None, ALU.mult)
                                    if bb == 3:
                                        frees(ins, j)
                                    V.tensor_copy(memn_hi[:, b, :], e)
                                    V.tensor_tensor(memn_lo[:, b, :], e, memn_hi[:, b, :].bitcast(F32), ALU.subtract).then_inc(mn_ready, 1)
            clear_all()

        with nc.Block() as block:
            @block.tensor
            def _(pe):
                for b in range(KB):
                    if b >= 2:
                        pe.wait_ge(epi_dve, b - 1)
                    for t in range(NT):
                        pe.transpose(slot[b % 2][:, 0, t * P:(t + 1) * P], xm[:, b, t * P:(t + 1) * P], cst(IDN))
                    pe.transpose(slot[b % 2][0:DEC_SEQ, 1, 0:P], xm[:, b, SEQ:TOK], cst(IDN)).then_inc(epi_pe, 1)

            @block.scalar
            def _(act):
                for b in range(KB):
                    act.wait_ge(epi_pe, b + 1)
                    nc.scalar.activation(xrow[:, :, b * P:(b + 1) * P], slot[b % 2][:, 0, :].rearrange("p (t c) -> p t c", t=NT),
                                         ACT.Copy).then_inc(epi_act, 1)

            @block.vector
            def _(dve):
                for b in range(KB):
                    dve.wait_ge(epi_act, b + 1)
                    nc.vector.tensor_copy(xrow_s[:, b * P:(b + 1) * P], slot[b % 2][0:DEC_SEQ, 1, 0:P]).then_inc(epi_dve, 1)

            @block.sync
            def _(sp):
                for q in range(4):
                    sp.wait_ge(epi_act, 2 * q + 2)
                    c = slice(2 * q * P, 2 * (q + 1) * P)
                    sp.dma_start(t_out["y_prompt"][0].rearrange("(t p) d -> p t d", p=P)[:, :, c], xrow[:, :, c]).then_inc(epi_io, 16)
                sp.wait_ge(epi_dve, KB)
                sp.dma_start(t_out["y_sample"][0], xrow_s).then_inc(epi_io, 16)
                sp.wait_ge(epi_io, 16 * 5)


_INS = ["x_prompt", "x_sample", "cache_win_k", "cache_win_v", "cache_band_k", "cache_band_v", "state_ret", "state_gla",
        "cache_mem_k", "cache_mem_v", "mem_prompt", "norm_mix", "w_in", "qn_a", "kn_a", "sink_a", "qn_b", "kn_b",
        "relbias_b", "gn_c", "w_alpha_up", "b_alpha", "gn_d", "w_branch", "w_merge", "w_out", "norm_x", "norm_mem",
        "w_xq", "w_xkv", "qn_x", "kn_x", "w_xo", "norm_ffn", "w_up", "w_down"]
_OUTS = [("y_prompt", (1, SEQ, D_MODEL)), ("y_sample", (1, DEC_SEQ, D_MODEL)),
         ("p_win_k", (DEPTH, 1, P, 2, HD)), ("p_win_v", (DEPTH, 1, P, 2, HD)),
         ("p_band_k", (DEPTH, 1, SEQ, 8, HD)), ("p_band_v", (DEPTH, 1, SEQ, 8, HD)),
         ("p_state_ret", (DEPTH, 1, 4, HD, P)), ("p_state_gla", (DEPTH, 1, 4, HD, P)),
         ("mem_k", (DEPTH, 1, MEM, XH, P)), ("mem_v", (DEPTH, 1, MEM, XH, P)),
         ("s_win_k", (DEPTH, 1, DEC_SEQ, 2, HD)), ("s_win_v", (DEPTH, 1, DEC_SEQ, 2, HD)),
         ("s_band_k", (DEPTH, 1, DEC_SEQ, 8, HD)), ("s_band_v", (DEPTH, 1, DEC_SEQ, 8, HD)),
         ("s_state_ret", (DEPTH, 1, 4, HD, P)), ("s_state_gla", (DEPTH, 1, 4, HD, P))]


def kernel(**inputs):
    import concourse.bacc as bacc
    from concourse.bass_utils import run_bass_kernel_spmd

    nc = bacc.Bacc("TRN2", target_bir_lowering=False, num_devices=1)
    arrays, t_in, t_out = {}, {}, {}
    for name, a in [(n, np.ascontiguousarray(inputs[n])) for n in _INS] + list(constants().items()):
        arrays[f"in_{name}"] = a
        t_in[name] = nc.dram_tensor(f"in_{name}", a.shape, mybir.dt.from_np(a.dtype), kind="ExternalInput").ap()
    for name, shape in _OUTS:
        t_out[name] = nc.dram_tensor(f"out_{name}", shape, F32, kind="ExternalOutput").ap()
    build(nc, t_in, t_out)
    r = run_bass_kernel_spmd(nc, [arrays], core_ids=[0])
    return tuple(r.results[0][f"out_{name}"] for name, _ in _OUTS)
```
